# Optimizing a Trainium2 kernel written in Bass

```python
import jax
import jax.numpy as jnp
from jax import lax
import numpy as np
import math

D_MODEL = 1024
BATCH = 1
SEQ = 512
DEPTH = 1

D_MIX = D_MODEL
D_GROUP = D_MIX // 4
HEAD_DIM = 64
N_HEADS = D_GROUP // HEAD_DIM
Q_BLOCK = 128
RWKV_LORA = 32
CONV_WIDTH = 4
LRU_C = 8.0
RMS_EPS = 1e-6
GN_EPS = 64e-5
N_RWKV_SHIFT = 3 * D_GROUP + 2 * RWKV_LORA
N_IN = 14 * D_GROUP + N_HEADS + 2 * RWKV_LORA


def rms_norm(x, g):
    x32 = x.astype(jnp.float32)
    y = x32 * lax.rsqrt(jnp.mean(x32 * x32, axis=-1, keepdims=True) + RMS_EPS)
    return (y * g.astype(jnp.float32)).astype(x.dtype)

def split_columns(p):
    G, H = D_GROUP, N_HEADS
    sizes = [G, G, G, G, H, G, G, G, G, N_RWKV_SHIFT, G, G, G]
    cuts, acc = [], 0
    for n in sizes[:-1]:
        acc += n
        cuts.append(acc)
    return jnp.split(p, cuts, axis=-1)

def to_heads(t):
    b, s, _ = t.shape
    return t.reshape(b, s, N_HEADS, HEAD_DIM).transpose(0, 2, 1, 3).astype(jnp.float32)

def query_blocks(t):
    b, h, s = t.shape[:3]
    t = t.reshape((b, h, s // Q_BLOCK, Q_BLOCK) + t.shape[3:])
    return jnp.moveaxis(t, 2, 0)

def merge_blocks(o):
    nb, b, h, q, d = o.shape
    return o.transpose(1, 0, 3, 2, 4).reshape(b, nb * q, h * d)

def forgetting_attention(q, k, v, log_f):
    s = q.shape[2]
    scale = HEAD_DIM ** -0.5
    cum = jnp.cumsum(log_f, axis=-1)
    key_pos = jnp.arange(s)

    def block(args):
        qb, cb, i = args
        q_pos = i * Q_BLOCK + jnp.arange(Q_BLOCK)
        logits = (jnp.einsum('bhqd,bhkd->bhqk', qb, k) * scale
                  + cb[..., None] - cum[:, :, None, :])
        logits = jnp.where(key_pos[None, :] <= q_pos[:, None], logits, -jnp.inf)
        return jnp.einsum('bhqk,bhkd->bhqd', jax.nn.softmax(logits, axis=-1), v)

    out = lax.map(block, (query_blocks(q), query_blocks(cum), jnp.arange(s // Q_BLOCK)))
    return merge_blocks(out)

def stick_breaking_attention(q, k, v):
    s = q.shape[2]
    scale = HEAD_DIM ** -0.5
    key_pos = jnp.arange(s)

    def block(args):
        qb, i = args
        q_pos = i * Q_BLOCK + jnp.arange(Q_BLOCK)
        z = jnp.einsum('bhqd,bhkd->bhqk', qb, k) * scale
        mask = key_pos[None, :] < q_pos[:, None]
        log_keep = jnp.where(mask, jax.nn.log_sigmoid(-z), 0.0)
        log_rest = lax.cumsum(log_keep, axis=3, reverse=True) - log_keep
        att = jnp.where(mask, jnp.exp(jax.nn.log_sigmoid(z) + log_rest), 0.0)
        return jnp.einsum('bhqk,bhkd->bhqd', att, v)

    out = lax.map(block, (query_blocks(q), jnp.arange(s // Q_BLOCK)))
    return merge_blocks(out)

def rwkv7_time_mix(p, mu, w0, w2, a0, a2, k_k, k_a, r_k, ln_g, ln_b):
    b, s, _ = p.shape
    G, R = D_GROUP, RWKV_LORA
    p = p.astype(jnp.float32)
    prev = jnp.pad(p, ((0, 0), (1, 0), (0, 0)))[:, :-1]
    p = p + (prev - p) * mu
    r, k, v, wl, al = jnp.split(p, [G, 2 * G, 3 * G, 3 * G + R], axis=-1)
    w = -jax.nn.softplus(-(w0 + jnp.tanh(wl) @ w2)) - 0.5
    decay = jnp.exp(-jnp.exp(w))
    a = jax.nn.sigmoid(a0 + al @ a2)
    hs = lambda t: t.reshape(b, s, N_HEADS, HEAD_DIM)
    kk = hs(k * k_k)
    kk = kk * lax.rsqrt(jnp.maximum(jnp.sum(kk * kk, axis=-1, keepdims=True), 1e-12))
    k = hs(k * (1.0 + (a - 1.0) * k_a))
    r, v, decay, a = hs(r), hs(v), hs(decay), hs(a)

    def step(state, inp):
        r_t, w_t, k_t, v_t, kk_t, a_t = inp
        sa = jnp.einsum('bhij,bhj->bhi', state, -kk_t)
        state = (state * w_t[:, :, None, :]
                 + sa[..., None] * (kk_t * a_t)[:, :, None, :]
                 + v_t[..., None] * k_t[:, :, None, :])
        return state, jnp.einsum('bhij,bhj->bhi', state, r_t)

    xs = tuple(jnp.moveaxis(t, 1, 0) for t in (r, decay, k, v, kk, a))
    state0 = jnp.zeros((b, N_HEADS, HEAD_DIM, HEAD_DIM), jnp.float32)
    _, y = lax.scan(step, state0, xs)
    y = jnp.moveaxis(y, 0, 1)
    mean = jnp.mean(y, axis=-1, keepdims=True)
    var = jnp.mean(jnp.square(y - mean), axis=-1, keepdims=True)
    y = ((y - mean) * lax.rsqrt(var + GN_EPS)).reshape(b, s, G) * ln_g + ln_b
    bonus = jnp.sum(r * k * r_k, axis=-1, keepdims=True) * v
    return y + bonus.reshape(b, s, G)

def rg_lru(x, conv_w, conv_b, w_a, b_a, w_x, b_x, lam):
    x = x.astype(jnp.float32)
    b, s, c = x.shape
    xc = lax.conv_general_dilated(
        x, conv_w.astype(jnp.float32)[:, None, :], window_strides=(1,),
        padding=[(CONV_WIDTH - 1, 0)], dimension_numbers=('NWC', 'WIO', 'NWC'),
        feature_group_count=c) + conv_b
    xh = xc.reshape(b, s, N_HEADS, HEAD_DIM)
    r = jax.nn.sigmoid(jnp.einsum('bsni,nij->bsnj', xh, w_a).reshape(b, s, c) + b_a)
    i = jax.nn.sigmoid(jnp.einsum('bsni,nij->bsnj', xh, w_x).reshape(b, s, c) + b_x)
    log_a = -LRU_C * r * jax.nn.softplus(-lam)
    a = jnp.exp(log_a)
    u = jnp.sqrt(-jnp.expm1(2.0 * log_a)) * (i * xc)

    def combine(lhs, rhs):
        a1, b1 = lhs
        a2, b2 = rhs
        return a1 * a2, a2 * b1 + b2

    _, h = lax.associative_scan(combine, (a, u), axis=1)
    return h

def first_inputs(seed: int = 0) -> dict:
    key = jax.random.key(seed)
    ks = jax.random.split(key, 24)
    f32 = jnp.float32
    L, D, G, H, R, N = DEPTH, D_MODEL, D_GROUP, N_HEADS, RWKV_LORA, HEAD_DIM

    def nrm(k, shape, scale):
        return scale * jax.random.normal(k, shape, f32)

    x = jax.random.normal(ks[0], (BATCH, SEQ, D), f32)
    norm_g = 1.0 + nrm(ks[1], (L, D), 0.05)
    w_in = nrm(ks[2], (L, D, N_IN), D ** -0.5)
    b_forget = 2.0 + nrm(ks[3], (L, H), 0.5)
    rwkv_mu = jax.random.uniform(ks[4], (L, N_RWKV_SHIFT), f32)
    rwkv_w0 = jax.random.uniform(ks[5], (L, G), f32, -6.0, 0.0)
    rwkv_w2 = nrm(ks[6], (L, R, G), 0.1 * R ** -0.5)
    rwkv_a0 = nrm(ks[7], (L, G), 0.1)
    rwkv_a2 = nrm(ks[8], (L, R, G), 0.1 * R ** -0.5)
    rwkv_k_k = 0.85 + nrm(ks[9], (L, G), 0.05)
    rwkv_k_a = 1.0 + nrm(ks[10], (L, G), 0.05)
    rwkv_r_k = nrm(ks[11], (L, H, N), 0.1)
    rwkv_ln_g = 1.0 + nrm(ks[12], (L, G), 0.05)
    rwkv_ln_b = nrm(ks[13], (L, G), 0.02)
    lru_conv_w = nrm(ks[14], (L, CONV_WIDTH, G), CONV_WIDTH ** -0.5)
    lru_conv_b = nrm(ks[15], (L, G), 0.02)
    lru_w_a = nrm(ks[16], (L, H, N, N), N ** -0.5)
    lru_b_a = nrm(ks[17], (L, G), 0.02)
    lru_w_x = nrm(ks[18], (L, H, N, N), N ** -0.5)
    lru_b_x = nrm(ks[19], (L, G), 0.02)
    a_pow_c = jax.random.uniform(ks[20], (L, G), f32, 0.9, 0.999)
    a_base = a_pow_c ** (1.0 / LRU_C)
    lru_lambda = jnp.log(a_base) - jnp.log1p(-a_base)
    w_out = nrm(ks[21], (L, D_MIX, D), D_MIX ** -0.5)
    final_g = 1.0 + nrm(ks[22], (D,), 0.05)
    return {"x": x, "norm_g": norm_g, "w_in": w_in, "b_forget": b_forget,
            "rwkv_mu": rwkv_mu, "rwkv_w0": rwkv_w0, "rwkv_w2": rwkv_w2,
            "rwkv_a0": rwkv_a0, "rwkv_a2": rwkv_a2, "rwkv_k_k": rwkv_k_k,
            "rwkv_k_a": rwkv_k_a, "rwkv_r_k": rwkv_r_k, "rwkv_ln_g": rwkv_ln_g,
            "rwkv_ln_b": rwkv_ln_b, "lru_conv_w": lru_conv_w, "lru_conv_b": lru_conv_b,
            "lru_w_a": lru_w_a, "lru_b_a": lru_b_a, "lru_w_x": lru_w_x,
            "lru_b_x": lru_b_x, "lru_lambda": lru_lambda, "w_out": w_out,
            "final_g": final_g}

def first_block(x, norm_g, w_in, b_forget, rwkv_mu, rwkv_w0, rwkv_w2, rwkv_a0, rwkv_a2,
              rwkv_k_k, rwkv_k_a, rwkv_r_k, rwkv_ln_g, rwkv_ln_b, lru_conv_w, lru_conv_b,
              lru_w_a, lru_b_a, lru_w_x, lru_b_x, lru_lambda, w_out, final_g):
    f32 = jnp.float32
    for l in range(DEPTH):
        h = rms_norm(x, norm_g[l])
        p = h @ w_in[l]
        (fq, fk, fv, fg, ff, sq, sk, sv, sg, rw, rg, lx, lg) = split_columns(p)
        log_f = jax.nn.log_sigmoid(ff.astype(f32) + b_forget[l]).transpose(0, 2, 1)
        y_fox = forgetting_attention(to_heads(fq), to_heads(fk), to_heads(fv), log_f)
        y_sb = stick_breaking_attention(to_heads(sq), to_heads(sk), to_heads(sv))
        y_rw = rwkv7_time_mix(rw, rwkv_mu[l], rwkv_w0[l], rwkv_w2[l], rwkv_a0[l], rwkv_a2[l],
                              rwkv_k_k[l], rwkv_k_a[l], rwkv_r_k[l], rwkv_ln_g[l], rwkv_ln_b[l])
        y_lru = rg_lru(lx, lru_conv_w[l], lru_conv_b[l], lru_w_a[l], lru_b_a[l],
                       lru_w_x[l], lru_b_x[l], lru_lambda[l])
        y = jnp.concatenate([
            y_fox * jax.nn.silu(fg.astype(f32)),
            y_sb * jax.nn.silu(sg.astype(f32)),
            y_rw * jax.nn.silu(rg.astype(f32)),
            y_lru * jax.nn.silu(lg.astype(f32)),
        ], axis=-1).astype(x.dtype)
        x = x + y @ w_out[l]
    return rms_norm(x, final_g)


DEPTH_2 = 2

GRID_W = 64
CTX_LEN = 256
N_MIXERS = 4
GROUP_W = D_MODEL // N_MIXERS
MIX_W = N_MIXERS * GROUP_W
N_FOURIER = GROUP_W // HEAD_DIM
N_DIFF = GROUP_W // HEAD_DIM
DIFF_QK = HEAD_DIM // 2
DIFF_V = HEAD_DIM
N_NA = GROUP_W // HEAD_DIM
NA_KH_MAX = 8
NA_KW = 16
N_GMLP = GROUP_W // HEAD_DIM
CHUNK = 128
D_FF = 2816
CONV_W = 3
ROPE_BASE = 10000.0
EPS = 1e-6
IN_W = GROUP_W + 3 * GROUP_W + 3 * GROUP_W + 2 * GROUP_W


def rms_norm_2(x, g):
    xf = x.astype(jnp.float32)
    y = xf * lax.rsqrt(jnp.mean(xf * xf, axis=-1, keepdims=True) + EPS)
    return (y * g.astype(jnp.float32)).astype(x.dtype)

def axial_rope_tables(n, dim, dtype):
    n_freq = dim // 4
    freqs = ROPE_BASE ** (-jnp.arange(n_freq, dtype=jnp.float32) / n_freq)
    t = jnp.arange(n)
    row = (t // GRID_W).astype(jnp.float32)
    col = (t % GRID_W).astype(jnp.float32)
    ang = jnp.concatenate([row[:, None] * freqs, col[:, None] * freqs], axis=-1)
    return jnp.cos(ang).astype(dtype), jnp.sin(ang).astype(dtype)

def apply_rope(x, cos, sin):
    x1, x2 = jnp.split(x, 2, axis=-1)
    return jnp.concatenate([x1 * cos - x2 * sin, x1 * sin + x2 * cos], axis=-1)

def dense_attention(q, k, v):
    s = jnp.einsum('bhqd,bhkd->bhqk', q, k).astype(jnp.float32) * (q.shape[-1] ** -0.5)
    a = jax.nn.softmax(s, axis=-1).astype(v.dtype)
    return jnp.einsum('bhqk,bhkd->bhqd', a, v)

def fourier_mix(p):
    b, n, _ = p.shape
    g = p.reshape(b, n, N_FOURIER, HEAD_DIM).astype(jnp.float32)
    f = jnp.fft.fft2(g, axes=(1, 3), norm='ortho').real
    return f.reshape(b, n, GROUP_W).astype(p.dtype)

def diff_q(p, qn):
    b, n, _ = p.shape
    q = rms_norm_2(p[..., :GROUP_W].reshape(b, n, N_DIFF, 2, DIFF_QK), qn)
    return q.transpose(0, 2, 3, 1, 4)

def diff_kv(p, kn):
    b, n, _ = p.shape
    k = rms_norm_2(p[..., GROUP_W:2 * GROUP_W].reshape(b, n, N_DIFF, 2, DIFF_QK), kn)
    v = p[..., 2 * GROUP_W:].reshape(b, n, N_DIFF, DIFF_V)
    return k.transpose(0, 2, 3, 1, 4), v.transpose(0, 2, 1, 3)

def diff_core(q, k, v, lam):
    s = jnp.einsum('bhcqd,bhckd->bhcqk', q, k).astype(jnp.float32) * (DIFF_QK ** -0.5)
    a = jax.nn.softmax(s, axis=-1)
    w = (a[:, :, 0] - lam * a[:, :, 1]).astype(v.dtype)
    return jnp.einsum('bhqk,bhkd->bhqd', w, v)

def diff_finish(o, subln, lam_init):
    b, _, n, _ = o.shape
    o = rms_norm_2(o, subln) * (1.0 - lam_init)
    return o.transpose(0, 2, 1, 3).reshape(b, n, GROUP_W)

def diff_attention_latent(p, kc, vc, qn, kn, lam, subln, lam_init, cos, sin):
    b, n, _ = p.shape
    q = apply_rope(diff_q(p, qn), cos, sin)
    k, v = diff_kv(p, kn)
    k = apply_rope(k, cos, sin)
    k_all = jnp.concatenate([k, kc], axis=3)
    v_all = jnp.concatenate([v, vc], axis=2)
    nb = n // Q_BLOCK
    qb = jnp.moveaxis(q.reshape(b, N_DIFF, 2, nb, Q_BLOCK, DIFF_QK), 3, 0)
    o = lax.map(lambda qq: diff_core(qq, k_all, v_all, lam), qb)
    o = jnp.moveaxis(o, 0, 2).reshape(b, N_DIFF, n, DIFF_V)
    return diff_finish(o, subln, lam_init)

def na_q(p, qn):
    b, n, _ = p.shape
    return rms_norm_2(p[..., :GROUP_W].reshape(b, n, N_NA, HEAD_DIM), qn).transpose(0, 2, 1, 3)

def na_kv(p, kn):
    b, n, _ = p.shape
    k = rms_norm_2(p[..., GROUP_W:2 * GROUP_W].reshape(b, n, N_NA, HEAD_DIM), kn)
    v = p[..., 2 * GROUP_W:].reshape(b, n, N_NA, HEAD_DIM)
    return k.transpose(0, 2, 1, 3), v.transpose(0, 2, 1, 3)

def na_attention_latent(p, kc, vc, qn, kn, rpb):
    b, n, _ = p.shape
    rows = n // GRID_W
    kh = min(NA_KH_MAX, rows)
    n_loc = kh * NA_KW
    q = na_q(p, qn)
    k, v = na_kv(p, kn)
    r = jnp.arange(rows)
    r0 = jnp.clip(r - kh // 2, 0, rows - kh)
    row_off = r0[:, None] + jnp.arange(kh)[None, :] - r[:, None] + NA_KH_MAX - 1
    j = jnp.arange(GRID_W)
    c0 = jnp.clip(j - NA_KW // 2, 0, GRID_W - NA_KW)
    col_idx = c0[:, None] + jnp.arange(NA_KW)[None, :]
    col_off = col_idx - j[:, None] + NA_KW - 1
    rpb_c = rpb[:, :, col_off]
    kg = k.reshape(b, N_NA, rows, GRID_W, HEAD_DIM)
    vg = v.reshape(b, N_NA, rows, GRID_W, HEAD_DIM)
    scale = HEAD_DIM ** -0.5

    def row_block(args):
        qr, start, roff = args
        kr = lax.dynamic_slice_in_dim(kg, start, kh, axis=2)[:, :, :, col_idx]
        vr = lax.dynamic_slice_in_dim(vg, start, kh, axis=2)[:, :, :, col_idx]
        bias = jnp.transpose(rpb_c[:, roff], (0, 2, 1, 3)).astype(jnp.float32)
        s_loc = jnp.einsum('bhjd,bhajkd->bhjak', qr, kr).astype(jnp.float32) * scale + bias
        s_ctx = jnp.einsum('bhjd,bhcd->bhjc', qr, kc).astype(jnp.float32) * scale
        s = jnp.concatenate([s_loc.reshape(b, N_NA, GRID_W, n_loc), s_ctx], axis=-1)
        a = jax.nn.softmax(s, axis=-1).astype(vr.dtype)
        a_loc = a[..., :n_loc].reshape(b, N_NA, GRID_W, kh, NA_KW)
        return (jnp.einsum('bhjak,bhajkd->bhjd', a_loc, vr)
                + jnp.einsum('bhjc,bhcd->bhjd', a[..., n_loc:], vc))

    qg = jnp.moveaxis(q.reshape(b, N_NA, rows, GRID_W, HEAD_DIM), 2, 0)
    o = lax.map(row_block, (qg, r0, row_off))
    o = jnp.moveaxis(o, 0, 2).reshape(b, N_NA, n, HEAD_DIM)
    return o.transpose(0, 2, 1, 3).reshape(b, n, GROUP_W)

def na_attention_context(p, kc, vc, qn):
    b, n, _ = p.shape
    o = dense_attention(na_q(p, qn), kc, vc)
    return o.transpose(0, 2, 1, 3).reshape(b, n, GROUP_W)

def chunk_gmlp(p, gn, ws, bs):
    b, n, _ = p.shape
    u, v = jnp.split(jax.nn.gelu(p), 2, axis=-1)
    v = rms_norm_2(v.reshape(b, n // CHUNK, CHUNK, N_GMLP, HEAD_DIM), gn.reshape(N_GMLP, HEAD_DIM))
    s = jnp.einsum('gpq,bnqgc->bnpgc', ws, v) + jnp.swapaxes(bs, 0, 1)[:, :, None]
    return u * s.reshape(b, n, GROUP_W)

def conv_ffn(h, w_up, w_conv, b_conv, w_down):
    z = h @ w_up
    ch = z.shape[-1]
    z = lax.conv_general_dilated(z, w_conv[:, None, :].astype(z.dtype), window_strides=(1,),
                                 padding=((CONV_W // 2, CONV_W // 2),),
                                 dimension_numbers=('NWC', 'WIO', 'NWC'),
                                 feature_group_count=ch) + b_conv
    g, v = jnp.split(z, 2, axis=-1)
    return (jax.nn.silu(g) * v) @ w_down

def second_inputs(seed: int = 0) -> dict:
    key = jax.random.key(seed)
    ks = jax.random.split(key, 24)
    f32 = jnp.float32

    def nrm(k, shape, s):
        return jax.random.normal(k, shape, f32) * s

    def gain(k, shape):
        return 1.0 + 0.02 * jax.random.normal(k, shape, f32)

    return {
        "x": nrm(ks[0], (BATCH, SEQ, D_MODEL), 1.0),
        "c": nrm(ks[1], (BATCH, D_MODEL), 1.0),
        "ctx": nrm(ks[2], (BATCH, CTX_LEN, D_MODEL), 1.0),
        "c_ctx": nrm(ks[3], (D_MODEL,), 1.0),
        "w_ada": nrm(ks[4], (DEPTH_2, D_MODEL, 6 * D_MODEL), 0.5 * D_MODEL ** -0.5),
        "b_ada": nrm(ks[5], (DEPTH_2, 6 * D_MODEL), 0.02),
        "g_mix": gain(ks[6], (DEPTH_2, D_MODEL)),
        "g_ffn": gain(ks[7], (DEPTH_2, D_MODEL)),
        "w_in": nrm(ks[8], (DEPTH_2, D_MODEL, IN_W), D_MODEL ** -0.5),
        "w_out": nrm(ks[9], (DEPTH_2, MIX_W, D_MODEL), MIX_W ** -0.5),
        "diff_qn": gain(ks[10], (DEPTH_2, DIFF_QK)),
        "diff_kn": gain(ks[11], (DEPTH_2, DIFF_QK)),
        "diff_lam": nrm(ks[12], (DEPTH_2, 4, DIFF_QK), 0.1),
        "diff_subln": gain(ks[13], (DEPTH_2, DIFF_V)),
        "na_qn": gain(ks[14], (DEPTH_2, HEAD_DIM)),
        "na_kn": gain(ks[15], (DEPTH_2, HEAD_DIM)),
        "na_rpb": nrm(ks[16], (DEPTH_2, N_NA, 2 * NA_KH_MAX - 1, 2 * NA_KW - 1), 0.02),
        "gmlp_norm": gain(ks[17], (DEPTH_2, GROUP_W)),
        "gmlp_ws": nrm(ks[18], (DEPTH_2, N_GMLP, CHUNK, CHUNK), CHUNK ** -0.5),
        "gmlp_b": nrm(ks[19], (DEPTH_2, N_GMLP, CHUNK), 0.02),
        "ffn_up": nrm(ks[20], (DEPTH_2, D_MODEL, 2 * D_FF), D_MODEL ** -0.5),
        "ffn_conv": nrm(ks[21], (DEPTH_2, CONV_W, 2 * D_FF), CONV_W ** -0.5),
        "ffn_conv_b": nrm(ks[22], (DEPTH_2, 2 * D_FF), 0.02),
        "ffn_down": nrm(ks[23], (DEPTH_2, D_FF, D_MODEL), D_FF ** -0.5),
    }

def second_block(x, c, ctx, c_ctx, w_ada, b_ada, g_mix, g_ffn, w_in, w_out, diff_qn, diff_kn, diff_lam,
              diff_subln, na_qn, na_kn, na_rpb, gmlp_norm, gmlp_ws, gmlp_b, ffn_up, ffn_conv, ffn_conv_b,
              ffn_down):
    n = x.shape[1]
    G = GROUP_W
    cos, sin = axial_rope_tables(n, DIFF_QK, x.dtype)
    s_lat = jax.nn.silu(c)[:, None, :]
    s_ctx = jax.nn.silu(c_ctx)
    for li in range(DEPTH_2):
        ctx_out = li < DEPTH_2 - 1
        lam_init = 0.8 - 0.6 * math.exp(-0.3 * li)
        lf = diff_lam[li].astype(jnp.float32)
        lam = jnp.exp(jnp.sum(lf[0] * lf[1])) - jnp.exp(jnp.sum(lf[2] * lf[3])) + lam_init
        m_lat = jnp.split(s_lat @ w_ada[li] + b_ada[li], 6, axis=-1)
        m_ctx = jnp.split(s_ctx @ w_ada[li] + b_ada[li], 6, axis=-1)

        h = rms_norm_2(x, g_mix[li]) * (1.0 + m_lat[1]) + m_lat[0]
        hc = rms_norm_2(ctx, g_mix[li]) * (1.0 + m_ctx[1]) + m_ctx[0]
        p = h @ w_in[li]
        pc = hc @ w_in[li]
        kc_d, vc_d = diff_kv(pc[..., G:4 * G], diff_kn[li])
        kc_n, vc_n = na_kv(pc[..., 4 * G:7 * G], na_kn[li])
        y = jnp.concatenate([
            fourier_mix(p[..., :G]),
            diff_attention_latent(p[..., G:4 * G], kc_d, vc_d, diff_qn[li], diff_kn[li], lam,
                                  diff_subln[li], lam_init, cos, sin),
            na_attention_latent(p[..., 4 * G:7 * G], kc_n, vc_n, na_qn[li], na_kn[li], na_rpb[li]),
            chunk_gmlp(p[..., 7 * G:], gmlp_norm[li], gmlp_ws[li], gmlp_b[li]),
        ], axis=-1)
        x = x + m_lat[2] * (y @ w_out[li])
        if ctx_out:
            yc = jnp.concatenate([
                fourier_mix(pc[..., :G]),
                diff_finish(diff_core(diff_q(pc[..., G:4 * G], diff_qn[li]), kc_d, vc_d, lam),
                            diff_subln[li], lam_init),
                na_attention_context(pc[..., 4 * G:7 * G], kc_n, vc_n, na_qn[li]),
                chunk_gmlp(pc[..., 7 * G:], gmlp_norm[li], gmlp_ws[li], gmlp_b[li]),
            ], axis=-1)
            ctx = ctx + m_ctx[2] * (yc @ w_out[li])

        h = rms_norm_2(x, g_ffn[li]) * (1.0 + m_lat[4]) + m_lat[3]
        x = x + m_lat[5] * conv_ffn(h, ffn_up[li], ffn_conv[li], ffn_conv_b[li], ffn_down[li])
        if ctx_out:
            hc = rms_norm_2(ctx, g_ffn[li]) * (1.0 + m_ctx[4]) + m_ctx[3]
            ctx = ctx + m_ctx[5] * conv_ffn(hc, ffn_up[li], ffn_conv[li], ffn_conv_b[li], ffn_down[li])
    return x


def setup_inputs(seed=0):
    out = dict(first_inputs(seed))
    for name, value in second_inputs(seed + 1).items():
        if name != "x":
            out[name + "_2"] = value
    return out


def reference(
    x, norm_g, w_in, b_forget, rwkv_mu, rwkv_w0, rwkv_w2, rwkv_a0, rwkv_a2, rwkv_k_k, rwkv_k_a,
    rwkv_r_k, rwkv_ln_g, rwkv_ln_b, lru_conv_w, lru_conv_b, lru_w_a, lru_b_a, lru_w_x, lru_b_x,
    lru_lambda, w_out, final_g, c_2, ctx_2, c_ctx_2, w_ada_2, b_ada_2, g_mix_2, g_ffn_2, w_in_2,
    w_out_2, diff_qn_2, diff_kn_2, diff_lam_2, diff_subln_2, na_qn_2, na_kn_2, na_rpb_2,
    gmlp_norm_2, gmlp_ws_2, gmlp_b_2, ffn_up_2, ffn_conv_2, ffn_conv_b_2, ffn_down_2,
):
    x = first_block(
        x, norm_g, w_in, b_forget, rwkv_mu, rwkv_w0, rwkv_w2, rwkv_a0, rwkv_a2, rwkv_k_k,
        rwkv_k_a, rwkv_r_k, rwkv_ln_g, rwkv_ln_b, lru_conv_w, lru_conv_b, lru_w_a, lru_b_a,
        lru_w_x, lru_b_x, lru_lambda, w_out, final_g,
    )
    return second_block(
        x, c_2, ctx_2, c_ctx_2, w_ada_2, b_ada_2, g_mix_2, g_ffn_2, w_in_2, w_out_2, diff_qn_2,
        diff_kn_2, diff_lam_2, diff_subln_2, na_qn_2, na_kn_2, na_rpb_2, gmlp_norm_2, gmlp_ws_2,
        gmlp_b_2, ffn_up_2, ffn_conv_2, ffn_conv_b_2, ffn_down_2,
    )


_drawn_inputs = setup_inputs


def setup_inputs(seed=0):
    import zlib

    import numpy as np

    out = dict(_drawn_inputs(seed))
    spreads = {}
    factors = {'rwkv_w2': 8.0,
     'rwkv_a0': 4.527,
     'rwkv_a2': 4.866,
     'rwkv_k_k': 4.205,
     'rwkv_k_a': 3.335,
     'rwkv_ln_g': 4.309,
     'rwkv_ln_b': 8.0,
     'lru_b_a': 8.0,
     'lru_b_x': 8.0,
     'g_mix_2': 8.0,
     'g_ffn_2': 6.663,
     'diff_qn_2': 8.0,
     'diff_kn_2': 8.0,
     'diff_lam_2': 8.0,
     'diff_subln_2': 64.0,
     'na_qn_2': 8.0,
     'na_kn_2': 8.0,
     'na_rpb_2': 64.0,
     'gmlp_norm_2': 8.0,
     'gmlp_b_2': 8.0,
     'ffn_conv_b_2': 7.089}
    for name, (base, spread) in spreads.items():
        noise = np.random.default_rng([zlib.crc32(name.encode()), seed]).standard_normal(out[name].shape)
        drawn = base * np.exp(spread * noise) if base else spread * noise
        out[name] = jnp.asarray(drawn.astype(out[name].dtype))
    for name, factor in factors.items():
        out[name] = (out[name] * factor).astype(out[name].dtype)
    return out
```

```python
from contextlib import ExitStack

import numpy as np

import concourse.bass as bass
from concourse import mybir

F32 = mybir.dt.float32
ALU = mybir.AluOpType
ACT = mybir.ActivationFunctionType
AX = mybir.AxisListType.X
ds = bass.ds

P = 128
D = 1024
KD = D // P
S = 512
C = 256
NT = S // P
CT = C // P
MT = NT + CT
G = 256
H = 4
HD = 64
R = 32
FF = 2816
KF = FF // P
EPS = 1e-6
GN_EPS = 64e-5
NEG = -1e30
PAD = 4
RING = 4
CH = 128
LEVELS = 7
DECAY = float(np.exp(-0.5))
HALF = DECAY * CH / 2

FQ, FK, SQ, SK, RR, RK, RV, MISC, LX, GATE = 0, 2, 4, 6, 8, 10, 12, 14, 15, 17
N1F, N1T = 25, 4
DK, NK, FO, DQ, NQ = 0, 2, 4, 6, 8
N2F = 10

CONST = {}
_at = 0
for _name, _n in (("ident", P), ("ones", P), ("block32", P), ("block64", P), ("tri_ge", P),
                  ("causal_add", P), ("stick_big", P), ("strict_t", P), ("incl_t", P),
                  ("rope_swap", P), ("head_row", H * P), ("head_pair", 2),
                  ("level", LEVELS * P), ("level0_t", P), ("window", HD), ("chunk_keep", S), ("keep_all", S),
                  ("dft64", 2 * P)):
    CONST[_name] = (_at, _at + _n)
    _at += _n
NCONST = _at

PRM = {}
_at = 0
for _name, _n in (("norm_g", KD), ("final_g", KD), ("mu", 7), ("w0", 2), ("a0", 2), ("k_k", 2),
                  ("k_a", 2), ("r_k", 2), ("conv_w", 8), ("conv_b", 2), ("b_a", 2), ("b_x", 2),
                  ("lam", 2), ("b_f", 1), ("c", 2 * KD),
                  ("g_mix", 2 * KD), ("g_ffn", 2 * KD), ("b_ada", 2 * 48), ("conv_b2", 2 * 44),
                  ("conv_w2", 2 * 3 * 44), ("dqn", 2), ("dkn", 2), ("nqn", 2), ("nkn", 2),
                  ("gmlp_b", 2 * H)):
    PRM[_name] = (_at, _at + _n)
    _at += _n
NPRM = _at

ROW = {}
_at = 0
for _name, _n in (("ln_g", G), ("ln_b", G), ("subln", 2 * G), ("gmlp_g", 2 * G), ("lam4", 2 * 128)):
    ROW[_name] = (_at, _at + _n)
    _at += _n
NROW = _at


def lambda_init(layer):
    return 0.8 - 0.6 * float(np.exp(-0.3 * layer))


class Kit:
    pass


class Signal:

    def __init__(self, nc, ctx, name):
        self.sem = ctx.enter_context(nc.semaphore(name))
        self.n = 0
        self.base = 0

    def up(self, instruction, by=1):
        instruction.then_inc(self.sem, by)
        self.n += by
        return self.n


def start_phase(K):
    for s in K.signals.values():
        s.base = s.n


def link(eng, signal, instruction):
    eng.wait_ge(signal.sem, signal.up(instruction))


def meet(K):
    goal = K.met.n + 4
    @K.block.tensor
    def _(e):
        e.drain().then_inc(K.met.sem, 1)
        e.wait_ge(K.met.sem, goal)
    @K.block.vector
    def _(e):
        e.drain().then_inc(K.met.sem, 1)
        e.wait_ge(K.met.sem, goal)
    @K.block.scalar
    def _(e):
        e.drain().then_inc(K.met.sem, 1)
        e.wait_ge(K.met.sem, goal)
    @K.block.gpsimd
    def _(e):
        e.drain().then_inc(K.met.sem, 1)
        e.wait_ge(K.met.sem, goal)
    K.met.n = goal
    start_phase(K)


def arena(K, ctx, name, shape):
    K.serial += 1
    return ctx.enter_context(K.nc.sbuf_tensor(f"{name}_{K.serial}", shape, F32))


def const(K, name, rows=slice(0, P)):
    a, b = CONST[name]
    return K.cst[rows, a:b]


def prm(K, name, col=0, n=1, rows=slice(0, P)):
    a = PRM[name][0] + col
    return K.prm[rows, a:a + n]


def row(K, name, first=0, n=G):
    a = ROW[name][0] + first
    return K.rows[:, a:a + n]



def stream_weights(K, n_units):
    @K.block.sync
    def _(sp):
        for j in range(RING):
            sp.dma_start(K.ring[:, j], K.w_units[j]).then_inc(K.slot_full[j].sem, 16)
        with sp.Fori(0, n_units // RING - 1) as i:
            for j in range(RING):
                sp.wait_ge(K.unit_used.sem, i * RING + j + 1)
                sp.dma_start(K.ring[:, j], K.w_units[ds(i * RING + (j + RING), 1)]
                             .rearrange("u p n -> (u p) n")).then_inc(K.slot_full[j].sem, 16)
        for u in range(n_units - n_units % RING, n_units):
            sp.wait_ge(K.unit_used.sem, u - RING + 1)
            sp.dma_start(K.ring[:, u % RING], K.w_units[u]).then_inc(K.slot_full[u % RING].sem, 16)



def rms_phase(K, src, dst, parts):
    square, stat, rstd_ready, normed = (K.signals[n] for n in ("square", "stat", "rstd", "normed"))
    with ExitStack() as ctx:
        sq = arena(K, ctx, "squares", [P, KD, S])
        rstd = arena(K, ctx, "rstd", [P, S + C])

        @K.block.scalar
        def _(act):
            for n, (c0, w, _, _) in enumerate(parts):
                if n:
                    act.wait_ge(stat.sem, stat.base + n)
                for k in range(KD):
                    square.up(act.activation(sq[:, k, 0:w], src[:, k, c0:c0 + w], ACT.Square))
                act.wait_ge(stat.sem, stat.base + n + 1)
                link(act, K.act_step, act.activation(rstd[:, c0:c0 + w], K.ps[n][:, 0:w], ACT.Ln,
                                                           bias=K.eps[:, 0:1], scale=1.0 / D))
                rstd_ready.up(act.activation(rstd[:, c0:c0 + w], rstd[:, c0:c0 + w], ACT.Exp,
                                                   scale=-0.5))

        @K.block.tensor
        def _(pe):
            for n, (c0, w, _, _) in enumerate(parts):
                for k in range(KD):
                    pe.wait_ge(square.sem, square.base + n * KD + k + 1)
                    mm = pe.matmul(K.ps[n][:, 0:w], const(K, "ones"), sq[:, k, 0:w],
                                   start=(k == 0), stop=(k == KD - 1))
                stat.up(mm)

        @K.block.vector
        def _(dve):
            for n, (c0, w, gain, shift) in enumerate(parts):
                dve.wait_ge(rstd_ready.sem, rstd_ready.base + n + 1)
                for k in range(KD):
                    ins = dve.scalar_tensor_tensor(dst[:, k, c0:c0 + w], src[:, k, c0:c0 + w], gain(k),
                                                   rstd[:, c0:c0 + w], ALU.mult, ALU.mult)
                    if shift is not None:
                        last = normed.up(ins)
                if shift is not None:
                    for k in range(KD):
                        dve.wait_ge(normed.sem, last - KD + k + 1)
                        dve.tensor_scalar(dst[:, k, c0:c0 + w], dst[:, k, c0:c0 + w], shift(k), None, ALU.add)
        meet(K)



def project(K, count, token_major, with_ctx, evac_main, evac_ctx, moving=None):
    src = K.hT if moving is None else moving
    main_free, ctx_free = K.signals["main_free"], K.signals["ctx_free"]
    first = K.unit
    turns, rest = divmod(count, RING)

    def unit(pe, j, i):
        u = i * RING + j
        q = first + j
        pe.wait_ge(K.slot_full[q % RING].sem, i * 16 + 16 * (q // RING + 1))
        pe.wait_ge(main_free.sem, u + main_free.base + 1)
        if with_ctx:
            pe.wait_ge(ctx_free.sem, u + ctx_free.base + 1)
        w = K.ring[:, q % RING]
        if token_major:
            tiles = MT if with_ctx else NT
            for m in range(tiles):
                bank, at = (j, m) if m < NT else (4 + j, m - NT)
                for k in range(KD):
                    mm = pe.matmul(K.ps[bank][:, at * P:at * P + P], src[:, k, m * P:m * P + P],
                                   w[:, k * P:k * P + P], start=(k == 0), stop=(k == KD - 1))
        else:
            for k in range(KD):
                mm = pe.matmul(K.ps[j][:, :], w[:, k * P:k * P + P], src[:, k, 0:S], start=(k == 0), stop=(k == KD - 1))
                if with_ctx:
                    mm = pe.matmul(K.ps[4 + j][:, 0:C], w[:, k * P:k * P + P], src[:, k, S:S + C],
                                   start=(k == 0), stop=(k == KD - 1))
        mm.then_inc(K.unit_used.sem, 1)

    base = K.unit_used.n

    @K.block.tensor
    def _(pe):
        if turns == 1:
            for j in range(RING):
                unit(pe, j, 0)
        elif turns:
            with pe.Fori(0, turns) as i:
                for j in range(RING):
                    unit(pe, j, i)
        for j in range(rest):
            unit(pe, j, turns)

    @K.block.vector
    def _(dve):
        dve.sem_inc(main_free.sem, RING)

        def one(j, i):
            dve.wait_ge(K.unit_used.sem, i * RING + (j + base + 1))
            evac_main(dve, i * RING + j, K.ps[j]).then_inc(main_free.sem, 1)
        if turns == 1:
            for j in range(RING):
                one(j, 0)
        elif turns:
            with dve.Fori(0, turns) as i:
                for j in range(RING):
                    one(j, i)
        for j in range(rest):
            one(j, turns)

    if with_ctx:
        @K.block.scalar
        def _(act):
            act.sem_inc(ctx_free.sem, RING)

            def one(j, i):
                act.wait_ge(K.unit_used.sem, i * RING + (j + base + 1))
                evac_ctx(act, i * RING + j, K.ps[4 + j]).then_inc(ctx_free.sem, 1)
            if turns == 1:
                for j in range(RING):
                    one(j, 0)
            elif turns:
                with act.Fori(0, turns) as i:
                    for j in range(RING):
                        one(j, i)
            for j in range(rest):
                one(j, turns)
        ctx_free.n += RING + count
    main_free.n += RING + count
    K.unit_used.n += count
    K.unit += count
    meet(K)



def softmax_attention(K, items, scale, neg_lam=None):
    n_comp = len(items[0]["scores"])
    scored, max_ready, exped, weighted, turned_up, turned_out, mixed, put = (K.signals[n] for n in (
        "scored", "max_ready", "exped", "weighted", "turned_up", "turned_out", "mixed", "put"))
    n_items = len(items)
    kmax = max(i["kw"] for i in items)
    biased = items[0]["bias"] is not None
    split = kmax > S
    copies = 2 if split else 1
    with ExitStack() as ctx:
        probs = arena(K, ctx, "probs", [P, 2, n_comp, kmax])
        turned = arena(K, ctx, "turned", [P, 2, kmax])
        logits = arena(K, ctx, "logits", [P, 2, kmax]) if biased else None
        neg_max = arena(K, ctx, "neg_max", [P, n_items, n_comp])
        row_sum = arena(K, ctx, "row_sum", [P, n_items, n_comp])
        inv = arena(K, ctx, "inv", [P, n_items, n_comp])

        def score_tile(t, c, a, b):
            first = 2 * S * ((t * n_comp + c) % 2)
            return K.psum[:, first + a:first + b]

        @K.block.tensor
        def _(pe):
            def scores(t):
                for c in range(n_comp):
                    n = t * n_comp + c
                    if n >= 2:
                        pe.wait_ge(exped.sem, exped.base + n - 1)
                    for group in items[t]["scores"][c]:
                        for g, (lhs, rhs, c0, w) in enumerate(group):
                            mm = pe.matmul(score_tile(t, c, c0, c0 + w), lhs, rhs,
                                           start=(g == 0), stop=(g == len(group) - 1),
                                           skip_group_check=len(group) > 1)
                    scored.up(mm)

            def turn(t):
                if n_comp == 1:
                    pe.wait_ge(exped.sem, exped.base + t + 1)
                else:
                    pe.wait_ge(weighted.sem, weighted.base + t + 1)
                if t >= 1:
                    pe.wait_ge(turned_out.sem, turned_out.base + copies * t)
                for b in range(items[t]["kw"] // P):
                    mm = pe.transpose(K.psum[:, 4 * S + b * P:4 * S + b * P + P],
                                      probs[:, t % 2, 0, b * P:b * P + P], const(K, "ident"))
                turned_up.up(mm)

            def mix(t):
                pe.wait_ge(turned_out.sem, turned_out.base + copies * (t + 1))
                if t >= 2:
                    pe.wait_ge(put.sem, put.base + t - 1)
                tiles = items[t]["tiles"]
                for b, tile in enumerate(tiles):
                    mm = pe.matmul(K.ps[6 + t % 2][:, 0:HD], turned[:, t % 2, b * P:b * P + P],
                                   items[t]["v"](tile), start=(b == 0), stop=(b == len(tiles) - 1))
                mixed.up(mm)

            for t in range(n_items + 2):
                if t < n_items:
                    scores(t)
                if 0 <= t - 1 < n_items:
                    turn(t - 1)
                if 0 <= t - 2 < n_items:
                    mix(t - 2)

        @K.block.vector
        def _(dve):
            def maxima(t):
                kw, bias = items[t]["kw"], items[t]["bias"]
                for c in range(n_comp):
                    dve.wait_ge(scored.sem, scored.base + t * n_comp + c + 1)
                    m = neg_max[:, t, c:c + 1]
                    if bias is None:
                        link(dve, K.dve_step, dve.reduce_max(m, score_tile(t, c, 0, kw), AX, negate=True))
                        max_ready.up(dve.tensor_scalar(m, m, scale, None, ALU.mult))
                        continue
                    if t >= 2:
                        dve.wait_ge(exped.sem, exped.base + t - 1)
                    ins = dve.scalar_tensor_tensor(logits[:, t % 2, 0:S], score_tile(t, c, 0, S), scale, bias,
                                                   ALU.mult, ALU.add)
                    if kw > S:
                        ins = dve.tensor_scalar(logits[:, t % 2, S:kw], score_tile(t, c, S, kw), scale, None,
                                                ALU.mult)
                    link(dve, K.dve_step, ins)
                    max_ready.up(dve.reduce_max(m, logits[:, t % 2, 0:kw], AX, negate=True))

            def combine(t):
                kw = items[t]["kw"]
                dve.wait_ge(exped.sem, exped.base + (t + 1) * n_comp)
                link(dve, K.dve_step, dve.reciprocal(inv[:, t, :], row_sum[:, t, :]))
                link(dve, K.dve_step, dve.tensor_tensor(inv[:, t, 1:2], inv[:, t, 1:2], neg_lam, ALU.mult))
                p0, p1 = probs[:, t % 2, 0, 0:kw], probs[:, t % 2, 1, 0:kw]
                link(dve, K.dve_step, dve.tensor_scalar(p1, p1, inv[:, t, 1:2], None, ALU.mult))
                weighted.up(dve.scalar_tensor_tensor(p0, p0, inv[:, t, 0:1], p1, ALU.mult, ALU.add))

            def copy_turned(t):
                dve.wait_ge(turned_up.sem, turned_up.base + t + 1)
                if t >= 2:
                    dve.wait_ge(mixed.sem, mixed.base + t - 1)
                w = min(items[t]["kw"], S)
                turned_out.up(dve.tensor_copy(turned[:, t % 2, 0:w], K.psum[:, 4 * S:4 * S + w]))

            def output(t):
                dve.wait_ge(mixed.sem, mixed.base + t + 1)
                src = K.ps[6 + t % 2][:, 0:HD]
                if n_comp == 1:
                    link(dve, K.dve_step, dve.reciprocal(inv[:, t, :], row_sum[:, t, :]))
                    put.up(dve.tensor_scalar(items[t]["out"], src, inv[:, t, 0:1], None, ALU.mult))
                else:
                    put.up(dve.tensor_copy(items[t]["out"], src))

            for t in range(n_items + 3):
                if t < n_items:
                    maxima(t)
                if n_comp == 2 and 0 <= t - 1 < n_items:
                    combine(t - 1)
                if 0 <= t - 2 < n_items:
                    copy_turned(t - 2)
                if 0 <= t - 3 < n_items:
                    output(t - 3)

        @K.block.scalar
        def _(act):
            def exponentials(t):
                kw, bias = items[t]["kw"], items[t]["bias"]
                if t >= 2:
                    act.wait_ge(turned_up.sem, turned_up.base + t - 1)
                for c in range(n_comp):
                    act.wait_ge(max_ready.sem, max_ready.base + t * n_comp + c + 1)
                    src = logits[:, t % 2, 0:kw] if bias is not None else score_tile(t, c, 0, kw)
                    exped.up(act.activation(probs[:, t % 2, c, 0:kw], src, ACT.Exp, bias=neg_max[:, t, c:c + 1],
                                            scale=1.0 if bias is not None else scale,
                                            accum_out=row_sum[:, t, c:c + 1]))

            def copy_turned(t):
                act.wait_ge(turned_up.sem, turned_up.base + t + 1)
                if t >= 2:
                    act.wait_ge(mixed.sem, mixed.base + t - 1)
                turned_out.up(act.copy(turned[:, t % 2, S:kmax], K.psum[:, 5 * S:4 * S + kmax]))

            for t in range(n_items + 2):
                if t < n_items:
                    exponentials(t)
                if split and 0 <= t - 2 < n_items:
                    copy_turned(t - 2)
        meet(K)


def to_feature_major(K, y, tiles, put):
    turned_up, put_done = K.signals["turned_up"], K.signals["put"]

    @K.block.tensor
    def _(pe):
        for u in range(2):
            for n, m in enumerate(tiles):
                mm = pe.transpose(K.ps[u][:, n * P:n * P + P], y[:, m, u * P:u * P + P], const(K, "ident"))
            turned_up.up(mm)

    @K.block.vector
    def _(dve):
        for u in range(2):
            dve.wait_ge(turned_up.sem, turned_up.base + u + 1)
            put_done.up(put(dve, u, K.ps[u][:, 0:len(tiles) * P]))
    meet(K)



def forgetting_attention(K, p, v, y):
    gates, = (K.signals[n] for n in ("prepared",))
    rows = slice(64, 64 + H)
    with ExitStack() as ctx:
        x = arena(K, ctx, "gate_x", [P, S])
        a = arena(K, ctx, "gate_a", [P, S])
        cum = arena(K, ctx, "neg_cum", [P, S])

        @K.block.vector
        def _(dve):
            dve.memset(cum[:, :], 0.0)
            link(dve, K.dve_step, dve.tensor_scalar(x[rows, :], p[rows, MISC, PAD:PAD + S],
                                                    prm(K, "b_f", rows=rows), None, ALU.add))
            gates.up(dve.tensor_scalar(a[rows, :], x[rows, :], -1.0, None, ALU.mult))
            dve.wait_ge(K.signals["soft"].sem, K.signals["soft"].base + 1)
            link(dve, K.dve_step, dve.tensor_scalar(x[rows, :], x[rows, :], 0.0, -1.0, ALU.min, ALU.mult))
            link(dve, K.dve_step, dve.tensor_tensor(x[rows, :], x[rows, :], a[rows, :], ALU.add))
            link(dve, K.dve_step, dve.tensor_tensor_scan(cum[rows, :], const(K, "keep_all", rows), x[rows, :], 0.0,
                                                         ALU.mult, ALU.add))

        @K.block.scalar
        def _(act):
            act.wait_ge(gates.sem, gates.base + 1)
            for func, scale, bias in ((ACT.Abs, 1.0, 0.0), (ACT.Exp, -1.0, 0.0)):
                link(act, K.act_step, act.activation(a[rows, :], a[rows, :], func, scale=scale))
            K.signals["soft"].up(act.activation(a[rows, :], a[rows, :], ACT.Ln, bias=K.one[rows, 0:1]))
        meet(K)

        items = []
        for h in range(H):
            i, r = h // 2, slice(64 * (h % 2), 64 * (h % 2) + HD)
            for t in range(NT):
                kw = (t + 1) * P
                q = p[r, FQ + i, PAD + t * P:PAD + t * P + P]
                items.append(dict(
                    scores=[[[(q, p[r, FK + i, PAD:PAD + kw], 0, kw),
                              (const(K, "head_row")[:, h * P:h * P + P], cum[:, 0:kw], 0, kw),
                              (const(K, "ident"), const(K, "causal_add"), t * P, P)]]],
                    kw=kw, tiles=range(t + 1), bias=None,
                    v=lambda m, h=h: v[:, m, h * HD:h * HD + HD], out=y[:, t, h * HD:h * HD + HD]))
        softmax_attention(K, items, HD ** -0.5)



def stick_breaking_attention(K, p, v, y):
    scored, zed, softp, summed, diff, weighed, mixed, put = (K.signals[n] for n in (
        "scored", "exped", "soft", "summed", "prepared", "weighted", "mixed", "put"))
    with ExitStack() as ctx:
        z = arena(K, ctx, "stick_z", [P, 2, S])
        e = arena(K, ctx, "stick_e", [P, 2, S])
        sp = arena(K, ctx, "stick_softplus", [P, 2, NT, S])
        w = arena(K, ctx, "stick_weights", [P, 2, NT, S])
        steps = [(h, t) for h in range(H) for t in reversed(range(NT))]

        @K.block.tensor
        def _(pe):
            def scores(n):
                h, t = steps[n]
                i, r = h // 2, slice(64 * (h % 2), 64 * (h % 2) + HD)
                if n >= 2:
                    pe.wait_ge(softp.sem, softp.base + n - 1)
                    pe.wait_ge(zed.sem, zed.base + n - 1)
                scored.up(pe.matmul(K.ps[n % 2][:, t * P:S], p[r, SK + i, PAD + t * P:PAD + t * P + P],
                                    p[r, SQ + i, PAD + t * P:PAD + S], start=True, stop=True))

            def sums(n):
                h, t = steps[n]
                pe.wait_ge(softp.sem, softp.base + n + 1)
                if n >= 2:
                    pe.wait_ge(diff.sem, diff.base + n - 1)
                bank = K.ps[2 + n % 2]
                pe.matmul(bank[:, t * P:S], const(K, "tri_ge"), sp[:, h % 2, t, t * P:S],
                          start=True, stop=False, skip_group_check=True)
                for j in range(t + 1, NT):
                    pe.matmul(bank[:, j * P:S], const(K, "ones"), sp[:, h % 2, j, j * P:S],
                              start=False, stop=False, skip_group_check=True)
                summed.up(pe.matmul(bank[:, t * P:t * P + P], const(K, "ident"), const(K, "stick_big"),
                                    start=False, stop=True, skip_group_check=True))

            def mix(h):
                pe.wait_ge(weighed.sem, weighed.base + NT * (h + 1))
                if h >= 2:
                    pe.wait_ge(put.sem, put.base + h - 1)
                bank = K.ps[4 + h % 2]
                for m in range(NT):
                    for t in range(m + 1):
                        mm = pe.matmul(bank[:, m * HD:m * HD + HD], w[:, h % 2, t, m * P:m * P + P],
                                       v[:, t, h * HD:h * HD + HD], start=(t == 0), stop=(t == m))
                mixed.up(mm)

            for n in range(len(steps) + 1):
                if n < len(steps):
                    scores(n)
                if n >= 1:
                    sums(n - 1)
                if n % NT == 1 and n > NT:
                    mix(n // NT - 1)
            mix(H - 1)

        @K.block.scalar
        def _(act):
            def soft(n):
                h, t = steps[n]
                src = K.ps[n % 2][:, t * P:S]
                act.wait_ge(scored.sem, scored.base + n + 1)
                if n >= 2:
                    act.wait_ge(softp.sem, softp.base + n - 1)
                    act.wait_ge(diff.sem, diff.base + n - 1)
                act.activation(z[:, n % 2, t * P:S], src, ACT.Identity, scale=HD ** -0.5)
                link(act, K.act_step, act.activation(e[:, n % 2, t * P:S], src, ACT.Abs, scale=HD ** -0.5))
                link(act, K.act_step, act.activation(e[:, n % 2, t * P:S], e[:, n % 2, t * P:S], ACT.Exp,
                                                     scale=-1.0))
                zed.up(act.activation(e[:, n % 2, t * P:S], e[:, n % 2, t * P:S], ACT.Ln, bias=K.one[:, 0:1]))

            def weigh(n):
                h, t = steps[n]
                act.wait_ge(diff.sem, diff.base + n + 1)
                part = w[:, h % 2, t, t * P:S]
                weighed.up(act.activation(part, part, ACT.Exp))

            for n in range(len(steps) + 1):
                if n < len(steps):
                    soft(n)
                if n >= 1:
                    weigh(n - 1)

        @K.block.vector
        def _(dve):
            def soft(n):
                h, t = steps[n]
                dve.wait_ge(zed.sem, zed.base + n + 1)
                if h >= 2 and t == NT - 1:
                    dve.wait_ge(summed.sem, summed.base + NT * (h - 1))
                part = sp[:, h % 2, t, t * P:S]
                link(dve, K.dve_step, dve.scalar_tensor_tensor(part, z[:, n % 2, t * P:S], 0.0,
                                                               e[:, n % 2, t * P:S], ALU.max, ALU.add))
                part = sp[:, h % 2, t, t * P:t * P + P]
                softp.up(dve.tensor_tensor(part, part, const(K, "strict_t"), ALU.mult))

            def differ(n):
                h, t = steps[n]
                dve.wait_ge(summed.sem, summed.base + n + 1)
                if h >= 2 and t == NT - 1:
                    dve.wait_ge(mixed.sem, mixed.base + h - 1)
                diff.up(dve.tensor_tensor(w[:, h % 2, t, t * P:S], z[:, n % 2, t * P:S],
                                          K.ps[2 + n % 2][:, t * P:S], ALU.subtract))

            def output(h):
                dve.wait_ge(mixed.sem, mixed.base + h + 1)
                put.up(dve.tensor_copy(y[:, :, h * HD:h * HD + HD],
                                       K.ps[4 + h % 2][:, 0:NT * HD].rearrange("p (m d) -> p m d", m=NT)))

            for n in range(len(steps) + 1):
                if n < len(steps):
                    soft(n)
                if n >= 1:
                    differ(n - 1)
                if n % NT == 2 and n > NT:
                    output(n // NT - 1)
            output(H - 1)
        meet(K)



def rg_lru(K, p, out):
    conv, gated, rate_ready, done = (K.signals[n] for n in ("prepared", "scored", "exped", "weighted"))
    with ExitStack() as ctx:
        xc = arena(K, ctx, "lru_x", [P, 2, S])
        r = arena(K, ctx, "lru_r", [P, 2, S])
        g = arena(K, ctx, "lru_i", [P, 2, S])
        a = arena(K, ctx, "lru_a", [P, 2, S])
        th = arena(K, ctx, "lru_tanh", [P, 2, S])
        s8 = arena(K, ctx, "lru_rate", [P, 2])
        w = arena(K, ctx, "lru_w", [P, 4, P])

        @K.block.gpsimd
        def _(pool):
            K.loaded_late.up(pool.dma_start(w[:, :, :], K.lru_w_dram.rearrange("p (a b) -> p a b", a=4)), 16)
        w_value = K.loaded_late.n

        @K.block.vector
        def _(dve):
            for i in range(2):
                x = lambda k: p[:, LX + i, PAD - 3 + k:PAD - 3 + k + S]
                cw = lambda k: prm(K, "conv_w", 2 * k + i)
                link(dve, K.dve_step, dve.tensor_scalar(xc[:, i], x(0), cw(0), prm(K, "conv_b", i),
                                                        ALU.mult, ALU.add))
                for k in range(1, 4):
                    ins = dve.scalar_tensor_tensor(xc[:, i], x(k), cw(k), xc[:, i], ALU.mult, ALU.add)
                    if k < 3:
                        link(dve, K.dve_step, ins)
                conv.up(ins)
            for i in range(2):
                dve.wait_ge(rate_ready.sem, rate_ready.base + 1 + i)
                link(dve, K.dve_step, dve.tensor_tensor(g[:, i], g[:, i], xc[:, i], ALU.mult))
                link(dve, K.dve_step, dve.scalar_tensor_tensor(th[:, i], r[:, i], 1.0, th[:, i], ALU.add, ALU.mult))
            done.up(dve.tensor_scalar(th[:, :, :], th[:, :, :], 0.0, None, ALU.max))
            dve.wait_ge(rate_ready.sem, rate_ready.base + 4)
            for i in range(2):
                link(dve, K.dve_step, dve.tensor_tensor(g[:, i], g[:, i], th[:, i], ALU.mult))
                link(dve, K.dve_step, dve.tensor_tensor_scan(xc[:, i], a[:, i], g[:, i], 0.0, ALU.mult, ALU.add))
                out(dve, i, xc[:, i])

        @K.block.tensor
        def _(pe):
            pe.wait_ge(K.loaded_late.sem, w_value)
            for i in range(2):
                pe.wait_ge(conv.sem, conv.base + i + 1)
                pe.matmul(K.ps[2 * i][:, :], w[:, i], xc[:, i], start=True, stop=True)
                gated.up(pe.matmul(K.ps[2 * i + 1][:, :], w[:, 2 + i], xc[:, i], start=True, stop=True))

        @K.block.scalar
        def _(act):
            t0, t1 = th[:, 0, 0:2], th[:, 0, 2:4]
            link(act, K.act_step, act.activation(t0, prm(K, "lam", 0, 2), ACT.Abs))
            link(act, K.act_step, act.activation(t0, t0, ACT.Exp, scale=-1.0))
            link(act, K.act_step, act.activation(t0, t0, ACT.Ln, bias=K.one[:, 0:1]))
            link(act, K.act_step, act.activation(t1, prm(K, "lam", 0, 2), ACT.Relu, scale=-1.0))
            link(act, K.act_step, act.activation(t1[:, 0:1], t1[:, 0:1], ACT.Identity, bias=t0[:, 0:1]))
            link(act, K.act_step, act.activation(t1[:, 1:2], t1[:, 1:2], ACT.Identity, bias=t0[:, 1:2]))
            link(act, K.act_step, act.activation(s8[:, :], t1, ACT.Identity, scale=-8.0))
            act.wait_ge(gated.sem, gated.base + 2)
            for i in range(2):
                act.activation(r[:, i], K.ps[2 * i][:, :], ACT.Sigmoid, bias=prm(K, "b_a", i))
                link(act, K.act_step, act.activation(g[:, i], K.ps[2 * i + 1][:, :], ACT.Sigmoid,
                                                     bias=prm(K, "b_x", i)))
            for i in range(2):
                link(act, K.act_step, act.activation(r[:, i], r[:, i], ACT.Identity, scale=s8[:, i:i + 1]))
                act.activation(a[:, i], r[:, i], ACT.Exp)
                link(act, K.act_step, act.activation(th[:, i], r[:, i], ACT.Tanh, scale=-1.0))
                rate_ready.up(act.activation(r[:, i], r[:, i], ACT.Exp, scale=2.0))
            act.wait_ge(done.sem, done.base + 1)
            for i in range(2):
                rate_ready.up(act.activation(th[:, i], th[:, i], ACT.Sqrt))
        meet(K)



def rwkv(K, p, y):
    sig = K.signals
    with ExitStack() as ctx:
        nd = arena(K, ctx, "log_decay", [P, 2, S])
        cl = arena(K, ctx, "cum_log_decay", [P, 2, S])
        rate = arena(K, ctx, "rate", [P, 2, S])
        kk = arena(K, ctx, "kk", [P, 2, S])
        t0 = arena(K, ctx, "rwkv_t0", [P, 2, S])
        t1 = arena(K, ctx, "rwkv_t1", [P, 2, S])
        t2 = arena(K, ctx, "rwkv_t2", [P, 2, S])
        rkr = arena(K, ctx, "rwkv_rkr", [P, 2, S])
        decay_end = arena(K, ctx, "decay_end", [P, 2, NT])
        one_less = arena(K, ctx, "one_less_k_a", [P, 2])
        inner = ctx.enter_context(ExitStack())
        shifted = arena(K, inner, "shifted", [P, S])
        low = arena(K, inner, "low_rank", [P, S])
        lora = arena(K, inner, "lora", [64, G])
        col = lambda u: p[:, u:u + 2, PAD:PAD + S]
        r, k, v = col(RR), col(RK), col(RV)

        @K.block.gpsimd
        def _(pool):
            K.loaded_late.up(pool.dma_start(lora[:, :], K.lora_dram), 16)
        lora_value = K.loaded_late.n

        mixed, low_ready, projected, act_out, kk_out, normed = (sig[n] for n in (
            "prepared", "soft", "scored", "exped", "weighted", "summed"))

        @K.block.vector
        def _(dve):
            for n, u in enumerate((MISC, RR, RR + 1, RK, RK + 1, RV, RV + 1)):
                rows = slice(0, 64) if u == MISC else slice(0, P)
                if n:
                    dve.wait_ge(mixed.sem, mixed.base + n)
                cur, prev = p[rows, u, PAD:PAD + S], p[rows, u, PAD - 1:PAD - 1 + S]
                link(dve, K.dve_step, dve.tensor_tensor(shifted[rows, :], prev, cur, ALU.subtract))
                mixed.up(dve.scalar_tensor_tensor(cur, shifted[rows, :], prm(K, "mu", (n - 1) % 7, rows=rows), cur,
                                                  ALU.mult, ALU.add))
            dve.wait_ge(mixed.sem, mixed.base + 7)
            dve.tensor_scalar(one_less[:, :], prm(K, "k_a", 0, 2), -1.0, 1.0, ALU.mult, ALU.add)
            for i in range(2):
                ins = dve.tensor_scalar(kk[:, i], k[:, i], prm(K, "k_k", i), None, ALU.mult)
            kk_out.up(ins)
            dve.wait_ge(act_out.sem, act_out.base + 1)
            link(dve, K.dve_step, dve.tensor_scalar(nd[:, :, :], nd[:, :, :], -DECAY, None, ALU.mult))
            for i in range(2):
                ins = dve.tensor_tensor_scan(cl[:, i], const(K, "chunk_keep"), nd[:, i], 0.0, ALU.mult, ALU.add)
            link(dve, K.dve_step, ins)
            kk_out.up(dve.tensor_tensor(nd[:, :, :], cl[:, :, :], nd[:, :, :], ALU.subtract))
            for i in range(2):
                ins = dve.tensor_scalar(t0[:, i], rate[:, i], prm(K, "k_a", i), one_less[:, i:i + 1],
                                        ALU.mult, ALU.add)
            link(dve, K.dve_step, ins)
            link(dve, K.dve_step, dve.tensor_tensor(k, k, t0[:, :, :], ALU.mult))
            for i in range(2):
                dve.scalar_tensor_tensor(rkr[:, i], r[:, i], prm(K, "r_k", i), k[:, i], ALU.mult, ALU.mult)
            dve.wait_ge(normed.sem, normed.base + 1)
            for i in range(2):
                ins = dve.tensor_scalar(t0[:, i], K.ps[4 + i][:, :], 1e-12, None, ALU.max)
            kk_out.up(ins)
            dve.wait_ge(act_out.sem, act_out.base + 2)
            link(dve, K.dve_step, dve.tensor_tensor(kk[:, :, :], kk[:, :, :], t0[:, :, :], ALU.mult))
            dve.wait_ge(act_out.sem, act_out.base + 3)
            link(dve, K.dve_step, dve.tensor_tensor(rate[:, :, :], rate[:, :, :], kk[:, :, :], ALU.mult))
            dve.tensor_tensor(rate[:, :, :], rate[:, :, :], t2[:, :, :], ALU.mult)
            dve.scalar_tensor_tensor(kk[:, :, :], kk[:, :, :], -1.0, nd[:, :, :], ALU.mult, ALU.mult)
            dve.tensor_tensor(k, k, t2[:, :, :], ALU.mult)
            dve.tensor_tensor(r, r, t1[:, :, :], ALU.mult)

        @K.block.scalar
        def _(act):
            act.wait_ge(mixed.sem, mixed.base + 1)
            low_ready.up(act.activation(low[0:32, :], p[0:32, MISC, PAD:PAD + S], ACT.Tanh))
            low_ready.up(act.copy(low[32:64, :], p[32:64, MISC, PAD:PAD + S]))
            act.wait_ge(projected.sem, projected.base + 1)
            for i in range(2):
                act.activation(nd[:, i], K.ps[i][:, :], ACT.Sigmoid, bias=prm(K, "w0", i))
                ins = act.activation(rate[:, i], K.ps[2 + i][:, :], ACT.Sigmoid, bias=prm(K, "a0", i))
            act_out.up(ins)
            act.wait_ge(kk_out.sem, kk_out.base + 1)
            low_ready.up(act.activation(t1[:, :, :], kk[:, :, :], ACT.Square))
            act.wait_ge(kk_out.sem, kk_out.base + 3)
            link(act, K.act_step, act.activation(t0[:, :, :], t0[:, :, :], ACT.Ln))
            act_out.up(act.activation(t0[:, :, :], t0[:, :, :], ACT.Exp, scale=-0.5))
            act.activation(t1[:, :, :], cl[:, :, :], ACT.Exp, bias=K.half[:, 0:1])
            act.activation(t2[:, :, :], cl[:, :, :], ACT.Exp, bias=K.minus_half[:, 0:1], scale=-1.0)
            act.activation(decay_end[:, :, :], cl[:, :, CH - 1::CH], ACT.Exp)
            act_out.up(act.activation(nd[:, :, :], nd[:, :, :], ACT.Exp, bias=K.half[:, 0:1]))

        @K.block.tensor
        def _(pe):
            pe.wait_ge(K.loaded_late.sem, lora_value)
            pe.wait_ge(low_ready.sem, low_ready.base + 2)
            for i in range(2):
                pe.matmul(K.ps[i][:, :], lora[0:32, i * P:i * P + P], low[0:32, :], start=True, stop=True)
            for i in range(2):
                mm = pe.matmul(K.ps[2 + i][:, :], lora[32:64, i * P:i * P + P], low[32:64, :], start=True, stop=True)
            projected.up(mm)
            pe.wait_ge(low_ready.sem, low_ready.base + 3)
            for i in range(2):
                mm = pe.matmul(K.ps[4 + i][:, :], const(K, "block64"), t1[:, i], start=True, stop=True)
            normed.up(mm)
        meet(K)
        inner.close()

        tok = [x[:, :, :].rearrange("p i s -> p (i s)").rearrange("p (c f) -> p c f", c=NT) for x in (t0, t1, t2, cl)]
        a_tok, b_tok, k_tok, v_tok = tok
        turned_up, turned_out = sig["turned_up"], sig["turned_out"]

        @K.block.tensor
        def _(pe):
            for q, x in enumerate((kk, rate, k, v)):
                for i in range(2):
                    for c in range(NT):
                        mm = pe.transpose(K.ps[2 * q + i][:, c * P:c * P + P], x[:, i, c * P:c * P + P],
                                          const(K, "ident"))
                    turned_up.up(mm)

        @K.block.vector
        def _(dve):
            for n in range(0, 8, 2):
                dve.wait_ge(turned_up.sem, turned_up.base + n + 1)
                dve.tensor_copy(tok[n // 2][:, :, 0:P], K.ps[n][:, :].rearrange("p (c f) -> p c f", c=NT))

        @K.block.scalar
        def _(act):
            for n in range(1, 8, 2):
                act.wait_ge(turned_up.sem, turned_up.base + n + 1)
                act.copy(tok[n // 2][:, :, P:2 * P], K.ps[n][:, :].rearrange("p (c f) -> p c f", c=NT))
        meet(K)
        rwkv_chunks(K, kk, rate, k, r, a_tok, b_tok, k_tok, v_tok, decay_end, rkr, y)


def rwkv_chunks(K, ad, bd, kd, rd, a_tok, b_tok, k_tok, v_tok, decay_end, rkr, y):
    sig = K.signals
    produced, taken, x_ready, x_used, m_up, m_out, t_up, t_out, w_up, w_out, u_up, u_out, y_up, y_out, s_out = (
        sig[n] for n in ("produced", "taken", "x_ready", "x_used", "m_up", "m_out", "t_up", "t_out", "w_up",
                         "w_out", "u_up", "u_out", "y_up", "y_out", "s_out"))
    heads = [(e, i) for e in range(2) for i in range(2)]
    wide = lambda ap: ap.unsqueeze(1).to_broadcast([P, 2, P])
    with ExitStack() as ctx:
        mat = lambda n: arena(K, ctx, n, [P, 2, 2, P])
        a_mat, ak_t, rk_t, rb_t, t_mat, t_t, m_mat = (mat(n) for n in (
            "a_mat", "ak_t", "rk_t", "rb_t", "t_mat", "t_t", "m_mat"))
        x_mat = arena(K, ctx, "x_mat", [P, 2, 2, 2, P])
        ta_t = arena(K, ctx, "ta_t", [P, 2, P])
        w1 = arena(K, ctx, "w1", [P, G])
        u = arena(K, ctx, "u", [P, G])
        state = arena(K, ctx, "state", [P, 2, HD])
        bonus = arena(K, ctx, "bonus", [P, NT, H])
        row64 = lambda e: slice(64 * e, 64 * e + HD)
        hcol = lambda e, i: slice(i * P + e * HD, i * P + e * HD + HD)

        @K.block.tensor
        def _(pe):
            for c in range(NT):
                tc_ = slice(c * CH, c * CH + CH)
                if c:
                    pe.wait_ge(y_out.sem, y_out.base + c)
                    pe.wait_ge(s_out.sem, s_out.base + c + 1)
                else:
                    pe.wait_ge(s_out.sem, s_out.base + 1)
                for e in range(2):
                    r = row64(e)
                    for n, (l, m) in enumerate(((ad, bd), (bd, ad), (kd, ad), (kd, rd), (bd, rd))):
                        for i in range(2):
                            at = (n % 2) * 2 * P + i * P
                            mm = pe.matmul(K.ps[3 * e + n // 2][:, at:at + P], l[r, i, tc_], m[r, i, tc_],
                                           start=True, stop=True)
                for i in range(2):
                    mm = pe.matmul(K.ps[7][:, i * 2:i * 2 + 2], rkr[:, i, tc_], const(K, "head_pair"),
                                   start=True, stop=True)
                produced.up(mm)
                for lev in range(1, LEVELS):
                    n = c * (LEVELS - 1) + lev - 1
                    pe.wait_ge(x_ready.sem, x_ready.base + n + 1)
                    pe.wait_ge(t_out.sem, t_out.base + c * LEVELS + lev)
                    for g, (e, i) in enumerate(heads):
                        mm = pe.matmul(K.ps[6][:, g * P:g * P + P], x_mat[:, n % 2, e, i], t_t[:, e, i],
                                       start=True, stop=True)
                    m_up.up(mm)
                    pe.wait_ge(m_out.sem, m_out.base + n + 1)
                    for g, (e, i) in enumerate(heads):
                        pe.matmul(K.ps[0][:, g * P:g * P + P], t_mat[:, e, i], m_mat[:, e, i],
                                  start=True, stop=True)
                    for g, (e, i) in enumerate(heads):
                        mm = pe.matmul(K.ps[1][:, g * P:g * P + P], m_mat[:, e, i], t_mat[:, e, i],
                                       start=True, stop=True)
                    t_up.up(mm)
                pe.wait_ge(t_out.sem, t_out.base + (c + 1) * LEVELS)
                for e, i in heads:
                    mm = pe.matmul(K.ps[2][:, hcol(e, i)], ak_t[:, e, i], v_tok[:, c, hcol(e, i)],
                                   start=True, stop=True)
                for e, i in heads:
                    mm = pe.matmul(K.ps[3][row64(e), i * P:i * P + P], a_tok[:, c, hcol(e, i)], t_t[:, e, i],
                                   start=True, stop=True)
                w_up.up(mm)
                pe.wait_ge(w_out.sem, w_out.base + c + 1)
                for e, i in heads:
                    pe.matmul(K.ps[4 + e][:, i * HD:i * HD + HD], t_t[:, e, i], w1[:, hcol(e, i)],
                              start=True, stop=False)
                    mm = pe.matmul(K.ps[4 + e][:, i * HD:i * HD + HD], ta_t[row64(e), i], state[row64(e), i],
                                   start=False, stop=True)
                u_up.up(mm)
                pe.wait_ge(u_out.sem, u_out.base + c + 1)
                for e, i in heads:
                    to = K.ps[2 + e][:, P * 2 + i * HD:P * 2 + i * HD + HD]
                    pe.matmul(to, rd[row64(e), i, tc_], state[row64(e), i], start=True, stop=False)
                    pe.matmul(to, rb_t[:, e, i], u[:, hcol(e, i)], start=False, stop=False)
                    pe.matmul(to, rk_t[:, e, i], v_tok[:, c, hcol(e, i)], start=False, stop=True)
                for e, i in heads:
                    to = K.ps[6][row64(e), i * HD:i * HD + HD]
                    pe.matmul(to, b_tok[:, c, hcol(e, i)], u[:, hcol(e, i)], start=True, stop=False)
                    mm = pe.matmul(to, k_tok[:, c, hcol(e, i)], v_tok[:, c, hcol(e, i)], start=False, stop=True)
                y_up.up(mm)

        @K.block.gpsimd
        def _(pool):
            for n in range(NT * (LEVELS - 1)):
                c, lev = divmod(n, LEVELS - 1)
                lev += 1
                pool.wait_ge(taken.sem, taken.base + c + 1)
                if n >= 2:
                    pool.wait_ge(m_up.sem, m_up.base + n - 1)
                mask = const(K, "level")[:, lev * P:lev * P + P]
                for e in range(2):
                    ins = pool.tensor_tensor(x_mat[:, n % 2, e], a_mat[:, e], wide(mask), ALU.mult)
                x_ready.up(ins)

        @K.block.vector
        def _(dve):
            s_out.up(dve.memset(state[:, :, :], 0.0))
            for c in range(NT):
                dve.wait_ge(produced.sem, produced.base + c + 1)
                if c:
                    dve.wait_ge(x_ready.sem, x_ready.base + c * (LEVELS - 1))
                prod = lambda n, e: K.ps[3 * e + n // 2][:, (n % 2) * 2 * P:(n % 2) * 2 * P + 2 * P] \
                    .rearrange("p (i t) -> p i t", i=2)
                for e in range(2):
                    ins = dve.tensor_copy(a_mat[:, e], prod(0, e))
                taken.up(ins)
                for e in range(2):
                    dve.tensor_tensor(t_mat[:, e], prod(0, e), wide(const(K, "level")[:, 0:P]), ALU.mult)
                    ins = dve.tensor_tensor(t_t[:, e], prod(1, e), wide(const(K, "level0_t")), ALU.mult)
                link(dve, K.dve_step, ins)
                for e in range(2):
                    dve.tensor_tensor(t_mat[:, e], t_mat[:, e], wide(const(K, "ident")), ALU.add)
                    dve.tensor_tensor(t_t[:, e], t_t[:, e], wide(const(K, "ident")), ALU.add)
                for e in range(2):
                    dve.tensor_tensor(ak_t[:, e], prod(2, e), wide(const(K, "strict_t")), ALU.mult)
                    dve.tensor_tensor(rk_t[:, e], prod(3, e), wide(const(K, "incl_t")), ALU.mult)
                    dve.tensor_tensor(rb_t[:, e], prod(4, e), wide(const(K, "incl_t")), ALU.mult)
                t_out.up(dve.tensor_copy(bonus[:, c, :], K.ps[7][:, 0:H]))
                for lev in range(1, LEVELS):
                    n = c * (LEVELS - 1) + lev - 1
                    dve.wait_ge(t_up.sem, t_up.base + n + 1)
                    dve.tensor_tensor(t_t[:, :, :, :].rearrange("p e i t -> p (e i t)"),
                                      t_t[:, :, :, :].rearrange("p e i t -> p (e i t)"), K.ps[0][:, :], ALU.add)
                    t_out.up(dve.tensor_tensor(t_mat[:, :, :, :].rearrange("p e i t -> p (e i t)"),
                                               t_mat[:, :, :, :].rearrange("p e i t -> p (e i t)"),
                                               K.ps[1][:, :], ALU.add))
                dve.wait_ge(w_up.sem, w_up.base + c + 1)
                dve.tensor_copy(w1[:, :], K.ps[2][:, 0:G])
                w_out.up(dve.tensor_copy(ta_t[:, :, :], K.ps[3][:, 0:2 * P].rearrange("p (i t) -> p i t", i=2)))
                dve.wait_ge(u_up.sem, u_up.base + c + 1)
                for e in range(2):
                    ins = dve.tensor_copy(u[:, :].rearrange("p (i e d) -> p e i d", i=2, e=2)[:, e],
                                          K.ps[4 + e][:, 0:2 * HD].rearrange("p (i d) -> p i d", i=2))
                u_out.up(ins)
                dve.wait_ge(y_up.sem, y_up.base + c + 1)
                for i in range(2):
                    ins = dve.tensor_scalar(state[:, i], state[:, i], decay_end[:, i, c:c + 1], None, ALU.mult)
                link(dve, K.dve_step, ins)
                for i in range(2):
                    ins = dve.scalar_tensor_tensor(state[:, i], K.ps[6][:, i * HD:i * HD + HD],
                                                   decay_end[:, i, c:c + 1], state[:, i], ALU.mult, ALU.add)
                s_out.up(ins)
                for e in range(2):
                    ins = dve.tensor_copy(y[:, c, :].rearrange("p (i e d) -> p e i d", i=2, e=2)[:, e],
                                          K.ps[2 + e][:, 2 * P:2 * P + 2 * HD].rearrange("p (i d) -> p i d", i=2))
                y_out.up(ins)

        @K.block.scalar
        def _(act):
            for n in range(NT * (LEVELS - 1)):
                act.wait_ge(m_up.sem, m_up.base + n + 1)
                if n:
                    act.wait_ge(t_up.sem, t_up.base + n)
                m_out.up(act.copy(m_mat[:, :, :, :].rearrange("p e i t -> p (e i t)"), K.ps[6][:, :]))
        meet(K)

        stats = arena(K, ctx, "gn_stats", [P, NT * H])
        stats2 = arena(K, ctx, "gn_stats2", [P, NT * H])
        sq = x_mat[:, :, :, :, :].rearrange("p b e i t -> p (b e i t)").rearrange("p (c f) -> p c f", c=NT)
        yh = y[:, :, :].rearrange("p c (h d) -> p (c h) d", d=HD)
        sqh = sq[:, :, :].rearrange("p c (h d) -> p (c h) d", d=HD)
        per_head = lambda ap: ap.unsqueeze(2).to_broadcast([P, NT * H, HD])
        per_tile = lambda ap: ap.unsqueeze(1).to_broadcast([P, NT, G])
        centred, squared, inv = sig["prepared"], sig["soft"], sig["exped"]

        @K.block.vector
        def _(dve):
            link(dve, K.dve_step, dve.tensor_reduce(stats[:, :], yh, AX, ALU.add))
            link(dve, K.dve_step, dve.tensor_scalar(stats[:, :], stats[:, :], 1.0 / HD, None, ALU.mult))
            centred.up(dve.tensor_tensor(yh, yh, per_head(stats[:, :]), ALU.subtract))
            dve.wait_ge(squared.sem, squared.base + 1)
            centred.up(dve.tensor_reduce(stats2[:, :], sqh, AX, ALU.add))
            dve.wait_ge(inv.sem, inv.base + 1)
            link(dve, K.dve_step, dve.tensor_tensor(yh, yh, per_head(stats2[:, :]), ALU.mult))
            link(dve, K.dve_step, dve.tensor_tensor(y[:, :, :], y[:, :, :], per_tile(row(K, "ln_g")), ALU.mult))
            dve.tensor_tensor(sqh, v_tok[:, :, :].rearrange("p c (h d) -> p (c h) d", d=HD),
                              per_head(bonus[:, :, :].rearrange("p c h -> p (c h)")), ALU.mult)
            link(dve, K.dve_step, dve.tensor_tensor(y[:, :, :], y[:, :, :], per_tile(row(K, "ln_b")), ALU.add))
            dve.tensor_tensor(y[:, :, :], y[:, :, :], sq[:, :, :], ALU.add)

        @K.block.scalar
        def _(act):
            act.wait_ge(centred.sem, centred.base + 1)
            squared.up(act.activation(sqh, yh, ACT.Square))
            act.wait_ge(centred.sem, centred.base + 2)
            link(act, K.act_step, act.activation(stats2[:, :], stats2[:, :], ACT.Ln, bias=K.gn_eps[:, 0:1],
                                                 scale=1.0 / HD))
            inv.up(act.activation(stats2[:, :], stats2[:, :], ACT.Exp, scale=-0.5))
        meet(K)



def modulation(K, layer):
    count = 6 * KD
    used, free = K.unit_used, K.signals["main_free"]
    first, base = K.unit, K.unit_used.n
    bank = lambda j: K.ps[j][:, 0:2]
    a_b = PRM["b_ada"][0] + layer * count

    def unit(pe, j, i):
        q = first + j
        pe.wait_ge(K.slot_full[q % RING].sem, i * 16 + 16 * (q // RING + 1))
        pe.wait_ge(free.sem, i * RING + (j + free.base + 1))
        for k in range(KD):
            mm = pe.matmul(bank(j), K.ring[:, q % RING, k * P:k * P + P], K.cond[:, k, :],
                           start=(k == 0), stop=(k == KD - 1))
        mm.then_inc(used.sem, 1)

    @K.block.tensor
    def _(pe):
        with pe.Fori(0, count // RING) as i:
            for j in range(RING):
                unit(pe, j, i)

    @K.block.vector
    def _(dve):
        dve.sem_inc(free.sem, RING)
        with dve.Fori(0, count // RING) as i:
            for j in range(RING):
                dve.wait_ge(used.sem, i * RING + (j + base + 1))
                dve.tensor_scalar(K.mods[:, layer, ds(i * RING + j, 1), :].rearrange("p a b -> p (a b)"), bank(j),
                                  K.prm[:, ds(i * RING + (a_b + j), 1)], None, ALU.add).then_inc(free.sem, 1)
    free.n += RING + count
    used.n += count
    K.unit += count
    meet(K)

    @K.block.vector
    def _(dve):
        for n, (name, at) in enumerate((("g_mix", KD), ("g_ffn", 4 * KD))):
            for s in range(2):
                dve.scalar_tensor_tensor(K.gains[:, layer, n, s, :], K.mods[:, layer, at:at + KD, s], 1.0,
                                         prm(K, name, layer * KD, KD), ALU.add, ALU.mult)
    meet(K)


def modulated_norm(K, layer, which, with_ctx):
    def part(s, c0, w):
        shift = 3 * KD * which
        return (c0, w, lambda k: K.gains[:, layer, which, s, k:k + 1],
                lambda k: K.mods[:, layer, shift + k, s:s + 1])
    rms_phase(K, K.xT, K.hT, [part(0, 0, S)] + ([part(1, S, C)] if with_ctx else []))



def query_key_norms(K, layer, p, with_ctx_q, rope):
    jobs = []
    for u, name, block, width in ((DK, "dkn", "block32", 32), (NK, "nkn", "block64", 64),
                                  (DQ, "dqn", "block32", 32), (NQ, "nqn", "block64", 64)):
        for i in range(2):
            jobs.append((u + i, name, block, width, 0, S))
            if with_ctx_q or u in (DK, NK):
                jobs.append((u + i, name, block, width, S, C))
    squared, summed, inv, done = (K.signals[n] for n in ("square", "stat", "rstd", "normed"))
    with ExitStack() as ctx:
        sq = arena(K, ctx, "qk_squares", [P, 2, S])
        rs = arena(K, ctx, "qk_rstd", [P, 2, S])
        turned = arena(K, ctx, "qk_turned", [P, 4, S])

        @K.block.scalar
        def _(act):
            def square(n):
                u, _, _, _, c0, w = jobs[n]
                if n >= 2:
                    act.wait_ge(summed.sem, summed.base + n - 1)
                squared.up(act.activation(sq[:, n % 2, 0:w], p[:, u, c0:c0 + w], ACT.Square))

            def root(n):
                u, _, _, width, c0, w = jobs[n]
                act.wait_ge(summed.sem, summed.base + n + 1)
                if n >= 2:
                    act.wait_ge(done.sem, done.base + n - 1)
                link(act, K.act_step, act.activation(rs[:, n % 2, 0:w], K.ps[n % 2][:, 0:w], ACT.Ln,
                                                     bias=K.eps[:, 0:1], scale=1.0 / width))
                inv.up(act.activation(rs[:, n % 2, 0:w], rs[:, n % 2, 0:w], ACT.Exp, scale=-0.5))

            for n in range(len(jobs) + 1):
                if n < len(jobs):
                    square(n)
                if n >= 1:
                    root(n - 1)

        @K.block.tensor
        def _(pe):
            for n, (u, _, block, _, c0, w) in enumerate(jobs):
                pe.wait_ge(squared.sem, squared.base + n + 1)
                if n >= 2:
                    pe.wait_ge(inv.sem, inv.base + n - 1)
                summed.up(pe.matmul(K.ps[n % 2][:, 0:w], const(K, block), sq[:, n % 2, 0:w],
                                    start=True, stop=True))

        @K.block.vector
        def _(dve):
            for n, (u, name, _, _, c0, w) in enumerate(jobs):
                dve.wait_ge(inv.sem, inv.base + n + 1)
                done.up(dve.scalar_tensor_tensor(p[:, u, c0:c0 + w], p[:, u, c0:c0 + w], prm(K, name, layer),
                                                 rs[:, n % 2, 0:w], ALU.mult, ALU.mult))
        meet(K)

        @K.block.tensor
        def _(pe):
            for n, u in enumerate((DK, DK + 1, DQ, DQ + 1)):
                summed.up(pe.matmul(K.ps[n][:, :], const(K, "rope_swap"), p[:, u, 0:S], start=True, stop=True))

        @K.block.vector
        def _(dve):
            for n, u in enumerate((DK, DK + 1, DQ, DQ + 1)):
                dve.wait_ge(summed.sem, summed.base + n + 1)
                dve.tensor_tensor(p[:, u, 0:S], p[:, u, 0:S], rope[:, 0], ALU.mult)
                link(dve, K.dve_step, dve.tensor_tensor(turned[:, n], K.ps[n][:, :], rope[:, 1], ALU.mult))
                dve.tensor_tensor(p[:, u, 0:S], p[:, u, 0:S], turned[:, n], ALU.add)
        meet(K)



def fourier(K, p, dft, parts):
    first_up, first_out, second_up, put = (K.signals[n] for n in ("scored", "exped", "mixed", "put"))
    jobs = [(i, c0, w) for c0, w in parts for i in range(2)]
    with ExitStack() as ctx:
        z = arena(K, ctx, "fourier_z", [P, 2, NT, 2 * P])

        @K.block.tensor
        def _(pe):
            def features(n):
                i, c0, w = jobs[n]
                for t in range(w // P):
                    if n:
                        pe.wait_ge(first_out.sem, first_out.base + 2 * n)
                    at = t * 2 * P if w == S else t * S
                    mm = pe.matmul(K.psum[:, at:at + 2 * P], p[:, FO + i, c0 + t * P:c0 + t * P + P],
                                   const(K, "dft64"), start=True, stop=True)
                first_up.up(mm)

            def tokens(n):
                i, c0, w = jobs[n]
                pe.wait_ge(first_out.sem, first_out.base + 2 * (n + 1))
                if n >= 2:
                    pe.wait_ge(put.sem, put.base + n - 1)
                for t in range(w // P):
                    for q in range(2):
                        mm = pe.matmul(K.ps[2 + n % 2][:, 0:w], z[:, n % 2, t, q * P:q * P + P],
                                       dft[:, q, t, 0:S:S // w], start=(t == 0 and q == 0),
                                       stop=(t == w // P - 1 and q == 1))
                second_up.up(mm)

            for n in range(len(jobs) + 1):
                if n < len(jobs):
                    features(n)
                if n:
                    tokens(n - 1)

        half = lambda buf, n, q, w: buf[:, n % 2, q * w // P // 2:(q + 1) * w // P // 2, :]
        src = lambda q, w: K.psum[:, q * S:q * S + w].rearrange("p (t f) -> p t f", f=2 * P) if w == S \
            else K.psum[:, q * S:q * S + 2 * P].unsqueeze(1)

        def first(eng, q, op):
            for n, (i, c0, w) in enumerate(jobs):
                eng.wait_ge(first_up.sem, first_up.base + n + 1)
                if n >= 2:
                    eng.wait_ge(second_up.sem, second_up.base + n - 1)
                first_out.up(op(half(z, n, q, w), src(q, w)))
                if q and n:
                    last(eng, n - 1)
            if q:
                last(eng, len(jobs) - 1)

        def last(act, n):
            i, c0, w = jobs[n]
            act.wait_ge(second_up.sem, second_up.base + n + 1)
            put.up(act.activation(K.yT[:, i, c0:c0 + w], K.ps[2 + n % 2][:, 0:w], ACT.Identity,
                                  scale=float((w * HD) ** -0.5)))

        @K.block.vector
        def _(dve):
            first(dve, 0, dve.tensor_copy)

        @K.block.scalar
        def _(act):
            first(act, 1, act.copy)
        meet(K)


def differential_attention(K, layer, p, v, y, tiles, key_tiles, key0):
    with ExitStack() as ctx:
        neg_lam = arena(K, ctx, "neg_lam", [P, 4])
        prod = arena(K, ctx, "lam_products", [P, 2, 32])
        summed, exped = K.signals["prepared"], K.signals["soft"]
        l4 = row(K, "lam4", layer * 128, 128).rearrange("p (a d) -> p a d", a=4)

        @K.block.vector
        def _(dve):
            link(dve, K.dve_step, dve.tensor_tensor(prod[:, :, :], l4[:, 0:4:2], l4[:, 1:4:2], ALU.mult))
            summed.up(dve.tensor_reduce(neg_lam[:, 0:2], prod[:, :, :], AX, ALU.add))
            dve.wait_ge(exped.sem, exped.base + 1)
            link(dve, K.dve_step, dve.tensor_tensor(neg_lam[:, 2:3], neg_lam[:, 1:2], neg_lam[:, 0:1], ALU.subtract))
            dve.tensor_scalar(neg_lam[:, 3:4], neg_lam[:, 2:3], -lambda_init(layer), None, ALU.add)

        @K.block.scalar
        def _(act):
            act.wait_ge(summed.sem, summed.base + 1)
            exped.up(act.activation(neg_lam[:, 0:2], neg_lam[:, 0:2], ACT.Exp))
        meet(K)

        kw = len(key_tiles) * P
        items = []
        for h in range(H):
            for m in tiles:
                scores = []
                for c in range(2):
                    first_row = 64 * (h % 2) + 32 * c
                    r, i = slice(first_row, first_row + 32), h // 2
                    q = p[r, DQ + i, m * P:m * P + P]
                    scores.append([[(q, p[r, DK + i, key0 + a:key0 + min(a + S, kw)], a, min(S, kw - a))]
                                   for a in range(0, kw, S)])
                items.append(dict(scores=scores, kw=kw, tiles=key_tiles, bias=None,
                                  v=lambda t, h=h: v[:, t, h * HD:h * HD + HD],
                                  out=y[:, m, h * HD:h * HD + HD]))
        softmax_attention(K, items, 1.0, neg_lam[:, 3:4])


def neighbourhood_attention(K, layer, p, v, y, tiles, key_tiles, key0, bias):
    kw = len(key_tiles) * P
    items = []
    for h in range(H):
        r, i = slice(64 * (h % 2), 64 * (h % 2) + HD), h // 2
        for m in tiles:
            q = p[r, NQ + i, m * P:m * P + P]
            first = 7 - 2 * m
            b = None if bias is None else bias[:, h, first:first + 8, :].rearrange("p a k -> p (a k)")
            items.append(dict(
                scores=[[[(q, p[r, NK + i, key0 + a:key0 + min(a + S, kw)], a, min(S, kw - a))]
                         for a in range(0, kw, S)]],
                kw=kw, tiles=key_tiles, bias=b, v=lambda t, h=h: v[:, t, G + h * HD:G + h * HD + HD],
                out=y[:, m, h * HD:h * HD + HD]))
    softmax_attention(K, items, 1.0)


def head_norm(K, src, gain, tiles, factor=1.0):
    n = len(tiles)
    m = slice(tiles[0], tiles[-1] + 1)
    squared, summed, inv = (K.signals[x] for x in ("square", "stat", "rstd"))
    with ExitStack() as ctx:
        sq = arena(K, ctx, "head_squares", [P, n, G])
        st = arena(K, ctx, "head_stats", [P, n, H])
        heads = lambda ap: ap.rearrange("p m (h d) -> p m h d", d=HD)

        @K.block.scalar
        def _(act):
            squared.up(act.activation(sq[:, :, :], src[:, m, :], ACT.Square))
            act.wait_ge(summed.sem, summed.base + 1)
            link(act, K.act_step, act.activation(st[:, :, :], st[:, :, :], ACT.Ln, bias=K.eps[:, 0:1],
                                                 scale=1.0 / HD))
            inv.up(act.activation(st[:, :, :], st[:, :, :], ACT.Exp, scale=-0.5))

        @K.block.vector
        def _(dve):
            dve.wait_ge(squared.sem, squared.base + 1)
            summed.up(dve.tensor_reduce(st[:, :, :], heads(sq[:, :, :]), AX, ALU.add))
            dve.wait_ge(inv.sem, inv.base + 1)
            for t in range(n):
                ins = dve.tensor_tensor(
                    src[:, tiles[0] + t, :].rearrange("p (h d) -> p h d", d=HD),
                    src[:, tiles[0] + t, :].rearrange("p (h d) -> p h d", d=HD),
                    st[:, t, :].unsqueeze(2).to_broadcast([P, H, HD]), ALU.mult)
            link(dve, K.dve_step, ins)
            for t in range(n):
                dve.scalar_tensor_tensor(src[:, tiles[0] + t, :], src[:, tiles[0] + t, :], factor, gain,
                                         ALU.mult, ALU.mult)
        meet(K)


def chunk_gmlp(K, layer, uv, y, tiles, ws):
    mixed, put = K.signals["mixed"], K.signals["put"]

    @K.block.tensor
    def _(pe):
        for n, m in enumerate(tiles):
            for h in range(H):
                mm = pe.matmul(K.ps[n][:, h * HD:h * HD + HD], ws[:, h], uv[:, m, G + h * HD:G + h * HD + HD],
                               start=True, stop=True)
            mixed.up(mm)

    @K.block.vector
    def _(dve):
        for n, m in enumerate(tiles):
            dve.wait_ge(mixed.sem, mixed.base + n + 1)
            for h in range(H):
                c = slice(h * HD, h * HD + HD)
                ins = dve.scalar_tensor_tensor(y[:, m, c], K.ps[n][:, c], prm(K, "gmlp_b", layer * H + h),
                                               uv[:, m, c], ALU.add, ALU.mult)
    meet(K)



def feed_forward(K, layer, with_ctx):
    W = S + C if with_ctx else S
    used, conv, gate_done = K.unit_used, K.signals["conv"], K.signals["silu"]
    emptied, pair_done = K.signals["main_free"], K.signals["pair_done"]
    ZW = S + C + 4
    spans = [(0, S, 1)] + ([(S, C, S + 3)] if with_ctx else [])
    first, base = K.unit, used.n
    wc = PRM["conv_w2"][0] + layer * 3 * 44
    bc = PRM["conv_b2"][0] + layer * 44
    with ExitStack() as ctx:
        hid = arena(K, ctx, "hidden", [P, KF, S + C])
        z = arena(K, ctx, "z", [P, 4, ZW])
        t = arena(K, ctx, "conv_out", [P, 4, S + C])

        @K.block.gpsimd
        def _(pool):
            pool.memset(z[:, :, :], 0.0)
        meet(K)

        @K.block.tensor
        def _(pe):
            with pe.Fori(0, 11) as i:
                for j in range(RING):
                    q = first + j
                    pe.wait_ge(K.slot_full[q % RING].sem, i * 16 + 16 * (q // RING + 1))
                    pe.wait_ge(emptied.sem, i * RING + (j + emptied.base + 1))
                    for k in range(KD):
                        w = K.ring[:, q % RING, k * P:k * P + P]
                        mm = pe.matmul(K.ps[j][:, :], w, K.hT[:, k, 0:S], start=(k == 0), stop=(k == KD - 1))
                        if with_ctx:
                            mm = pe.matmul(K.ps[4 + j][:, 0:C], w, K.hT[:, k, S:S + C],
                                           start=(k == 0), stop=(k == KD - 1))
                    mm.then_inc(used.sem, 1)

        @K.block.scalar
        def _(act):
            act.sem_inc(emptied.sem, RING)
            with act.Fori(0, 11) as i:
                for j in range(RING):
                    act.wait_ge(used.sem, i * RING + (j + base + 1))
                    act.wait_ge(conv.sem, i * RING + (j + conv.base + 1))
                    for n, (c0, w, z0) in enumerate(spans):
                        ins = act.copy(z[:, j, z0:z0 + w], K.ps[4 * n + j][:, 0:w])
                    ins.then_inc(emptied.sem, 1)
                    if j % 2:
                        act.wait_ge(conv.sem, i * RING + (j + conv.base + RING))
                        act.activation(t[:, j - 1, 0:W], t[:, j - 1, 0:W], ACT.Silu).then_inc(gate_done.sem, 1)

        @K.block.vector
        def _(dve):
            dve.sem_inc(conv.sem, RING)
            with dve.Fori(0, 11) as i:
                for j in range(RING):
                    tile = (j % 2) * KF + j // 2
                    col = lambda c: K.prm[:, ds(i * 2 + (c + tile), 1)]
                    dve.wait_ge(emptied.sem, i * RING + (j + emptied.base + RING + 1))
                    for s, (c0, w, z0) in enumerate(spans):
                        ins = dve.tensor_scalar(t[:, j, c0:c0 + w], z[:, j, z0 - 1:z0 - 1 + w], col(wc), col(bc),
                                                ALU.mult, ALU.add)
                    ins.then_inc(K.conv_step.sem, 1)
                    dve.wait_ge(K.conv_step.sem, i * (2 * RING) + (2 * j + K.conv_step.base + 1))
                    for s, (c0, w, z0) in enumerate(spans):
                        ins = dve.scalar_tensor_tensor(t[:, j, c0:c0 + w], z[:, j, z0:z0 + w], col(wc + 44),
                                                       t[:, j, c0:c0 + w], ALU.mult, ALU.add)
                    ins.then_inc(K.conv_step.sem, 1)
                    dve.wait_ge(K.conv_step.sem, i * (2 * RING) + (2 * j + K.conv_step.base + 2))
                    for s, (c0, w, z0) in enumerate(spans):
                        ins = dve.scalar_tensor_tensor(t[:, j, c0:c0 + w], z[:, j, z0 + 1:z0 + 1 + w],
                                                       col(wc + 88), t[:, j, c0:c0 + w], ALU.mult, ALU.add)
                    ins.then_inc(conv.sem, 1)
                    if j % 2:
                        dve.wait_ge(conv.sem, i * RING + (j + conv.base + RING + 1))
                        dve.wait_ge(gate_done.sem, i * 2 + (j // 2 + gate_done.base + 1))
                        dve.tensor_tensor(hid[:, ds(i * 2 + j // 2, 1), 0:W].rearrange("p a w -> p (a w)"),
                                          t[:, j - 1, 0:W], t[:, j, 0:W], ALU.mult)

        K.conv_step.n += 11 * 2 * RING
        conv.n += RING + 44
        gate_done.n += 22
        emptied.n += RING + 44
        used.n += 44
        K.unit += 44
        meet(K)

        up, out = K.signals["mixed"], K.signals["put"]

        @K.block.tensor
        def _(pe):
            def step(i, j, n, a, b):
                q = unit0 + j
                pe.wait_ge(K.slot_full[q % RING].sem, i * 16 + 16 * (q // RING + 1))
                for kk in range(2):
                    start, stop = a and kk == 0, b and kk == 1
                    for o in range(4):
                        w = K.ring[:, q % RING, (kk * 4 + o) * P:(kk * 4 + o) * P + P]
                        k = n * 2 + kk
                        mv = hid[:, ds(k, 1), :].rearrange("p a w -> p (a w)") if not isinstance(k, int) \
                            else hid[:, k, :]
                        mm = pe.matmul(K.ps[o][:, :], w, mv[:, 0:S], start=start, stop=stop,
                                       skip_group_check=True)
                        if with_ctx:
                            mm = pe.matmul(K.ps[4 + o][:, 0:C], w, mv[:, S:S + C], start=start, stop=stop,
                                           skip_group_check=True)
                mm.then_inc(used.sem, 1)
                return mm

            for half in range(2):
                unit0 = K.unit + 11 * half
                if half:
                    pe.wait_ge(out.sem, out.base + 1)
                    if with_ctx:
                        pe.wait_ge(K.signals["ctx_put"].sem, K.signals["ctx_put"].base + 1)
                step(0, 0, 0, True, False)
                unit0 += 1
                with pe.Fori(0, 2) as i:
                    for j in range(RING):
                        step(i, j, i * RING + (j + 1), False, False)
                unit0 += 8
                step(0, 0, 9, False, False)
                unit0 += 1
                step(0, 0, 10, False, True)
        used.n += 22
        K.unit += 22

        @K.block.vector
        def _(dve):
            for half in range(2):
                dve.wait_ge(used.sem, base + 44 + 11 * (half + 1))
                for o in range(4):
                    n = 4 * half + o
                    ins = dve.scalar_tensor_tensor(K.xT[:, n, 0:S], K.ps[o][:, :], K.mods[:, layer, 5 * KD + n, 0:1],
                                                   K.xT[:, n, 0:S], ALU.mult, ALU.add)
                out.up(ins)
                if with_ctx:
                    for o in range(4):
                        n = 4 * half + o
                        ins = dve.scalar_tensor_tensor(K.xT[:, n, S:S + C], K.ps[4 + o][:, 0:C],
                                                       K.mods[:, layer, 5 * KD + n, 1:2], K.xT[:, n, S:S + C],
                                                       ALU.mult, ALU.add)
                    K.signals["ctx_put"].up(ins)
        meet(K)



SIGNALS = ("met", "act_step", "dve_step", "conv_step", "unit_used", "loaded_late", "square", "stat", "rstd",
           "normed", "main_free", "ctx_free", "scored", "max_ready", "exped", "weighted", "turned_up",
           "turned_out", "mixed", "put", "ctx_put", "prepared", "soft", "summed", "produced", "taken", "x_ready",
           "x_used", "m_up", "m_out", "t_up", "t_out", "w_up", "w_out", "u_up", "u_out", "y_up", "y_out",
           "s_out", "conv", "silu", "pair_done", "loaded", "stored")

N_UNITS = N1F + N1T + KD + 2 * 6 * KD + 2 * (N2F + 8 + KD + 44 + 22)


def build(nc, dram):
    with ExitStack() as ctx:
        K = Kit()
        K.nc, K.serial, K.unit = nc, 0, 0
        K.signals = {n: Signal(nc, ctx, n) for n in SIGNALS}
        K.met, K.unit_used, K.loaded_late = (K.signals[n] for n in ("met", "unit_used", "loaded_late"))
        K.act_step, K.dve_step, K.conv_step = (K.signals[n] for n in ("act_step", "dve_step", "conv_step"))
        K.slot_full = [Signal(nc, ctx, f"slot_full{j}") for j in range(RING)]
        K.w_units, K.lru_w_dram, K.lora_dram = dram["w_units"], dram["lru_w"], dram["lora"]
        sb = lambda name, shape: ctx.enter_context(nc.sbuf_tensor(name, shape, F32))
        K.psum = ctx.enter_context(nc.psum_tensor("psum", [P, 8 * S], F32))
        K.ps = [K.psum[:, j * S:(j + 1) * S] for j in range(8)]
        K.ring = sb("ring", [P, RING, KD * P])
        K.xT = sb("xT", [P, KD, S + C])
        K.hT = sb("hT", [P, KD, S + C])
        K.yT = K.hT
        K.cst = sb("constants", [P, NCONST])
        K.prm = sb("parameters", [P, NPRM])
        K.rows = sb("row_parameters", [P, NROW])
        K.mods = sb("mods", [P, 2, 6 * KD, 2])
        K.gains = sb("gains", [P, 2, 2, 2, KD])
        K.cond = sb("cond", [P, KD, 2])
        scal = sb("scalars", [P, 8])
        K.eps, K.gn_eps, K.one, K.half, K.minus_half = (scal[:, j:j + 1] for j in range(5))
        K.block = ctx.enter_context(nc.Block())
        loaded = K.signals["loaded"]

        @K.block.scalar
        def _(act):
            for dst, src in ((K.xT[:, :, 0:S], dram["x"]), (K.cst[:, :], dram["constants"]),
                             (K.prm[:, :], dram["parameters"]), (K.rows[:, :], dram["row_parameters"]),
                             (K.xT[:, :, S:S + C], dram["ctx"])):
                loaded.up(act.dma_start(dst, src), 16)
            act.wait_ge(loaded.sem, loaded.n)

        @K.block.gpsimd
        def _(pool):
            for at, value in ((K.eps, EPS), (K.gn_eps, GN_EPS), (K.one, 1.0), (K.half, HALF),
                              (K.minus_half, -HALF)):
                pool.memset(at, value)
        stream_weights(K, N_UNITS)
        meet(K)

        first_block(K, ctx)
        second_block(K, dram)

        @K.block.sync
        def _(sp):
            sp.wait_ge(K.met.sem, K.met.n)
            sp.dma_start(dram["out"], K.xT[:, :, 0:S]).then_inc(K.signals["stored"].sem, 16)
            sp.wait_ge(K.signals["stored"].sem, 16)


def first_block(K, outer):
    rms_phase(K, K.xT, K.hT, [(0, S, lambda k: prm(K, "norm_g", k), None)])
    with ExitStack() as ctx:
        p = arena(K, ctx, "p", [P, N1F, PAD + S])
        v = arena(K, ctx, "v", [P, NT, 2 * G])
        y = arena(K, ctx, "y", [P, NT, G])

        @K.block.gpsimd
        def _(pool):
            pool.memset(p[:, :, 0:PAD], 0.0)
        project(K, N1F, False, False,
                lambda dve, u, bank: dve.tensor_copy(at_unit(p, u, PAD, PAD + S), bank[:, :]), None)
        project(K, N1T, True, False,
                lambda dve, u, bank: dve.tensor_copy(v[:, :, u * P:u * P + P],
                                                     bank.rearrange("p (m f) -> p m f", f=P)), None)

        @K.block.scalar
        def _(act):
            for u in range(GATE, GATE + 8):
                act.activation(p[:, u, PAD:], p[:, u, PAD:], ACT.Silu)
        meet(K)

        def gated(group):
            return lambda dve, u, psum: dve.tensor_tensor(K.yT[:, 2 * group + u, 0:S], psum,
                                                          p[:, GATE + 2 * group + u, PAD:], ALU.mult)
        tiles = range(NT)
        forgetting_attention(K, p, v[:, :, 0:G], y)
        to_feature_major(K, y, tiles, gated(0))
        stick_breaking_attention(K, p, v[:, :, G:2 * G], y)
        to_feature_major(K, y, tiles, gated(1))
        rg_lru(K, p, lambda dve, i, h: dve.tensor_tensor(K.yT[:, 6 + i, 0:S], h, p[:, GATE + 6 + i, PAD:],
                                                         ALU.mult))
        rwkv(K, p, y)
        to_feature_major(K, y, tiles, gated(2))

    def add_to_x(dve, u, bank):
        x = at_unit(K.xT, u, 0, S)
        return dve.tensor_tensor(x, x, bank[:, :], ALU.add)
    project(K, KD, False, False, add_to_x, None, K.yT)
    rms_phase(K, K.xT, K.xT, [(0, S, lambda k: prm(K, "final_g", k), None)])


def at_unit(buf, u, a, b):
    if isinstance(u, int):
        return buf[:, u, a:b]
    return buf[:, ds(u, 1), a:b].rearrange("p a w -> p (a w)")


def second_block(K, dram):
    @K.block.scalar
    def _(act):
        act.activation(K.cond[:, :, :], prm(K, "c", 0, 2 * KD).rearrange("p (s k) -> p k s", s=2), ACT.Silu)
    @K.block.vector
    def _(dve):
        dve.tensor_scalar(prm(K, "dqn", 0, 2), prm(K, "dqn", 0, 2), 32 ** -0.5, None, ALU.mult)
        dve.tensor_scalar(prm(K, "nqn", 0, 2), prm(K, "nqn", 0, 2), HD ** -0.5, None, ALU.mult)
    meet(K)
    for layer in range(2):
        modulation(K, layer)
    for layer in range(2):
        ctx_out = layer == 0
        mixers(K, layer, ctx_out, dram)

        def lat(dve, u, bank):
            x = at_unit(K.xT, u, 0, S)
            m = K.mods[:, layer, ds(u + 2 * KD, 1), 0:1].rearrange("p a b -> p (a b)")
            return dve.scalar_tensor_tensor(x, bank[:, :], m, x, ALU.mult, ALU.add)

        def cnt(act, u, bank):
            m = K.mods[:, layer, ds(u + 2 * KD, 1), 1:2].rearrange("p a b -> p (a b)")
            return act.activation(at_unit(K.yT_next, u, S, S + C), bank[:, 0:C], ACT.Identity, scale=m)
        with ExitStack() as ctx:
            if ctx_out:
                K.yT_next = arena(K, ctx, "ctx_gain", [P, KD, S + C])
            project(K, KD, False, ctx_out, lat, cnt, K.yT)
            if ctx_out:
                @K.block.vector
                def _(dve):
                    dve.tensor_tensor(K.xT[:, :, S:S + C], K.xT[:, :, S:S + C], K.yT_next[:, :, S:S + C], ALU.add)
                meet(K)
        modulated_norm(K, layer, 1, ctx_out)
        feed_forward(K, layer, ctx_out)


def mixers(K, layer, ctx_out, dram):
    late = K.loaded_late
    lat_tiles, ctx_tiles, all_tiles = range(NT), range(NT, MT), range(MT)
    modulated_norm(K, layer, 0, True)
    with ExitStack() as ctx:
        p = arena(K, ctx, "p", [P, N2F, S + C])
        v = arena(K, ctx, "v", [P, MT, 4 * P])
        uv = arena(K, ctx, "uv", [P, MT, 4 * P])
        y = arena(K, ctx, "y", [P, MT, G])

        def feature(first):
            return (lambda dve, u, bank: dve.tensor_copy(at_unit(p, u + first, 0, S), bank[:, :]),
                    lambda act, u, bank: act.copy(at_unit(p, u + first, S, S + C), bank[:, 0:C]))

        def token(buf):
            def dst(u, a, b):
                if isinstance(u, int):
                    return buf[:, a:b, u * P:u * P + P]
                return buf[:, a:b, ds(u * P, P)]
            split = lambda bank, n: bank[:, 0:n * P].rearrange("p (m f) -> p m f", f=P)
            return (lambda dve, u, bank: dve.tensor_copy(dst(u, 0, NT), split(bank, NT)),
                    lambda act, u, bank: act.copy(dst(u, NT, MT), split(bank, CT)))
        project(K, 4, False, True, *feature(0))
        project(K, 6, False, ctx_out, *feature(4))
        project(K, 4, True, True, *token(v))
        project(K, 4, True, ctx_out, *token(uv))

        tiles = all_tiles if ctx_out else lat_tiles
        with ExitStack() as inner:
            dft = arena(K, inner, "dft", [P, 2, NT, S])

            @K.block.gpsimd
            def _(pool):
                late.up(pool.dma_start(dft[:, :, :, :], dram["dft"]), 16)
                pool.wait_ge(late.sem, late.n)

            @K.block.scalar
            def _(act):
                act.activation(uv[:, 0:len(tiles), :], uv[:, 0:len(tiles), :], ACT.Gelu_apprx_tanh)
            meet(K)
            fourier(K, p, dft, [(0, S)] + ([(S, C)] if ctx_out else []))

        def put_unit(first, c0):
            return lambda dve, u, psum: dve.tensor_copy(K.yT[:, first + u, c0:c0 + psum.shape[1]], psum)

        def turn_all(first):
            to_feature_major(K, y, lat_tiles, put_unit(first, 0))
            if ctx_out:
                to_feature_major(K, y, ctx_tiles, put_unit(first, S))

        with ExitStack() as inner:
            ws = arena(K, inner, "gmlp_ws", [P, H, P])

            @K.block.gpsimd
            def _(pool):
                late.up(pool.dma_start(ws[:, :, :], dram["gmlp_ws"][:, layer]), 16)
                pool.wait_ge(late.sem, late.n)
            head_norm(K, uv[:, :, G:2 * G], row(K, "gmlp_g", layer * G), tiles)
            chunk_gmlp(K, layer, uv, y, tiles, ws)
            turn_all(6)
        with ExitStack() as inner:
            rope = arena(K, inner, "rope", [P, 2, S])

            @K.block.gpsimd
            def _(pool):
                late.up(pool.dma_start(rope[:, :, :], dram["rope"]), 16)
                pool.wait_ge(late.sem, late.n)
            meet(K)
            query_key_norms(K, layer, p, ctx_out, rope)
        differential_attention(K, layer, p, v, y, lat_tiles, all_tiles, 0)
        if ctx_out:
            differential_attention(K, layer, p, v, y, ctx_tiles, ctx_tiles, S)
        head_norm(K, y, row(K, "subln", layer * G), tiles, 1.0 - lambda_init(layer))
        turn_all(2)
        with ExitStack() as inner:
            bias = arena(K, inner, "bias", [P, H, 16, HD])

            @K.block.gpsimd
            def _(pool):
                late.up(pool.dma_start(bias[:, :, :, :], dram["na_bias"][:, layer]), 16)
                pool.wait_ge(late.sem, late.n)
                for h in range(H):
                    pool.tensor_tensor(bias[:, h], bias[:, h],
                                       const(K, "window").unsqueeze(1).to_broadcast([P, 16, HD]), ALU.add)
            meet(K)
            neighbourhood_attention(K, layer, p, v, y, lat_tiles, all_tiles, 0, bias)
        if ctx_out:
            neighbourhood_attention(K, layer, p, v, y, ctx_tiles, ctx_tiles, S, None)
        turn_all(4)



def constant_table():
    t = np.zeros((P, NCONST), np.float32)
    i, j = np.arange(P)[:, None], np.arange(P)[None, :]

    def put(name, value):
        a, b = CONST[name]
        t[:, a:b] = value
    put("ident", i == j)
    put("ones", 1.0)
    put("block32", i // 32 == j // 32)
    put("block64", i // 64 == j // 64)
    put("tri_ge", i >= j)
    put("causal_add", np.where(j > i, NEG, 0.0))
    put("stick_big", np.where(i >= j, -NEG, 0.0))
    put("strict_t", i < j)
    put("incl_t", i <= j)
    put("rope_swap", np.where(i // 32 == j // 32, np.where(i == j + 16, -1.0, np.where(i == j - 16, 1.0, 0.0)), 0.0))
    head_row = np.zeros((P, H, P))
    for h in range(H):
        head_row[64 + h, h] = HD ** 0.5
    put("head_row", head_row.reshape(P, -1))
    put("head_pair", i // 64 == np.arange(2)[None, :])
    level = np.zeros((P, LEVELS, P))
    for n in range(LEVELS):
        level[:, n] = (i // 2 ** n == j // 2 ** n + 1) & (i // 2 ** n % 2 == 1)
    put("level", level.reshape(P, -1))
    put("level0_t", level[:, 0].T)
    q, k = i % HD, np.arange(HD)[None, :]
    c0 = np.clip(q - 8, 0, HD - 16)
    put("window", np.where((k >= c0) & (k < c0 + 16), 0.0, NEG))
    put("chunk_keep", np.arange(S)[None, :] % CH != 0)
    put("keep_all", 1.0)
    d = np.arange(HD)
    angle = 2 * np.pi * np.outer(d, d) / HD
    two = lambda m: np.kron(np.eye(2), m)
    put("dft64", np.concatenate([two(np.cos(angle)), -two(np.sin(angle))], axis=1))
    return t


def dft_table():
    n = np.arange(S)
    angle = 2 * np.pi * (np.outer(n, n) % S) / S
    both = np.stack([np.cos(angle), np.sin(angle)])
    return np.ascontiguousarray(both.reshape(2, NT, P, S).transpose(2, 0, 1, 3)).astype(np.float32)


def rope_table():
    freqs = 10000.0 ** (-np.arange(8, dtype=np.float32) / 8)
    t = np.arange(S)
    angle = np.concatenate([(t // 64)[None, :] * freqs[:, None], (t % 64)[None, :] * freqs[:, None]])
    full = np.tile(angle, (8, 1))
    return np.stack([np.cos(full), np.sin(full)], axis=1).astype(np.float32)



def tile_units(w):
    n = w.shape[1] // P
    return w.reshape(KD, P, n, P).transpose(2, 1, 0, 3).reshape(n, P, KD * P)


def down_units(w):
    w = w.reshape(KF // 2, 2, P, 2, 4, P)
    return w.transpose(3, 0, 2, 1, 4, 5).reshape(KF, P, 8 * P)


def lay_out(a):
    cols = lambda w, at, n: w[:, at:at + n]
    g = G
    w1 = a["w_in"][0]
    at = {n: o for n, o in zip(("fq", "fk", "fv", "fg", "ff", "sq", "sk", "sv", "sg", "rw", "rg", "lx", "lg"),
                               np.cumsum([0, g, g, g, g, H, g, g, g, g, 3 * g + 2 * R, g, g]))}
    rw = at["rw"]
    first = [cols(w1, at[n], g) for n in ("fq", "fk", "sq", "sk")]
    first += [cols(w1, rw, 3 * g), cols(w1, rw + 3 * g, 2 * R), cols(w1, at["ff"], H),
              np.zeros((D, P - 2 * R - H), np.float32)]
    first += [cols(w1, at[n], g) for n in ("lx", "fg", "sg", "rg", "lg", "fv", "sv")]
    units = [tile_units(np.concatenate(first, axis=1)), tile_units(a["w_out"][0])]
    units += [tile_units(a["w_ada_2"][l]) for l in range(2)]
    for l in range(2):
        w = a["w_in_2"][l]
        order = [2, 5, 0, 1, 4, 3, 6, 7, 8]
        units.append(tile_units(np.concatenate([cols(w, n * g, g) for n in order], axis=1)))
        units.append(tile_units(a["w_out_2"][l]))
        up = a["ffn_up_2"][l].reshape(D, 2, KF, P).transpose(0, 2, 1, 3).reshape(D, 2 * FF)
        units += [tile_units(up), down_units(a["ffn_down_2"][l])]
    w_units = np.concatenate(units)

    prm_table = np.zeros((P, NPRM), np.float32)

    def put(name, values, col=0):
        f = PRM[name][0] + col
        v = np.asarray(values).reshape(-1, P)
        prm_table[:, f:f + len(v)] = v.T
    for name, src in (("norm_g", "norm_g"), ("w0", "rwkv_w0"), ("a0", "rwkv_a0"), ("k_k", "rwkv_k_k"),
                      ("k_a", "rwkv_k_a"), ("r_k", "rwkv_r_k"), ("conv_w", "lru_conv_w"), ("conv_b", "lru_conv_b"),
                      ("b_a", "lru_b_a"), ("b_x", "lru_b_x"), ("lam", "lru_lambda"), ("final_g", "final_g"),
                      ("g_mix", "g_mix_2"), ("g_ffn", "g_ffn_2"), ("b_ada", "b_ada_2"),
                      ("conv_w2", "ffn_conv_2"), ("conv_b2", "ffn_conv_b_2"), ("c", "c_2")):
        put(name, a[src])
    put("c", a["c_ctx_2"], KD)
    put("mu", np.concatenate([a["rwkv_mu"][0], np.zeros(64, np.float32)]))
    prm_table[64:64 + H, PRM["b_f"][0]] = a["b_forget"][0]
    for name, src, n in (("dqn", "diff_qn_2", 4), ("dkn", "diff_kn_2", 4), ("nqn", "na_qn_2", 2), ("nkn", "na_kn_2", 2)):
        put(name, np.tile(a[src], (1, n)))
    put("gmlp_b", a["gmlp_b_2"])

    row_table = np.concatenate([a["rwkv_ln_g"][0], a["rwkv_ln_b"][0], np.tile(a["diff_subln_2"], (1, H)).ravel(),
                                a["gmlp_norm_2"].ravel(), a["diff_lam_2"].ravel()])
    row_table = np.ascontiguousarray(np.broadcast_to(row_table, (P, NROW)))

    lru_w = np.zeros((P, 4, P), np.float32)
    for n, src in enumerate(("lru_w_a", "lru_w_x")):
        for i in range(2):
            for e in range(2):
                lru_w[64 * e:64 * e + HD, 2 * n + i, 64 * e:64 * e + HD] = a[src][0, 2 * i + e]
    lora = np.concatenate([a["rwkv_w2"][0], a["rwkv_a2"][0]])

    q, k = np.arange(HD)[:, None], np.arange(HD)[None, :]
    off = k - q + 15
    rpb = a["na_rpb_2"]
    spread = np.where((off >= 0) & (off <= 30), rpb[:, :, :, np.clip(off, 0, 30)], np.float32(0))
    bias = np.zeros((2, HD, 2, H, 16, HD), np.float32)
    for e in range(2):
        bias[e, :, :, :, e:e + 15] = spread.transpose(3, 0, 1, 2, 4)
    tokens = lambda x: np.ascontiguousarray(x.reshape(-1, KD, P).transpose(2, 1, 0))
    return {
        "x": tokens(a["x"][0]), "ctx": tokens(a["ctx_2"][0]), "w_units": w_units,
        "constants": constant_table(), "parameters": prm_table, "row_parameters": row_table,
        "lru_w": lru_w.reshape(P, -1), "lora": np.ascontiguousarray(lora), "dft": dft_table(), "rope": rope_table(),
        "gmlp_ws": np.ascontiguousarray(a["gmlp_ws_2"].transpose(3, 0, 1, 2)),
        "na_bias": bias.reshape(P, 2, H, 16, HD),
    }


def kernel(**inputs):
    import concourse.bacc as bacc
    from concourse.bass_utils import run_bass_kernel_spmd

    arrays = lay_out({k: np.asarray(v) for k, v in inputs.items()})
    nc = bacc.Bacc("TRN2", target_bir_lowering=False, num_devices=1)
    dram = {n: nc.dram_tensor(f"in_{n}", v.shape, F32, kind="ExternalInput").ap() for n, v in arrays.items()}
    dram["out"] = nc.dram_tensor("out_x", (P, KD, S), F32, kind="ExternalOutput").ap()
    build(nc, dram)
    r = run_bass_kernel_spmd(nc, [{f"in_{n}": v for n, v in arrays.items()}], core_ids=[0])
    out = r.results[0]["out_x"]
    return out.transpose(2, 1, 0).reshape(1, S, D)
```

```python
from contextlib import ExitStack

import numpy as np

import concourse.bass as bass
from concourse import mybir

F32 = mybir.dt.float32
F32R = mybir.dt.float32r
ALU = mybir.AluOpType
ACT = mybir.ActivationFunctionType
AX = mybir.AxisListType.X
ds = bass.ds

P = 128
D = 1024
KD = D // P
S = 512
C = 256
NT = S // P
CT = C // P
MT = NT + CT
G = 256
H = 4
HD = 64
R = 32
FF = 2816
KF = FF // P
EPS = 1e-6
GN_EPS = 64e-5
NEG = -1e30
PAD = 4
RING = 4
CH = 128
LEVELS = 7
DECAY = float(np.exp(-0.5))
HALF = DECAY * CH / 2

FQ, FK, SQ, SK, RR, RK, RV, MISC, LX, GATE = 0, 2, 4, 6, 8, 10, 12, 14, 15, 17
N1F, N1T = 25, 4
DK, NK, FO, DQ, NQ = 0, 2, 4, 6, 8
N2F = 10

CONST, CONST_FIRST = {}, {}
for _table, _entries in (
        (CONST, (("ident", P), ("ones", P), ("block32", P), ("block64", P), ("rope_swap", P), ("window", HD),
                 ("dft64", 2 * P))),
        (CONST_FIRST, (("tri_ge", P), ("causal_add", P), ("stick_big", P), ("strict_t", P), ("incl_t", P),
                       ("head_row", H * P), ("head_pair", 2), ("level", LEVELS * P), ("level0_t", P),
                       ("chunk_keep", S), ("keep_all", S)))):
    _at = 0
    for _name, _n in _entries:
        _table[_name] = (_at, _at + _n)
        _at += _n

PRM = {}
_at = 0
for _name, _n in (("norm_g", KD), ("final_g", KD), ("mu", 7), ("w0", 2), ("a0", 2), ("k_k", 2),
                  ("k_a", 2), ("r_k", 2), ("conv_w", 8), ("conv_b", 2), ("b_a", 2), ("b_x", 2),
                  ("lam", 2), ("b_f", 1), ("c", 2 * KD),
                  ("g_mix", 2 * KD), ("g_ffn", 2 * KD), ("b_ada", 2 * 48), ("conv_b2", 2 * 44),
                  ("conv_w2", 2 * 3 * 44), ("dqn", 2), ("dkn", 2), ("nqn", 2), ("nkn", 2),
                  ("gmlp_b", 2 * H)):
    PRM[_name] = (_at, _at + _n)
    _at += _n
NPRM = _at

ROW = {}
_at = 0
for _name, _n in (("ln_g", G), ("ln_b", G), ("subln", 2 * G), ("gmlp_g", 2 * G), ("lam4", 2 * 128)):
    ROW[_name] = (_at, _at + _n)
    _at += _n
NROW = _at
ROWS_FIRST = 2 * G


def lambda_init(layer):
    return 0.8 - 0.6 * float(np.exp(-0.3 * layer))


class Kit:
    pass


class Signal:

    def __init__(self, nc, ctx, name):
        self.sem = ctx.enter_context(nc.semaphore(name))
        self.n = 0
        self.base = 0

    def up(self, instruction, by=1):
        instruction.then_inc(self.sem, by)
        self.n += by
        return self.n


def start_phase(K):
    for s in K.signals.values():
        s.base = s.n


def link(eng, signal, instruction):
    eng.wait_ge(signal.sem, signal.up(instruction))


def exp_and_log(act):
    act.preload_act_table_set("natural_log_exp_and_others")


def meet(K):
    goal = K.met.n + 4
    @K.block.tensor
    def _(e):
        e.drain().then_inc(K.met.sem, 1)
        e.wait_ge(K.met.sem, goal)
    @K.block.vector
    def _(e):
        e.drain().then_inc(K.met.sem, 1)
        e.wait_ge(K.met.sem, goal)
    @K.block.scalar
    def _(e):
        e.drain().then_inc(K.met.sem, 1)
        e.wait_ge(K.met.sem, goal)
    @K.block.gpsimd
    def _(e):
        e.drain().then_inc(K.met.sem, 1)
        e.wait_ge(K.met.sem, goal)
    K.met.n = goal
    start_phase(K)


def arena(K, ctx, name, shape, dtype=F32):
    K.serial += 1
    return ctx.enter_context(K.nc.sbuf_tensor(f"{name}_{K.serial}", shape, dtype))


def arena_pair(K, ctx, name, shape):
    return arena(K, ctx, name + "_high", shape, F32R), arena(K, ctx, name + "_low", shape, F32R)


def three_products(pe, out, lhs, rhs, first, last):
    (lh, ll), (rh, rl) = lhs, rhs
    pe.matmul(out, lh, rh, start=first, stop=False, skip_group_check=True)
    pe.matmul(out, lh, rl, start=False, stop=False, skip_group_check=True)
    return pe.matmul(out, ll, rh, start=False, stop=last, skip_group_check=True)


def const(K, name, rows=slice(0, P)):
    if name in CONST:
        a, b = CONST[name]
        return K.cst[rows, a:b]
    a, b = CONST_FIRST[name]
    return K.cst_first[rows, a:b]


def prm(K, name, col=0, n=1, rows=slice(0, P)):
    a = PRM[name][0] + col
    return K.prm[rows, a:a + n]


def row(K, name, first=0, n=G):
    a = ROW[name][0] + first
    return K.rows_first[:, a:a + n] if a < ROWS_FIRST else K.rows[:, a - ROWS_FIRST:a - ROWS_FIRST + n]



def stream_weights(K, n_units):
    @K.block.sync
    def _(sp):
        for j in range(RING):
            sp.dma_start(K.ring[:, j], K.w_units[j]).then_inc(K.slot_full[j].sem, 16)
        with sp.Fori(0, n_units // RING - 1) as i:
            for j in range(RING):
                sp.wait_ge(K.unit_used.sem, i * RING + j + 1)
                sp.dma_start(K.ring[:, j], K.w_units[ds(i * RING + (j + RING), 1)]
                             .rearrange("u p n -> (u p) n")).then_inc(K.slot_full[j].sem, 16)
        for u in range(n_units - n_units % RING, n_units):
            sp.wait_ge(K.unit_used.sem, u - RING + 1)
            sp.dma_start(K.ring[:, u % RING], K.w_units[u]).then_inc(K.slot_full[u % RING].sem, 16)



def rms_phase(K, src, dst, parts, room=None):
    square, stat, rstd_ready, scaled, high_ready, low_ready = (K.signals[n] for n in (
        "square", "stat", "rstd", "normed", "high_ready", "low_ready"))
    split = isinstance(dst, tuple)
    with ExitStack() as ctx:
        sq, rstd = room or (arena(K, ctx, "squares", [P, KD, S]),
                            arena(K, ctx, "rstd", [P, max(c0 + w for c0, w, _, _ in parts)]))

        @K.block.scalar
        def _(act):
            exp_and_log(act)
            for n, (c0, w, _, shift) in enumerate(parts):
                if n:
                    act.wait_ge(low_ready.sem, low_ready.base + n * KD)
                for k in range(KD):
                    square.up(act.activation(sq[:, k, 0:w], src[:, k, c0:c0 + w], ACT.Square))
                act.wait_ge(stat.sem, stat.base + n + 1)
                link(act, K.act_step, act.activation(rstd[:, c0:c0 + w], K.ps[n][:, 0:w], ACT.Ln,
                                                     bias=K.eps[:, 0:1], scale=1.0 / D))
                rstd_ready.up(act.activation(rstd[:, c0:c0 + w], rstd[:, c0:c0 + w], ACT.Exp, scale=-0.5))
                for k in range(KD if split else 0):
                    act.wait_ge(scaled.sem, scaled.base + n * KD + k + 1)
                    t = sq[:, k, 0:w]
                    if shift is None:
                        high_ready.up(act.copy(dst[0][:, k, c0:c0 + w], t))
                    else:
                        link(act, K.act_step, act.activation(t, t, ACT.Identity, bias=shift(k)))
                        high_ready.up(act.copy(dst[0][:, k, c0:c0 + w], t))

        @K.block.tensor
        def _(pe):
            for n, (c0, w, _, _) in enumerate(parts):
                for k in range(KD):
                    pe.wait_ge(square.sem, square.base + n * KD + k + 1)
                    mm = pe.matmul(K.ps[n][:, 0:w], const(K, "ones"), sq[:, k, 0:w],
                                   start=(k == 0), stop=(k == KD - 1))
                stat.up(mm)

        @K.block.vector
        def _(dve):
            for n, (c0, w, gain, shift) in enumerate(parts):
                dve.wait_ge(rstd_ready.sem, rstd_ready.base + n + 1)
                for k in range(KD):
                    to = sq[:, k, 0:w] if split else dst[:, k, c0:c0 + w]
                    scaled.up(dve.scalar_tensor_tensor(to, src[:, k, c0:c0 + w], gain(k), rstd[:, c0:c0 + w],
                                                       ALU.mult, ALU.mult))
                for k in range(KD if split else 0):
                    dve.wait_ge(high_ready.sem, high_ready.base + n * KD + k + 1)
                    low_ready.up(dve.tensor_tensor(dst[1][:, k, c0:c0 + w], sq[:, k, 0:w],
                                                   dst[0][:, k, c0:c0 + w].bitcast(F32), ALU.subtract))
        meet(K)


def split_phase(K, src, dst, w):
    high_ready = K.signals["high_ready"]

    @K.block.scalar
    def _(act):
        for k in range(KD):
            high_ready.up(act.copy(dst[0][:, k, 0:w], src[:, k, 0:w]))

    @K.block.vector
    def _(dve):
        for k in range(KD):
            dve.wait_ge(high_ready.sem, high_ready.base + k + 1)
            dve.tensor_tensor(dst[1][:, k, 0:w], src[:, k, 0:w], dst[0][:, k, 0:w].bitcast(F32), ALU.subtract)
    meet(K)



def split_high(K, act, i, j, guard=True):
    q = K.unit + j
    act.wait_ge(K.slot_full[q % RING].sem, i * 16 + 16 * (q // RING + 1))
    if guard:
        act.wait_ge(K.unit_done.sem, i * RING + (K.unit_done.base + j - 1))
    act.copy(K.w_high[:, q % 2], K.ring[:, q % RING]).then_inc(K.high_split.sem, 1)


def split_low(K, dve, i, j):
    q = K.unit + j
    dve.wait_ge(K.high_split.sem, i * RING + (K.high_split.base + j + 1))
    dve.tensor_tensor(K.w_low[:, q % 2], K.ring[:, q % RING], K.w_high[:, q % 2].bitcast(F32),
                      ALU.subtract).then_inc(K.unit_used.sem, 1)


def weights(K, q, k):
    c = slice(k * P, k * P + P)
    return K.w_high[:, q % 2, c], K.w_low[:, q % 2, c]


def in_turns(eng, count, body):
    turns, rest = divmod(count, RING)
    if turns == 1:
        for j in range(RING):
            body(0, j)
    elif turns:
        with eng.Fori(0, turns) as i:
            for j in range(RING):
                body(i, j)
    for j in range(rest):
        body(turns, j)


def project(K, count, with_ctx, evac_main, evac_ctx, moving):
    main_free, ctx_free = K.signals["main_free"], K.signals["ctx_free"]
    first = K.unit
    part = lambda k, a, b: tuple(m[:, k, a:b] for m in moving)

    @K.block.tensor
    def _(pe):
        def unit(i, j):
            q = first + j
            pe.wait_ge(K.unit_used.sem, i * RING + (q + 1))
            pe.wait_ge(main_free.sem, i * RING + (j + main_free.base + 1))
            if with_ctx:
                pe.wait_ge(ctx_free.sem, i * RING + (j + ctx_free.base + 1))
            for k in range(KD):
                mm = three_products(pe, K.ps[j][:, :], weights(K, q, k), part(k, 0, S), k == 0, k == KD - 1)
                if with_ctx:
                    mm = three_products(pe, K.ps[4 + j][:, 0:C], weights(K, q, k), part(k, S, S + C),
                                        k == 0, k == KD - 1)
            mm.then_inc(K.unit_done.sem, 1)
        in_turns(pe, count, unit)

    @K.block.vector
    def _(dve):
        def empty(i, j):
            dve.wait_ge(K.unit_done.sem, i * RING + (j + K.unit_done.base + 1))
            evac_main(dve, i * RING + j, K.ps[j]).then_inc(main_free.sem, 1)

        def unit(i, j):
            split_low(K, dve, i, j + 1)
            empty(i, j)
        dve.sem_inc(main_free.sem, RING)
        split_low(K, dve, 0, 0)
        in_turns(dve, count - 1, unit)
        empty(*divmod(count - 1, RING))

    @K.block.scalar
    def _(act):
        def empty(i, j):
            if with_ctx:
                act.wait_ge(K.unit_done.sem, i * RING + (j + K.unit_done.base + 1))
                evac_ctx(act, i * RING + j, K.ps[4 + j]).then_inc(ctx_free.sem, 1)

        def unit(i, j):
            split_high(K, act, i, j + 1)
            empty(i, j)
        if with_ctx:
            act.sem_inc(ctx_free.sem, RING)
        split_high(K, act, 0, 0, guard=False)
        in_turns(act, count - 1, unit)
        empty(*divmod(count - 1, RING))
    if with_ctx:
        ctx_free.n += RING + count
    main_free.n += RING + count
    K.unit_used.n += count
    K.unit_done.n += count
    K.high_split.n += count
    K.unit += count
    meet(K)


def project_tokens(K, buf, tiles, moving):
    tile_done = K.signals["tile_done"]
    first, units = K.unit, 4

    @K.block.tensor
    def _(pe):
        for j in range(units):
            q = first + j
            pe.wait_ge(K.unit_used.sem, q + 1)
            for m in range(tiles):
                for kk in range(2):
                    k, c = 2 * j + kk, slice(kk * S, kk * S + S)
                    mm = three_products(pe, K.ps[m][:, :], tuple(x[:, k, m * P:m * P + P] for x in moving),
                                        (K.w_high[:, q % 2, c], K.w_low[:, q % 2, c]), k == 0, k == KD - 1)
                if j == units - 1:
                    tile_done.up(mm)
            if j < units - 1:
                mm.then_inc(K.unit_done.sem, 1)
        pe.sem_inc(K.unit_done.sem, 1)

    @K.block.vector
    def _(dve):
        for j in range(units):
            split_low(K, dve, 0, j)
        for m in range(min(NT, tiles)):
            dve.wait_ge(tile_done.sem, tile_done.base + m + 1)
            dve.tensor_copy(buf[:, m, :], K.ps[m][:, :])

    @K.block.scalar
    def _(act):
        for j in range(units):
            split_high(K, act, 0, j, guard=j > 0)
        for m in range(NT, tiles):
            act.wait_ge(tile_done.sem, tile_done.base + m + 1)
            act.copy(buf[:, m, :], K.ps[m][:, :])
    for s in (K.unit_used, K.unit_done, K.high_split):
        s.n += units
    K.unit += units
    meet(K)



def softmax_attention(K, items, scale, neg_lam=None, beside=None):
    n_comp = len(items[0]["scores"])
    scored, max_ready, exped, weighted, turned_up, turned_out, mixed, put = (K.signals[n] for n in (
        "scored", "max_ready", "exped", "weighted", "turned_up", "turned_out", "mixed", "put"))
    n_items = len(items)
    kmax = max(i["kw"] for i in items)
    biased = items[0]["bias"] is not None
    split = kmax > S
    copies = 2 if split else 1
    slot, out_bank = (2 * S, 6) if split else (S, 2)
    with ExitStack() as ctx:
        probs = arena(K, ctx, "probs", [P, 2, n_comp, kmax])
        turned = arena(K, ctx, "turned", [P, 2, kmax])
        logits = arena(K, ctx, "logits", [P, 2, kmax]) if biased else None
        neg_max = arena(K, ctx, "neg_max", [P, n_items, n_comp])
        row_sum = arena(K, ctx, "row_sum", [P, n_items, n_comp])
        inv = arena(K, ctx, "inv", [P, n_items, n_comp])

        def score_tile(t, c, a, b):
            first = slot * ((t * n_comp + c) % 2)
            return K.psum[:, first + a:first + b]

        @K.block.tensor
        def _(pe):
            def scores(t):
                for c in range(n_comp):
                    n = t * n_comp + c
                    if n >= 2:
                        pe.wait_ge(exped.sem, exped.base + n - 1)
                    for group in items[t]["scores"][c]:
                        for g, (lhs, rhs, c0, w) in enumerate(group):
                            mm = pe.matmul(score_tile(t, c, c0, c0 + w), lhs, rhs,
                                           start=(g == 0), stop=(g == len(group) - 1),
                                           skip_group_check=len(group) > 1)
                    scored.up(mm)

            def turn(t):
                if n_comp == 1:
                    pe.wait_ge(exped.sem, exped.base + t + 1)
                else:
                    pe.wait_ge(weighted.sem, weighted.base + t + 1)
                if t >= 1:
                    pe.wait_ge(turned_out.sem, turned_out.base + copies * t)
                for b in range(items[t]["kw"] // P):
                    mm = pe.transpose(K.psum[:, 4 * S + b * P:4 * S + b * P + P],
                                      probs[:, t % 2, 0, b * P:b * P + P], const(K, "ident"))
                turned_up.up(mm)

            def mix(t):
                pe.wait_ge(turned_out.sem, turned_out.base + copies * (t + 1))
                if t >= 2:
                    pe.wait_ge(put.sem, put.base + t - 1)
                tiles = items[t]["tiles"]
                for b, tile in enumerate(tiles):
                    mm = pe.matmul(K.ps[out_bank + t % 2][:, 0:HD], turned[:, t % 2, b * P:b * P + P],
                                   items[t]["v"](tile), start=(b == 0), stop=(b == len(tiles) - 1))
                mixed.up(mm)

            for t in range(n_items + 2):
                if t < n_items:
                    scores(t)
                if beside:
                    beside(pe)
                if 0 <= t - 1 < n_items:
                    turn(t - 1)
                if 0 <= t - 2 < n_items:
                    mix(t - 2)

        @K.block.vector
        def _(dve):
            def maxima(t):
                kw, bias = items[t]["kw"], items[t]["bias"]
                for c in range(n_comp):
                    dve.wait_ge(scored.sem, scored.base + t * n_comp + c + 1)
                    m = neg_max[:, t, c:c + 1]
                    if bias is None:
                        link(dve, K.dve_step, dve.reduce_max(m, score_tile(t, c, 0, kw), AX, negate=True))
                        max_ready.up(dve.tensor_scalar(m, m, scale, None, ALU.mult))
                        continue
                    if t >= 2:
                        dve.wait_ge(exped.sem, exped.base + t - 1)
                    ins = dve.scalar_tensor_tensor(logits[:, t % 2, 0:S], score_tile(t, c, 0, S), scale, bias,
                                                   ALU.mult, ALU.add)
                    if kw > S:
                        ins = dve.tensor_scalar(logits[:, t % 2, S:kw], score_tile(t, c, S, kw), scale, None,
                                                ALU.mult)
                    link(dve, K.dve_step, ins)
                    max_ready.up(dve.reduce_max(m, logits[:, t % 2, 0:kw], AX, negate=True))

            def combine(t):
                kw = items[t]["kw"]
                dve.wait_ge(exped.sem, exped.base + (t + 1) * n_comp)
                link(dve, K.dve_step, dve.reciprocal(inv[:, t, :], row_sum[:, t, :]))
                link(dve, K.dve_step, dve.tensor_tensor(inv[:, t, 1:2], inv[:, t, 1:2], neg_lam, ALU.mult))
                p0, p1 = probs[:, t % 2, 0, 0:kw], probs[:, t % 2, 1, 0:kw]
                link(dve, K.dve_step, dve.tensor_scalar(p1, p1, inv[:, t, 1:2], None, ALU.mult))
                weighted.up(dve.scalar_tensor_tensor(p0, p0, inv[:, t, 0:1], p1, ALU.mult, ALU.add))

            def copy_turned(t):
                dve.wait_ge(turned_up.sem, turned_up.base + t + 1)
                if t >= 2:
                    dve.wait_ge(mixed.sem, mixed.base + t - 1)
                w = min(items[t]["kw"], S)
                turned_out.up(dve.tensor_copy(turned[:, t % 2, 0:w], K.psum[:, 4 * S:4 * S + w]))

            def output(t):
                dve.wait_ge(mixed.sem, mixed.base + t + 1)
                src = K.ps[out_bank + t % 2][:, 0:HD]
                if n_comp == 1:
                    link(dve, K.dve_step, dve.reciprocal(inv[:, t, :], row_sum[:, t, :]))
                    put.up(dve.tensor_scalar(items[t]["out"], src, inv[:, t, 0:1], None, ALU.mult))
                else:
                    put.up(dve.tensor_copy(items[t]["out"], src))

            for t in range(n_items + 2):
                if n_comp == 2 and 0 <= t - 1 < n_items:
                    combine(t - 1)
                if t < n_items:
                    maxima(t)
                if 0 <= t - 1 < n_items:
                    copy_turned(t - 1)
                if 0 <= t - 2 < n_items:
                    output(t - 2)

        @K.block.scalar
        def _(act):
            def exponentials(t):
                kw, bias = items[t]["kw"], items[t]["bias"]
                if t >= 2:
                    act.wait_ge(turned_up.sem, turned_up.base + t - 1)
                for c in range(n_comp):
                    act.wait_ge(max_ready.sem, max_ready.base + t * n_comp + c + 1)
                    src = logits[:, t % 2, 0:kw] if bias is not None else score_tile(t, c, 0, kw)
                    exped.up(act.activation(probs[:, t % 2, c, 0:kw], src, ACT.Exp, bias=neg_max[:, t, c:c + 1],
                                            scale=1.0 if bias is not None else scale,
                                            accum_out=row_sum[:, t, c:c + 1]))

            def copy_turned(t):
                act.wait_ge(turned_up.sem, turned_up.base + t + 1)
                if t >= 2:
                    act.wait_ge(mixed.sem, mixed.base + t - 1)
                turned_out.up(act.copy(turned[:, t % 2, S:kmax], K.psum[:, 5 * S:4 * S + kmax]))

            act.preload_act_table(ACT.Exp)
            for t in range(n_items + 1):
                if t < n_items:
                    exponentials(t)
                if split and 0 <= t - 1 < n_items:
                    copy_turned(t - 1)
        meet(K)


def to_feature_major(K, y, tiles, put):
    turned_up, put_done = K.signals["turned_up"], K.signals["put"]

    @K.block.tensor
    def _(pe):
        for u in range(2):
            for n, m in enumerate(tiles):
                mm = pe.transpose(K.ps[u][:, n * P:n * P + P], y[:, m, u * P:u * P + P], const(K, "ident"))
            turned_up.up(mm)

    @K.block.vector
    def _(dve):
        for u in range(2):
            dve.wait_ge(turned_up.sem, turned_up.base + u + 1)
            put_done.up(put(dve, u, K.ps[u][:, 0:len(tiles) * P]))
    meet(K)



def forgetting_attention(K, p, v, y):
    gates, = (K.signals[n] for n in ("prepared",))
    rows = slice(64, 64 + H)
    with ExitStack() as ctx:
        x = arena(K, ctx, "gate_x", [P, S])
        a = arena(K, ctx, "gate_a", [P, S])
        cum = arena(K, ctx, "neg_cum", [P, S])

        @K.block.vector
        def _(dve):
            dve.memset(cum[:, :], 0.0)
            link(dve, K.dve_step, dve.tensor_scalar(x[rows, :], p[rows, MISC, PAD:PAD + S],
                                                    prm(K, "b_f", rows=rows), None, ALU.add))
            gates.up(dve.tensor_scalar(a[rows, :], x[rows, :], -1.0, None, ALU.mult))
            dve.wait_ge(K.signals["soft"].sem, K.signals["soft"].base + 1)
            link(dve, K.dve_step, dve.tensor_scalar(x[rows, :], x[rows, :], 0.0, -1.0, ALU.min, ALU.mult))
            link(dve, K.dve_step, dve.tensor_tensor(x[rows, :], x[rows, :], a[rows, :], ALU.add))
            link(dve, K.dve_step, dve.tensor_tensor_scan(cum[rows, :], const(K, "keep_all", rows), x[rows, :], 0.0,
                                                         ALU.mult, ALU.add))

        @K.block.scalar
        def _(act):
            exp_and_log(act)
            act.wait_ge(gates.sem, gates.base + 1)
            for func, scale, bias in ((ACT.Abs, 1.0, 0.0), (ACT.Exp, -1.0, 0.0)):
                link(act, K.act_step, act.activation(a[rows, :], a[rows, :], func, scale=scale))
            K.signals["soft"].up(act.activation(a[rows, :], a[rows, :], ACT.Ln, bias=K.one[rows, 0:1]))
        meet(K)

        items = []
        for h in range(H):
            i, r = h // 2, slice(64 * (h % 2), 64 * (h % 2) + HD)
            for t in range(NT):
                kw = (t + 1) * P
                q = p[r, FQ + i, PAD + t * P:PAD + t * P + P]
                items.append(dict(
                    scores=[[[(q, p[r, FK + i, PAD:PAD + kw], 0, kw),
                              (const(K, "head_row")[:, h * P:h * P + P], cum[:, 0:kw], 0, kw),
                              (const(K, "ident"), const(K, "causal_add"), t * P, P)]]],
                    kw=kw, tiles=range(t + 1), bias=None,
                    v=lambda m, h=h: v[:, m, h * HD:h * HD + HD], out=y[:, t, h * HD:h * HD + HD]))
        softmax_attention(K, items, HD ** -0.5, beside=lambda pe: modulation_units(K, pe, 2))



def stick_breaking_attention(K, p, v, y):
    scored, zed, softp, summed, diff, weighed, mixed, put = (K.signals[n] for n in (
        "scored", "exped", "soft", "summed", "prepared", "weighted", "mixed", "put"))
    with ExitStack() as ctx:
        z = arena(K, ctx, "stick_z", [P, 2, S])
        e = arena(K, ctx, "stick_e", [P, 2, S])
        sp = arena(K, ctx, "stick_softplus", [P, 2, NT, S])
        w = arena(K, ctx, "stick_weights", [P, 2, NT, S])
        steps = [(h, t) for h in range(H) for t in reversed(range(NT))]

        @K.block.tensor
        def _(pe):
            def scores(n):
                h, t = steps[n]
                i, r = h // 2, slice(64 * (h % 2), 64 * (h % 2) + HD)
                if n >= 2:
                    pe.wait_ge(softp.sem, softp.base + n - 1)
                    pe.wait_ge(zed.sem, zed.base + n - 1)
                scored.up(pe.matmul(K.ps[n % 2][:, t * P:S], p[r, SK + i, PAD + t * P:PAD + t * P + P],
                                    p[r, SQ + i, PAD + t * P:PAD + S], start=True, stop=True))

            def sums(n):
                h, t = steps[n]
                pe.wait_ge(softp.sem, softp.base + n + 1)
                if n >= 2:
                    pe.wait_ge(diff.sem, diff.base + n - 1)
                bank = K.ps[2 + n % 2]
                pe.matmul(bank[:, t * P:S], const(K, "tri_ge"), sp[:, h % 2, t, t * P:S],
                          start=True, stop=False, skip_group_check=True)
                for j in range(t + 1, NT):
                    pe.matmul(bank[:, j * P:S], const(K, "ones"), sp[:, h % 2, j, j * P:S],
                              start=False, stop=False, skip_group_check=True)
                summed.up(pe.matmul(bank[:, t * P:t * P + P], const(K, "ident"), const(K, "stick_big"),
                                    start=False, stop=True, skip_group_check=True))

            def mix(h):
                pe.wait_ge(weighed.sem, weighed.base + NT * (h + 1))
                if h >= 2:
                    pe.wait_ge(put.sem, put.base + h - 1)
                bank = K.ps[4 + h % 2]
                for m in range(NT):
                    for t in range(m + 1):
                        mm = pe.matmul(bank[:, m * HD:m * HD + HD], w[:, h % 2, t, m * P:m * P + P],
                                       v[:, t, h * HD:h * HD + HD], start=(t == 0), stop=(t == m))
                mixed.up(mm)

            for n in range(len(steps) + 1):
                if n < len(steps):
                    scores(n)
                modulation_units(K, pe, 2)
                if n >= 1:
                    sums(n - 1)
                if n % NT == 1 and n > NT:
                    mix(n // NT - 1)
            mix(H - 1)

        @K.block.scalar
        def _(act):
            def soft(n):
                h, t = steps[n]
                src = K.ps[n % 2][:, t * P:S]
                act.wait_ge(scored.sem, scored.base + n + 1)
                if n >= 2:
                    act.wait_ge(softp.sem, softp.base + n - 1)
                    act.wait_ge(diff.sem, diff.base + n - 1)
                act.activation(z[:, n % 2, t * P:S], src, ACT.Identity, scale=HD ** -0.5)
                link(act, K.act_step, act.activation(e[:, n % 2, t * P:S], src, ACT.Abs, scale=HD ** -0.5))
                link(act, K.act_step, act.activation(e[:, n % 2, t * P:S], e[:, n % 2, t * P:S], ACT.Exp,
                                                     scale=-1.0))
                zed.up(act.activation(e[:, n % 2, t * P:S], e[:, n % 2, t * P:S], ACT.Ln, bias=K.one[:, 0:1]))

            def weigh(n):
                h, t = steps[n]
                act.wait_ge(diff.sem, diff.base + n + 1)
                part = w[:, h % 2, t, t * P:S]
                weighed.up(act.activation(part, part, ACT.Exp))

            exp_and_log(act)
            for n in range(len(steps) + 1):
                if n < len(steps):
                    soft(n)
                if n >= 1:
                    weigh(n - 1)

        @K.block.vector
        def _(dve):
            def soft(n):
                h, t = steps[n]
                dve.wait_ge(zed.sem, zed.base + n + 1)
                if h >= 2 and t == NT - 1:
                    dve.wait_ge(summed.sem, summed.base + NT * (h - 1))
                part = sp[:, h % 2, t, t * P:S]
                link(dve, K.dve_step, dve.scalar_tensor_tensor(part, z[:, n % 2, t * P:S], 0.0,
                                                               e[:, n % 2, t * P:S], ALU.max, ALU.add))
                part = sp[:, h % 2, t, t * P:t * P + P]
                softp.up(dve.tensor_tensor(part, part, const(K, "strict_t"), ALU.mult))

            def differ(n):
                h, t = steps[n]
                dve.wait_ge(summed.sem, summed.base + n + 1)
                if h >= 2 and t == NT - 1:
                    dve.wait_ge(mixed.sem, mixed.base + h - 1)
                diff.up(dve.tensor_tensor(w[:, h % 2, t, t * P:S], z[:, n % 2, t * P:S],
                                          K.ps[2 + n % 2][:, t * P:S], ALU.subtract))

            def output(h):
                dve.wait_ge(mixed.sem, mixed.base + h + 1)
                put.up(dve.tensor_copy(y[:, :, h * HD:h * HD + HD],
                                       K.ps[4 + h % 2][:, 0:NT * HD].rearrange("p (m d) -> p m d", m=NT)))

            for n in range(len(steps) + 1):
                if n < len(steps):
                    soft(n)
                if n >= 1:
                    differ(n - 1)
                if n % NT == 2 and n > NT:
                    output(n // NT - 1)
            output(H - 1)
        meet(K)



def rg_lru(K, p, out):
    conv, gated, rate_ready, done = (K.signals[n] for n in ("prepared", "scored", "exped", "weighted"))
    with ExitStack() as ctx:
        xc = arena(K, ctx, "lru_x", [P, 2, S])
        r = arena(K, ctx, "lru_r", [P, 2, S])
        g = arena(K, ctx, "lru_i", [P, 2, S])
        a = arena(K, ctx, "lru_a", [P, 2, S])
        th = arena(K, ctx, "lru_tanh", [P, 2, S])
        s8 = arena(K, ctx, "lru_rate", [P, 2])
        w = arena(K, ctx, "lru_w", [P, 4, P])

        @K.block.gpsimd
        def _(pool):
            K.loaded_late.up(pool.dma_start(w[:, :, :], K.lru_w_dram.rearrange("p (a b) -> p a b", a=4)), 16)
        w_value = K.loaded_late.n

        @K.block.vector
        def _(dve):
            for i in range(2):
                x = lambda k: p[:, LX + i, PAD - 3 + k:PAD - 3 + k + S]
                cw = lambda k: prm(K, "conv_w", 2 * k + i)
                link(dve, K.dve_step, dve.tensor_scalar(xc[:, i], x(0), cw(0), prm(K, "conv_b", i),
                                                        ALU.mult, ALU.add))
                for k in range(1, 4):
                    ins = dve.scalar_tensor_tensor(xc[:, i], x(k), cw(k), xc[:, i], ALU.mult, ALU.add)
                    if k < 3:
                        link(dve, K.dve_step, ins)
                conv.up(ins)
            for i in range(2):
                dve.wait_ge(rate_ready.sem, rate_ready.base + 1 + i)
                link(dve, K.dve_step, dve.tensor_tensor(g[:, i], g[:, i], xc[:, i], ALU.mult))
                link(dve, K.dve_step, dve.scalar_tensor_tensor(th[:, i], r[:, i], 1.0, th[:, i], ALU.add, ALU.mult))
            done.up(dve.tensor_scalar(th[:, :, :], th[:, :, :], 0.0, None, ALU.max))
            dve.wait_ge(rate_ready.sem, rate_ready.base + 4)
            for i in range(2):
                link(dve, K.dve_step, dve.tensor_tensor(g[:, i], g[:, i], th[:, i], ALU.mult))
                link(dve, K.dve_step, dve.tensor_tensor_scan(xc[:, i], a[:, i], g[:, i], 0.0, ALU.mult, ALU.add))
                out(dve, i, xc[:, i])

        @K.block.tensor
        def _(pe):
            pe.wait_ge(K.loaded_late.sem, w_value)
            for i in range(2):
                pe.wait_ge(conv.sem, conv.base + i + 1)
                pe.matmul(K.ps[2 * i][:, :], w[:, i], xc[:, i], start=True, stop=True)
                gated.up(pe.matmul(K.ps[2 * i + 1][:, :], w[:, 2 + i], xc[:, i], start=True, stop=True))

        @K.block.scalar
        def _(act):
            t0, t1 = th[:, 0, 0:2], th[:, 0, 2:4]
            link(act, K.act_step, act.activation(t0, prm(K, "lam", 0, 2), ACT.Abs))
            link(act, K.act_step, act.activation(t0, t0, ACT.Exp, scale=-1.0))
            link(act, K.act_step, act.activation(t0, t0, ACT.Ln, bias=K.one[:, 0:1]))
            link(act, K.act_step, act.activation(t1, prm(K, "lam", 0, 2), ACT.Relu, scale=-1.0))
            link(act, K.act_step, act.activation(t1[:, 0:1], t1[:, 0:1], ACT.Identity, bias=t0[:, 0:1]))
            link(act, K.act_step, act.activation(t1[:, 1:2], t1[:, 1:2], ACT.Identity, bias=t0[:, 1:2]))
            link(act, K.act_step, act.activation(s8[:, :], t1, ACT.Identity, scale=-8.0))
            act.wait_ge(gated.sem, gated.base + 2)
            for i in range(2):
                act.activation(r[:, i], K.ps[2 * i][:, :], ACT.Sigmoid, bias=prm(K, "b_a", i))
                link(act, K.act_step, act.activation(g[:, i], K.ps[2 * i + 1][:, :], ACT.Sigmoid,
                                                     bias=prm(K, "b_x", i)))
            for i in range(2):
                link(act, K.act_step, act.activation(r[:, i], r[:, i], ACT.Identity, scale=s8[:, i:i + 1]))
                act.activation(a[:, i], r[:, i], ACT.Exp)
                link(act, K.act_step, act.activation(th[:, i], r[:, i], ACT.Tanh, scale=-1.0))
                rate_ready.up(act.activation(r[:, i], r[:, i], ACT.Exp, scale=2.0))
            act.wait_ge(done.sem, done.base + 1)
            for i in range(2):
                rate_ready.up(act.activation(th[:, i], th[:, i], ACT.Sqrt))
        meet(K)



def rwkv(K, p, y):
    sig = K.signals
    with ExitStack() as ctx:
        nd = arena(K, ctx, "log_decay", [P, 2, S])
        cl = arena(K, ctx, "cum_log_decay", [P, 2, S])
        rate = arena(K, ctx, "rate", [P, 2, S])
        kk = arena(K, ctx, "kk", [P, 2, S])
        t0 = arena(K, ctx, "rwkv_t0", [P, 2, S])
        t1 = arena(K, ctx, "rwkv_t1", [P, 2, S])
        t2 = arena(K, ctx, "rwkv_t2", [P, 2, S])
        rkr = arena(K, ctx, "rwkv_rkr", [P, 2, S])
        decay_end = arena(K, ctx, "decay_end", [P, 2, NT])
        one_less = arena(K, ctx, "one_less_k_a", [P, 2])
        inner = ctx.enter_context(ExitStack())
        shifted = arena(K, inner, "shifted", [P, S])
        low = arena(K, inner, "low_rank", [P, S])
        lora = arena(K, inner, "lora", [64, G])
        col = lambda u: p[:, u:u + 2, PAD:PAD + S]
        r, k, v = col(RR), col(RK), col(RV)

        @K.block.gpsimd
        def _(pool):
            K.loaded_late.up(pool.dma_start(lora[:, :], K.lora_dram), 16)
        lora_value = K.loaded_late.n

        mixed, low_ready, projected, act_out, kk_out, normed = (sig[n] for n in (
            "prepared", "soft", "scored", "exped", "weighted", "summed"))

        @K.block.vector
        def _(dve):
            for n, u in enumerate((MISC, RR, RR + 1, RK, RK + 1, RV, RV + 1)):
                rows = slice(0, 64) if u == MISC else slice(0, P)
                if n:
                    dve.wait_ge(mixed.sem, mixed.base + n)
                cur, prev = p[rows, u, PAD:PAD + S], p[rows, u, PAD - 1:PAD - 1 + S]
                link(dve, K.dve_step, dve.tensor_tensor(shifted[rows, :], prev, cur, ALU.subtract))
                mixed.up(dve.scalar_tensor_tensor(cur, shifted[rows, :], prm(K, "mu", (n - 1) % 7, rows=rows), cur,
                                                  ALU.mult, ALU.add))
            dve.wait_ge(mixed.sem, mixed.base + 7)
            dve.tensor_scalar(one_less[:, :], prm(K, "k_a", 0, 2), -1.0, 1.0, ALU.mult, ALU.add)
            for i in range(2):
                ins = dve.tensor_scalar(kk[:, i], k[:, i], prm(K, "k_k", i), None, ALU.mult)
            kk_out.up(ins)
            dve.wait_ge(act_out.sem, act_out.base + 1)
            link(dve, K.dve_step, dve.tensor_scalar(nd[:, :, :], nd[:, :, :], -DECAY, None, ALU.mult))
            for i in range(2):
                ins = dve.tensor_tensor_scan(cl[:, i], const(K, "chunk_keep"), nd[:, i], 0.0, ALU.mult, ALU.add)
            link(dve, K.dve_step, ins)
            kk_out.up(dve.tensor_tensor(nd[:, :, :], cl[:, :, :], nd[:, :, :], ALU.subtract))
            for i in range(2):
                ins = dve.tensor_scalar(t0[:, i], rate[:, i], prm(K, "k_a", i), one_less[:, i:i + 1],
                                        ALU.mult, ALU.add)
            link(dve, K.dve_step, ins)
            link(dve, K.dve_step, dve.tensor_tensor(k, k, t0[:, :, :], ALU.mult))
            for i in range(2):
                dve.scalar_tensor_tensor(rkr[:, i], r[:, i], prm(K, "r_k", i), k[:, i], ALU.mult, ALU.mult)
            dve.wait_ge(normed.sem, normed.base + 1)
            for i in range(2):
                ins = dve.tensor_scalar(t0[:, i], K.ps[4 + i][:, :], 1e-12, None, ALU.max)
            kk_out.up(ins)
            dve.wait_ge(act_out.sem, act_out.base + 2)
            link(dve, K.dve_step, dve.tensor_tensor(kk[:, :, :], kk[:, :, :], t0[:, :, :], ALU.mult))
            dve.wait_ge(act_out.sem, act_out.base + 3)
            link(dve, K.dve_step, dve.tensor_tensor(rate[:, :, :], rate[:, :, :], kk[:, :, :], ALU.mult))
            dve.tensor_tensor(rate[:, :, :], rate[:, :, :], t2[:, :, :], ALU.mult)
            dve.scalar_tensor_tensor(kk[:, :, :], kk[:, :, :], -1.0, nd[:, :, :], ALU.mult, ALU.mult)
            dve.tensor_tensor(k, k, t2[:, :, :], ALU.mult)
            dve.tensor_tensor(r, r, t1[:, :, :], ALU.mult)

        @K.block.scalar
        def _(act):
            act.wait_ge(mixed.sem, mixed.base + 1)
            low_ready.up(act.activation(low[0:32, :], p[0:32, MISC, PAD:PAD + S], ACT.Tanh))
            low_ready.up(act.copy(low[32:64, :], p[32:64, MISC, PAD:PAD + S]))
            act.wait_ge(projected.sem, projected.base + 1)
            for i in range(2):
                act.activation(nd[:, i], K.ps[i][:, :], ACT.Sigmoid, bias=prm(K, "w0", i))
                ins = act.activation(rate[:, i], K.ps[2 + i][:, :], ACT.Sigmoid, bias=prm(K, "a0", i))
            act_out.up(ins)
            act.wait_ge(kk_out.sem, kk_out.base + 1)
            low_ready.up(act.activation(t1[:, :, :], kk[:, :, :], ACT.Square))
            act.wait_ge(kk_out.sem, kk_out.base + 3)
            link(act, K.act_step, act.activation(t0[:, :, :], t0[:, :, :], ACT.Ln))
            act_out.up(act.activation(t0[:, :, :], t0[:, :, :], ACT.Exp, scale=-0.5))
            act.activation(t1[:, :, :], cl[:, :, :], ACT.Exp, bias=K.half[:, 0:1])
            act.activation(t2[:, :, :], cl[:, :, :], ACT.Exp, bias=K.minus_half[:, 0:1], scale=-1.0)
            act.activation(decay_end[:, :, :], cl[:, :, CH - 1::CH], ACT.Exp)
            act_out.up(act.activation(nd[:, :, :], nd[:, :, :], ACT.Exp, bias=K.half[:, 0:1]))

        @K.block.tensor
        def _(pe):
            pe.wait_ge(K.loaded_late.sem, lora_value)
            pe.wait_ge(low_ready.sem, low_ready.base + 2)
            for i in range(2):
                pe.matmul(K.ps[i][:, :], lora[0:32, i * P:i * P + P], low[0:32, :], start=True, stop=True)
            for i in range(2):
                mm = pe.matmul(K.ps[2 + i][:, :], lora[32:64, i * P:i * P + P], low[32:64, :], start=True, stop=True)
            projected.up(mm)
            pe.wait_ge(low_ready.sem, low_ready.base + 3)
            for i in range(2):
                mm = pe.matmul(K.ps[4 + i][:, :], const(K, "block64"), t1[:, i], start=True, stop=True)
            normed.up(mm)
        meet(K)
        inner.close()

        tok = [x[:, :, :].rearrange("p i s -> p (i s)").rearrange("p (c f) -> p c f", c=NT) for x in (t0, t1, t2, cl)]
        a_tok, b_tok, k_tok, v_tok = tok
        turned_up, turned_out = sig["turned_up"], (sig["turned_out"], sig["put"])

        @K.block.tensor
        def _(pe):
            for q, x in enumerate((kk, rate, k, v)):
                for i in range(2):
                    if q == 3:
                        pe.wait_ge(turned_out[i].sem, turned_out[i].base + 1)
                    for c in range(NT):
                        mm = pe.transpose(K.ps[(2 * q + i) % 6][:, c * P:c * P + P], x[:, i, c * P:c * P + P],
                                          const(K, "ident"))
                    turned_up.up(mm)

        @K.block.vector
        def _(dve):
            for n in range(0, 8, 2):
                dve.wait_ge(turned_up.sem, turned_up.base + n + 1)
                ins = dve.tensor_copy(tok[n // 2][:, :, 0:P], K.ps[n % 6][:, :].rearrange("p (c f) -> p c f", c=NT))
                turned_out[0].up(ins)

        @K.block.scalar
        def _(act):
            for n in range(1, 8, 2):
                act.wait_ge(turned_up.sem, turned_up.base + n + 1)
                turned_out[1].up(act.copy(tok[n // 2][:, :, P:2 * P],
                                          K.ps[n % 6][:, :].rearrange("p (c f) -> p c f", c=NT)))
        meet(K)
        rwkv_chunks(K, kk, rate, k, r, a_tok, b_tok, k_tok, v_tok, decay_end, rkr, p, y)


def rwkv_chunks(K, ad, bd, kd, rd, a_tok, b_tok, k_tok, v_tok, decay_end, rkr, p, y):
    sig = K.signals
    produced, taken, x_ready, x_used, m_up, m_out, t_up, t_out, w_up, w_out, u_up, u_out, y_up, y_out, s_out = (
        sig[n] for n in ("produced", "taken", "x_ready", "x_used", "m_up", "m_out", "t_up", "t_out", "w_up",
                         "w_out", "u_up", "u_out", "y_up", "y_out", "s_out"))
    heads = [(e, i) for e in range(2) for i in range(2)]
    wide = lambda ap: ap.unsqueeze(1).to_broadcast([P, 2, P])
    with ExitStack() as ctx:
        a_mat, ak_t, rk_t, rb_t, t_mat, t_t, m_mat = (
            p[:, u, PAD:].rearrange("p (e i t) -> p e i t", e=2, i=2) for u in range(FQ, FQ + 7))
        x_mat = arena(K, ctx, "x_mat", [P, 2, 2, 2, P])
        ta_t = arena(K, ctx, "ta_t", [P, 2, P])
        w1 = arena(K, ctx, "w1", [P, G])
        u = arena(K, ctx, "u", [P, G])
        state = arena(K, ctx, "state", [P, 2, HD])
        bonus = arena(K, ctx, "bonus", [P, NT, H])
        row64 = lambda e: slice(64 * e, 64 * e + HD)
        hcol = lambda e, i: slice(i * P + e * HD, i * P + e * HD + HD)

        @K.block.tensor
        def _(pe):
            for c in range(NT):
                tc_ = slice(c * CH, c * CH + CH)
                if c:
                    pe.wait_ge(y_out.sem, y_out.base + c)
                    pe.wait_ge(s_out.sem, s_out.base + c + 1)
                else:
                    pe.wait_ge(s_out.sem, s_out.base + 1)
                for e in range(2):
                    r = row64(e)
                    for n, (l, m) in enumerate(((ad, bd), (bd, ad), (kd, ad), (kd, rd), (bd, rd))):
                        for i in range(2):
                            at = (n % 2) * 2 * P + i * P
                            mm = pe.matmul(K.ps[3 * e + n // 2][:, at:at + P], l[r, i, tc_], m[r, i, tc_],
                                           start=True, stop=True)
                for i in range(2):
                    mm = pe.matmul(K.ps[5][:, 2 * P + i * 2:2 * P + i * 2 + 2], rkr[:, i, tc_], const(K, "head_pair"),
                                   start=True, stop=True)
                produced.up(mm)
                for lev in range(1, LEVELS):
                    n = c * (LEVELS - 1) + lev - 1
                    pe.wait_ge(x_ready.sem, x_ready.base + n + 1)
                    pe.wait_ge(t_out.sem, t_out.base + c * LEVELS + lev)
                    for g, (e, i) in enumerate(heads):
                        mm = pe.matmul(K.ps[6][:, g * P:g * P + P], x_mat[:, n % 2, e, i], t_t[:, e, i],
                                       start=True, stop=True)
                    m_up.up(mm)
                    modulation_units(K, pe, 2)
                    pe.wait_ge(m_out.sem, m_out.base + n + 1)
                    for g, (e, i) in enumerate(heads):
                        pe.matmul(K.ps[0][:, g * P:g * P + P], t_mat[:, e, i], m_mat[:, e, i],
                                  start=True, stop=True)
                    for g, (e, i) in enumerate(heads):
                        mm = pe.matmul(K.ps[1][:, g * P:g * P + P], m_mat[:, e, i], t_mat[:, e, i],
                                       start=True, stop=True)
                    t_up.up(mm)
                    modulation_units(K, pe, 1)
                pe.wait_ge(t_out.sem, t_out.base + (c + 1) * LEVELS)
                for e, i in heads:
                    mm = pe.matmul(K.ps[2][:, hcol(e, i)], ak_t[:, e, i], v_tok[:, c, hcol(e, i)],
                                   start=True, stop=True)
                for e, i in heads:
                    mm = pe.matmul(K.ps[3][row64(e), i * P:i * P + P], a_tok[:, c, hcol(e, i)], t_t[:, e, i],
                                   start=True, stop=True)
                w_up.up(mm)
                pe.wait_ge(w_out.sem, w_out.base + c + 1)
                for e, i in heads:
                    pe.matmul(K.ps[4 + e][:, i * HD:i * HD + HD], t_t[:, e, i], w1[:, hcol(e, i)],
                              start=True, stop=False)
                    mm = pe.matmul(K.ps[4 + e][:, i * HD:i * HD + HD], ta_t[row64(e), i], state[row64(e), i],
                                   start=False, stop=True)
                u_up.up(mm)
                pe.wait_ge(u_out.sem, u_out.base + c + 1)
                for e, i in heads:
                    to = K.ps[2 + e][:, P * 2 + i * HD:P * 2 + i * HD + HD]
                    pe.matmul(to, rd[row64(e), i, tc_], state[row64(e), i], start=True, stop=False)
                    pe.matmul(to, rb_t[:, e, i], u[:, hcol(e, i)], start=False, stop=False)
                    pe.matmul(to, rk_t[:, e, i], v_tok[:, c, hcol(e, i)], start=False, stop=True)
                for e, i in heads:
                    to = K.ps[6][row64(e), i * HD:i * HD + HD]
                    pe.matmul(to, b_tok[:, c, hcol(e, i)], u[:, hcol(e, i)], start=True, stop=False)
                    mm = pe.matmul(to, k_tok[:, c, hcol(e, i)], v_tok[:, c, hcol(e, i)], start=False, stop=True)
                y_up.up(mm)

        @K.block.gpsimd
        def _(pool):
            for n in range(NT * (LEVELS - 1)):
                c, lev = divmod(n, LEVELS - 1)
                lev += 1
                pool.wait_ge(taken.sem, taken.base + c + 1)
                if n >= 2:
                    pool.wait_ge(m_up.sem, m_up.base + n - 1)
                mask = const(K, "level")[:, lev * P:lev * P + P]
                for e in range(2):
                    ins = pool.tensor_tensor(x_mat[:, n % 2, e], a_mat[:, e], wide(mask), ALU.mult)
                x_ready.up(ins)

        @K.block.vector
        def _(dve):
            s_out.up(dve.memset(state[:, :, :], 0.0))
            for c in range(NT):
                dve.wait_ge(produced.sem, produced.base + c + 1)
                if c:
                    dve.wait_ge(x_ready.sem, x_ready.base + c * (LEVELS - 1))
                prod = lambda n, e: K.ps[3 * e + n // 2][:, (n % 2) * 2 * P:(n % 2) * 2 * P + 2 * P] \
                    .rearrange("p (i t) -> p i t", i=2)
                for e in range(2):
                    ins = dve.tensor_copy(a_mat[:, e], prod(0, e))
                taken.up(ins)
                for e in range(2):
                    dve.tensor_tensor(t_mat[:, e], prod(0, e), wide(const(K, "level")[:, 0:P]), ALU.mult)
                    ins = dve.tensor_tensor(t_t[:, e], prod(1, e), wide(const(K, "level0_t")), ALU.mult)
                link(dve, K.dve_step, ins)
                for e in range(2):
                    dve.tensor_tensor(t_mat[:, e], t_mat[:, e], wide(const(K, "ident")), ALU.add)
                    dve.tensor_tensor(t_t[:, e], t_t[:, e], wide(const(K, "ident")), ALU.add)
                for e in range(2):
                    dve.tensor_tensor(ak_t[:, e], prod(2, e), wide(const(K, "strict_t")), ALU.mult)
                    dve.tensor_tensor(rk_t[:, e], prod(3, e), wide(const(K, "incl_t")), ALU.mult)
                    dve.tensor_tensor(rb_t[:, e], prod(4, e), wide(const(K, "incl_t")), ALU.mult)
                t_out.up(dve.tensor_copy(bonus[:, c, :], K.ps[5][:, 2 * P:2 * P + H]))
                for lev in range(1, LEVELS):
                    n = c * (LEVELS - 1) + lev - 1
                    dve.wait_ge(t_up.sem, t_up.base + n + 1)
                    dve.tensor_tensor(t_t[:, :, :, :].rearrange("p e i t -> p (e i t)"),
                                      t_t[:, :, :, :].rearrange("p e i t -> p (e i t)"), K.ps[0][:, :], ALU.add)
                    t_out.up(dve.tensor_tensor(t_mat[:, :, :, :].rearrange("p e i t -> p (e i t)"),
                                               t_mat[:, :, :, :].rearrange("p e i t -> p (e i t)"),
                                               K.ps[1][:, :], ALU.add))
                dve.wait_ge(w_up.sem, w_up.base + c + 1)
                dve.tensor_copy(w1[:, :], K.ps[2][:, 0:G])
                w_out.up(dve.tensor_copy(ta_t[:, :, :], K.ps[3][:, 0:2 * P].rearrange("p (i t) -> p i t", i=2)))
                dve.wait_ge(u_up.sem, u_up.base + c + 1)
                for e in range(2):
                    ins = dve.tensor_copy(u[:, :].rearrange("p (i e d) -> p e i d", i=2, e=2)[:, e],
                                          K.ps[4 + e][:, 0:2 * HD].rearrange("p (i d) -> p i d", i=2))
                u_out.up(ins)
                dve.wait_ge(y_up.sem, y_up.base + c + 1)
                for i in range(2):
                    ins = dve.tensor_scalar(state[:, i], state[:, i], decay_end[:, i, c:c + 1], None, ALU.mult)
                link(dve, K.dve_step, ins)
                for i in range(2):
                    ins = dve.scalar_tensor_tensor(state[:, i], K.ps[6][:, i * HD:i * HD + HD],
                                                   decay_end[:, i, c:c + 1], state[:, i], ALU.mult, ALU.add)
                s_out.up(ins)
                for e in range(2):
                    ins = dve.tensor_copy(y[:, c, :].rearrange("p (i e d) -> p e i d", i=2, e=2)[:, e],
                                          K.ps[2 + e][:, 2 * P:2 * P + 2 * HD].rearrange("p (i d) -> p i d", i=2))
                y_out.up(ins)

        @K.block.scalar
        def _(act):
            for n in range(NT * (LEVELS - 1)):
                act.wait_ge(m_up.sem, m_up.base + n + 1)
                if n:
                    act.wait_ge(t_up.sem, t_up.base + n)
                m_out.up(act.copy(m_mat[:, :, :, :].rearrange("p e i t -> p (e i t)"), K.ps[6][:, :]))
        meet(K)

        stats = arena(K, ctx, "gn_stats", [P, NT * H])
        stats2 = arena(K, ctx, "gn_stats2", [P, NT * H])
        sq = x_mat[:, :, :, :, :].rearrange("p b e i t -> p (b e i t)").rearrange("p (c f) -> p c f", c=NT)
        yh = y[:, :, :].rearrange("p c (h d) -> p (c h) d", d=HD)
        sqh = sq[:, :, :].rearrange("p c (h d) -> p (c h) d", d=HD)
        per_head = lambda ap: ap.unsqueeze(2).to_broadcast([P, NT * H, HD])
        per_tile = lambda ap: ap.unsqueeze(1).to_broadcast([P, NT, G])
        centred, squared, inv = sig["prepared"], sig["soft"], sig["exped"]

        @K.block.vector
        def _(dve):
            link(dve, K.dve_step, dve.tensor_reduce(stats[:, :], yh, AX, ALU.add))
            link(dve, K.dve_step, dve.tensor_scalar(stats[:, :], stats[:, :], 1.0 / HD, None, ALU.mult))
            centred.up(dve.tensor_tensor(yh, yh, per_head(stats[:, :]), ALU.subtract))
            dve.wait_ge(squared.sem, squared.base + 1)
            centred.up(dve.tensor_reduce(stats2[:, :], sqh, AX, ALU.add))
            dve.wait_ge(inv.sem, inv.base + 1)
            link(dve, K.dve_step, dve.tensor_tensor(yh, yh, per_head(stats2[:, :]), ALU.mult))
            link(dve, K.dve_step, dve.tensor_tensor(y[:, :, :], y[:, :, :], per_tile(row(K, "ln_g")), ALU.mult))
            dve.tensor_tensor(sqh, v_tok[:, :, :].rearrange("p c (h d) -> p (c h) d", d=HD),
                              per_head(bonus[:, :, :].rearrange("p c h -> p (c h)")), ALU.mult)
            link(dve, K.dve_step, dve.tensor_tensor(y[:, :, :], y[:, :, :], per_tile(row(K, "ln_b")), ALU.add))
            dve.tensor_tensor(y[:, :, :], y[:, :, :], sq[:, :, :], ALU.add)

        @K.block.scalar
        def _(act):
            exp_and_log(act)
            act.wait_ge(centred.sem, centred.base + 1)
            squared.up(act.activation(sqh, yh, ACT.Square))
            act.wait_ge(centred.sem, centred.base + 2)
            link(act, K.act_step, act.activation(stats2[:, :], stats2[:, :], ACT.Ln, bias=K.gn_eps[:, 0:1],
                                                 scale=1.0 / HD))
            inv.up(act.activation(stats2[:, :], stats2[:, :], ACT.Exp, scale=-0.5))
        meet(K)



def modulation_units(K, pe, n):
    for _ in range(min(n, 2 * 6 * KD - K.tiles_modulated)):
        q, t = K.modulation_first + K.tiles_modulated, K.tiles_modulated
        pe.wait_ge(K.slot_full[q % RING].sem, 16 * (q // RING + 1))
        for k in range(KD):
            mm = pe.matmul(K.ps[7][:, 2 * t:2 * t + 2], K.ring[:, q % RING, k * P:k * P + P], K.cond[:, k, :],
                           start=(k == 0), stop=(k == KD - 1))
        K.unit_used.up(mm)
        K.unit += 1
        K.tiles_modulated += 1


def finish_modulation(K):
    @K.block.tensor
    def _(pe):
        modulation_units(K, pe, 2 * 6 * KD)
    meet(K)

    @K.block.vector
    def _(dve):
        n = 2 * 6 * KD
        link(dve, K.dve_step, dve.tensor_tensor(
            K.mods[:, :, :, :].rearrange("p l n s -> p (l n) s"),
            K.ps[7][:, 0:2 * n].rearrange("p (n s) -> p n s", s=2),
            prm(K, "b_ada", 0, n).unsqueeze(2).to_broadcast([P, n, 2]), ALU.add))
        for layer in range(2):
            for n, (name, at) in enumerate((("g_mix", KD), ("g_ffn", 4 * KD))):
                for s in range(2):
                    dve.scalar_tensor_tensor(K.gains[:, layer, n, s, :], K.mods[:, layer, at:at + KD, s], 1.0,
                                             prm(K, name, layer * KD, KD), ALU.add, ALU.mult)
    meet(K)


def modulated_norm(K, layer, which, with_ctx, h, room=None):
    def part(s, c0, w):
        shift = 3 * KD * which
        return (c0, w, lambda k: K.gains[:, layer, which, s, k:k + 1],
                lambda k: K.mods[:, layer, shift + k, s:s + 1])
    rms_phase(K, K.xT, h, [part(0, 0, S)] + ([part(1, S, C)] if with_ctx else []), room)



def query_key_norms(K, layer, p, with_ctx_q, rope):
    jobs = []
    for u, name, block, width in ((DK, "dkn", "block32", 32), (NK, "nkn", "block64", 64),
                                  (DQ, "dqn", "block32", 32), (NQ, "nqn", "block64", 64)):
        for i in range(2):
            jobs.append((u + i, name, block, width, 0, S))
            if with_ctx_q or u in (DK, NK):
                jobs.append((u + i, name, block, width, S, C))
    squared, summed, inv, done = (K.signals[n] for n in ("square", "stat", "rstd", "normed"))
    with ExitStack() as ctx:
        sq = arena(K, ctx, "qk_squares", [P, 2, S])
        rs = arena(K, ctx, "qk_rstd", [P, 2, S])
        turned = arena(K, ctx, "qk_turned", [P, 4, S])

        @K.block.scalar
        def _(act):
            def square(n):
                u, _, _, _, c0, w = jobs[n]
                if n >= 2:
                    act.wait_ge(summed.sem, summed.base + n - 1)
                squared.up(act.activation(sq[:, n % 2, 0:w], p[:, u, c0:c0 + w], ACT.Square))

            def root(n):
                u, _, _, width, c0, w = jobs[n]
                act.wait_ge(summed.sem, summed.base + n + 1)
                if n >= 2:
                    act.wait_ge(done.sem, done.base + n - 1)
                link(act, K.act_step, act.activation(rs[:, n % 2, 0:w], K.ps[n % 2][:, 0:w], ACT.Ln,
                                                     bias=K.eps[:, 0:1], scale=1.0 / width))
                inv.up(act.activation(rs[:, n % 2, 0:w], rs[:, n % 2, 0:w], ACT.Exp, scale=-0.5))

            exp_and_log(act)
            for n in range(len(jobs) + 1):
                if n < len(jobs):
                    square(n)
                if n >= 1:
                    root(n - 1)

        @K.block.tensor
        def _(pe):
            for n, (u, _, block, _, c0, w) in enumerate(jobs):
                pe.wait_ge(squared.sem, squared.base + n + 1)
                if n >= 2:
                    pe.wait_ge(inv.sem, inv.base + n - 1)
                summed.up(pe.matmul(K.ps[n % 2][:, 0:w], const(K, block), sq[:, n % 2, 0:w],
                                    start=True, stop=True))

        @K.block.vector
        def _(dve):
            for n, (u, name, _, _, c0, w) in enumerate(jobs):
                dve.wait_ge(inv.sem, inv.base + n + 1)
                done.up(dve.scalar_tensor_tensor(p[:, u, c0:c0 + w], p[:, u, c0:c0 + w], prm(K, name, layer),
                                                 rs[:, n % 2, 0:w], ALU.mult, ALU.mult))
        meet(K)

        @K.block.tensor
        def _(pe):
            for n, u in enumerate((DK, DK + 1, DQ, DQ + 1)):
                summed.up(pe.matmul(K.ps[n][:, :], const(K, "rope_swap"), p[:, u, 0:S], start=True, stop=True))

        @K.block.vector
        def _(dve):
            for n, u in enumerate((DK, DK + 1, DQ, DQ + 1)):
                dve.wait_ge(summed.sem, summed.base + n + 1)
                dve.tensor_tensor(p[:, u, 0:S], p[:, u, 0:S], rope[:, 0], ALU.mult)
                link(dve, K.dve_step, dve.tensor_tensor(turned[:, n], K.ps[n][:, :], rope[:, 1], ALU.mult))
                dve.tensor_tensor(p[:, u, 0:S], p[:, u, 0:S], turned[:, n], ALU.add)
        meet(K)



def fourier(K, p, dft, parts):
    first_up, first_out, second_up, put = (K.signals[n] for n in ("scored", "exped", "mixed", "put"))
    jobs = [(i, c0, w) for c0, w in parts for i in range(2)]
    with ExitStack() as ctx:
        z = arena(K, ctx, "fourier_z", [P, 2, NT, 2 * P])

        @K.block.tensor
        def _(pe):
            def features(n):
                i, c0, w = jobs[n]
                for t in range(w // P):
                    if n:
                        pe.wait_ge(first_out.sem, first_out.base + 2 * n)
                    at = t * 2 * P if w == S else t * S
                    mm = pe.matmul(K.psum[:, at:at + 2 * P], p[:, FO + i, c0 + t * P:c0 + t * P + P],
                                   const(K, "dft64"), start=True, stop=True)
                first_up.up(mm)

            def tokens(n):
                i, c0, w = jobs[n]
                pe.wait_ge(first_out.sem, first_out.base + 2 * (n + 1))
                if n >= 2:
                    pe.wait_ge(put.sem, put.base + n - 1)
                for t in range(w // P):
                    for q in range(2):
                        mm = pe.matmul(K.ps[2 + n % 2][:, 0:w], z[:, n % 2, t, q * P:q * P + P],
                                       dft[:, q, t, 0:S:S // w], start=(t == 0 and q == 0),
                                       stop=(t == w // P - 1 and q == 1))
                second_up.up(mm)

            for n in range(len(jobs) + 1):
                if n < len(jobs):
                    features(n)
                if n:
                    tokens(n - 1)

        half = lambda buf, n, q, w: buf[:, n % 2, q * w // P // 2:(q + 1) * w // P // 2, :]
        src = lambda q, w: K.psum[:, q * S:q * S + w].rearrange("p (t f) -> p t f", f=2 * P) if w == S \
            else K.psum[:, q * S:q * S + 2 * P].unsqueeze(1)

        def first(eng, q, op):
            for n, (i, c0, w) in enumerate(jobs):
                eng.wait_ge(first_up.sem, first_up.base + n + 1)
                if n >= 2:
                    eng.wait_ge(second_up.sem, second_up.base + n - 1)
                first_out.up(op(half(z, n, q, w), src(q, w)))
                if q and n:
                    last(eng, n - 1)
            if q:
                last(eng, len(jobs) - 1)

        def last(act, n):
            i, c0, w = jobs[n]
            act.wait_ge(second_up.sem, second_up.base + n + 1)
            put.up(act.activation(K.yT[:, i, c0:c0 + w], K.ps[2 + n % 2][:, 0:w], ACT.Identity,
                                  scale=float((w * HD) ** -0.5)))

        @K.block.vector
        def _(dve):
            first(dve, 0, dve.tensor_copy)

        @K.block.scalar
        def _(act):
            first(act, 1, act.copy)
        meet(K)


def differential_attention(K, layer, p, v, y, tiles, key_tiles, key0):
    with ExitStack() as ctx:
        neg_lam = arena(K, ctx, "neg_lam", [P, 4])
        prod = arena(K, ctx, "lam_products", [P, 2, 32])
        summed, exped = K.signals["prepared"], K.signals["soft"]
        l4 = row(K, "lam4", layer * 128, 128).rearrange("p (a d) -> p a d", a=4)

        @K.block.vector
        def _(dve):
            link(dve, K.dve_step, dve.tensor_tensor(prod[:, :, :], l4[:, 0:4:2], l4[:, 1:4:2], ALU.mult))
            summed.up(dve.tensor_reduce(neg_lam[:, 0:2], prod[:, :, :], AX, ALU.add))
            dve.wait_ge(exped.sem, exped.base + 1)
            link(dve, K.dve_step, dve.tensor_tensor(neg_lam[:, 2:3], neg_lam[:, 1:2], neg_lam[:, 0:1], ALU.subtract))
            dve.tensor_scalar(neg_lam[:, 3:4], neg_lam[:, 2:3], -lambda_init(layer), None, ALU.add)

        @K.block.scalar
        def _(act):
            act.wait_ge(summed.sem, summed.base + 1)
            exped.up(act.activation(neg_lam[:, 0:2], neg_lam[:, 0:2], ACT.Exp))
        meet(K)

        kw = len(key_tiles) * P
        items = []
        for h in range(H):
            for m in tiles:
                scores = []
                for c in range(2):
                    first_row = 64 * (h % 2) + 32 * c
                    r, i = slice(first_row, first_row + 32), h // 2
                    q = p[r, DQ + i, m * P:m * P + P]
                    scores.append([[(q, p[r, DK + i, key0 + a:key0 + min(a + S, kw)], a, min(S, kw - a))]
                                   for a in range(0, kw, S)])
                items.append(dict(scores=scores, kw=kw, tiles=key_tiles, bias=None,
                                  v=lambda t, h=h: v[:, t, h * HD:h * HD + HD],
                                  out=y[:, m, h * HD:h * HD + HD]))
        softmax_attention(K, items, 1.0, neg_lam[:, 3:4])


def neighbourhood_attention(K, layer, p, v, y, tiles, key_tiles, key0, bias):
    kw = len(key_tiles) * P
    items = []
    for h in range(H):
        r, i = slice(64 * (h % 2), 64 * (h % 2) + HD), h // 2
        for m in tiles:
            q = p[r, NQ + i, m * P:m * P + P]
            first = 7 - 2 * m
            b = None if bias is None else bias[:, h, first:first + 8, :].rearrange("p a k -> p (a k)")
            items.append(dict(
                scores=[[[(q, p[r, NK + i, key0 + a:key0 + min(a + S, kw)], a, min(S, kw - a))]
                         for a in range(0, kw, S)]],
                kw=kw, tiles=key_tiles, bias=b, v=lambda t, h=h: v[:, t, G + h * HD:G + h * HD + HD],
                out=y[:, m, h * HD:h * HD + HD]))
    softmax_attention(K, items, 1.0)


def head_norm(K, src, gain, tiles, factor=1.0):
    n = len(tiles)
    m = slice(tiles[0], tiles[-1] + 1)
    squared, summed, inv = (K.signals[x] for x in ("square", "stat", "rstd"))
    with ExitStack() as ctx:
        sq = arena(K, ctx, "head_squares", [P, n, G])
        st = arena(K, ctx, "head_stats", [P, n, H])
        heads = lambda ap: ap.rearrange("p m (h d) -> p m h d", d=HD)

        @K.block.scalar
        def _(act):
            exp_and_log(act)
            squared.up(act.activation(sq[:, :, :], src[:, m, :], ACT.Square))
            act.wait_ge(summed.sem, summed.base + 1)
            link(act, K.act_step, act.activation(st[:, :, :], st[:, :, :], ACT.Ln, bias=K.eps[:, 0:1],
                                                 scale=1.0 / HD))
            inv.up(act.activation(st[:, :, :], st[:, :, :], ACT.Exp, scale=-0.5))

        @K.block.vector
        def _(dve):
            dve.wait_ge(squared.sem, squared.base + 1)
            summed.up(dve.tensor_reduce(st[:, :, :], heads(sq[:, :, :]), AX, ALU.add))
            dve.wait_ge(inv.sem, inv.base + 1)
            for t in range(n):
                ins = dve.tensor_tensor(
                    src[:, tiles[0] + t, :].rearrange("p (h d) -> p h d", d=HD),
                    src[:, tiles[0] + t, :].rearrange("p (h d) -> p h d", d=HD),
                    st[:, t, :].unsqueeze(2).to_broadcast([P, H, HD]), ALU.mult)
            link(dve, K.dve_step, ins)
            for t in range(n):
                dve.scalar_tensor_tensor(src[:, tiles[0] + t, :], src[:, tiles[0] + t, :], factor, gain,
                                         ALU.mult, ALU.mult)
        meet(K)


def chunk_gmlp(K, layer, uv, y, tiles, ws):
    mixed, put = K.signals["mixed"], K.signals["put"]

    @K.block.tensor
    def _(pe):
        for n, m in enumerate(tiles):
            for h in range(H):
                mm = pe.matmul(K.ps[n][:, h * HD:h * HD + HD], ws[:, h], uv[:, m, G + h * HD:G + h * HD + HD],
                               start=True, stop=True)
            mixed.up(mm)

    @K.block.vector
    def _(dve):
        for n, m in enumerate(tiles):
            dve.wait_ge(mixed.sem, mixed.base + n + 1)
            for h in range(H):
                c = slice(h * HD, h * HD + HD)
                ins = dve.scalar_tensor_tensor(y[:, m, c], K.ps[n][:, c], prm(K, "gmlp_b", layer * H + h),
                                               uv[:, m, c], ALU.add, ALU.mult)
    meet(K)



def feed_forward(K, layer, with_ctx):
    W = S + C if with_ctx else S
    conv, gate_done, emptied = K.signals["conv"], K.signals["silu"], K.signals["main_free"]
    ZW = S + C + 4
    spans = [(0, S, 1)] + ([(S, C, S + 3)] if with_ctx else [])
    first = K.unit
    wc = PRM["conv_w2"][0] + layer * 3 * 44
    bc = PRM["conv_b2"][0] + layer * 44
    TURNS = 2 * KF // RING
    with ExitStack() as ctx:
        h = arena_pair(K, ctx, "h", [P, KD, S + C])
        modulated_norm(K, layer, 1, with_ctx, h)
        hid = arena(K, ctx, "hidden", [P, KF, S + C])
        inner = ctx.enter_context(ExitStack())
        z = arena(K, inner, "z", [P, 4, ZW])
        t = arena(K, inner, "conv_out", [P, 4, S + C])

        @K.block.gpsimd
        def _(pool):
            pool.memset(z[:, :, :], 0.0)
        meet(K)

        @K.block.tensor
        def _(pe):
            def unit(i, j):
                q = first + j
                pe.wait_ge(K.unit_used.sem, i * RING + (q + 1))
                pe.wait_ge(emptied.sem, i * RING + (j + emptied.base + 1))
                for k in range(KD):
                    mm = three_products(pe, K.ps[j][:, :], weights(K, q, k), (h[0][:, k, 0:S], h[1][:, k, 0:S]),
                                        k == 0, k == KD - 1)
                    if with_ctx:
                        mm = three_products(pe, K.ps[4 + j][:, 0:C], weights(K, q, k),
                                            (h[0][:, k, S:S + C], h[1][:, k, S:S + C]), k == 0, k == KD - 1)
                mm.then_inc(K.unit_done.sem, 1)
            in_turns(pe, 2 * KF, unit)

        @K.block.scalar
        def _(act):
            def empty(i, j):
                act.wait_ge(K.unit_done.sem, i * RING + (j + K.unit_done.base + 1))
                act.wait_ge(conv.sem, i * RING + (j + conv.base + 1))
                for n, (c0, w, z0) in enumerate(spans):
                    ins = act.copy(z[:, j, z0:z0 + w], K.ps[4 * n + j][:, 0:w])
                ins.then_inc(emptied.sem, 1)
                if j % 2:
                    act.wait_ge(conv.sem, i * RING + (j + conv.base + RING))
                    act.activation(t[:, j - 1, 0:W], t[:, j - 1, 0:W], ACT.Silu).then_inc(gate_done.sem, 1)

            def unit(i, j):
                split_high(K, act, i, j + 1)
                empty(i, j)
            act.sem_inc(emptied.sem, RING)
            split_high(K, act, 0, 0, guard=False)
            in_turns(act, 2 * KF - 1, unit)
            empty(*divmod(2 * KF - 1, RING))

        @K.block.vector
        def _(dve):
            def convolve(i, j):
                tile = (j % 2) * KF + j // 2
                column = lambda c: K.prm[:, ds(i * 2 + (c + tile), 1)]
                dve.wait_ge(emptied.sem, i * RING + (j + emptied.base + RING + 1))
                if j % 2 == 0:
                    dve.wait_ge(K.conv_step.sem, i * STEPS + (K.conv_step.base + 1))
                at = 1 + 5 * (j // 2) + 2 * (j % 2)
                for tap in range(3):
                    if tap:
                        dve.wait_ge(K.conv_step.sem, i * STEPS + (K.conv_step.base + at + tap))
                    for s, (c0, w, z0) in enumerate(spans):
                        to, src = t[:, j, c0:c0 + w], z[:, j, z0 - 1 + tap:z0 - 1 + tap + w]
                        if tap == 0:
                            ins = dve.tensor_scalar(to, src, column(wc), column(bc), ALU.mult, ALU.add)
                        else:
                            ins = dve.scalar_tensor_tensor(to, src, column(wc + 44 * tap), to, ALU.mult, ALU.add)
                    ins.then_inc(conv.sem if tap == 2 else K.conv_step.sem, 1)
                if j % 2:
                    dve.wait_ge(conv.sem, i * RING + (j + conv.base + RING + 1))
                    dve.wait_ge(gate_done.sem, i * 2 + (j // 2 + gate_done.base + 1))
                    dve.tensor_tensor(hid[:, ds(i * 2 + j // 2, 1), 0:W].rearrange("p a w -> p (a w)"),
                                      t[:, j - 1, 0:W], t[:, j, 0:W], ALU.mult).then_inc(K.conv_step.sem, 1)

            def unit(i, j):
                split_low(K, dve, i, j + 1)
                convolve(i, j)
            STEPS = 10
            dve.sem_inc(conv.sem, RING)
            dve.sem_inc(K.conv_step.sem, 1)
            split_low(K, dve, 0, 0)
            in_turns(dve, 2 * KF - 1, unit)
            convolve(*divmod(2 * KF - 1, RING))

        K.conv_step.n += TURNS * 10 + 1
        conv.n += RING + 2 * KF
        gate_done.n += KF
        emptied.n += RING + 2 * KF
        for s in (K.unit_used, K.unit_done, K.high_split):
            s.n += 2 * KF
        K.unit += 2 * KF
        meet(K)
        inner.close()

        put, ctx_put, high_ready, low_ready = (K.signals[n] for n in ("put", "ctx_put", "high_ready", "low_ready"))
        mv = arena_pair(K, ctx, "hidden_part", [P, 2, 2, S + C])
        first, half = K.unit, KF // 2

        def hidden(n):
            return hid[:, ds(n * 2, 2), 0:W]

        @K.block.tensor
        def _(pe):
            def unit(i, j, n=None):
                q = first + j
                n = j if n is None else n
                pe.wait_ge(K.unit_used.sem, i * RING + (q + 1))
                pe.wait_ge(low_ready.sem, i * RING + (low_ready.base + j + 1))
                for kk in range(2):
                    start, stop = n % half == 0 and kk == 0, n % half == half - 1 and kk == 1
                    for o in range(4):
                        w = weights(K, q, kk * 4 + o)
                        mm = three_products(pe, K.ps[o][:, :], w, tuple(m[:, q % 2, kk, 0:S] for m in mv),
                                            start, stop)
                        if with_ctx:
                            mm = three_products(pe, K.ps[4 + o][:, 0:C], w,
                                                tuple(m[:, q % 2, kk, S:S + C] for m in mv), start, stop)
                mm.then_inc(K.unit_done.sem, 1)

            for a in (0, half):
                if a:
                    pe.wait_ge(put.sem, put.base + 1)
                    if with_ctx:
                        pe.wait_ge(ctx_put.sem, ctx_put.base + 1)
                unit(0, a)
                with pe.Fori(0, 2) as i:
                    for j in range(RING):
                        unit(i, a + 1 + j, 1)
                unit(0, a + 9)
                unit(0, a + 10)

        @K.block.scalar
        def _(act):
            def each(i, j, n):
                q = first + j
                act.wait_ge(K.slot_full[q % RING].sem, i * 16 + 16 * (q // RING + 1))
                act.wait_ge(K.unit_done.sem, i * RING + (K.unit_done.base + j - 1))
                act.copy(K.w_high[:, q % 2], K.ring[:, q % RING]).then_inc(K.high_split.sem, 1)
                act.copy(mv[0][:, q % 2, :, 0:W], hidden(n)).then_inc(high_ready.sem, 1)
            for a in (0, half):
                with act.Fori(0, 2) as i:
                    for j in range(RING):
                        each(i, a + j, i * RING + j)
                for j in range(8, half):
                    each(0, a + j, j)

        @K.block.vector
        def _(dve):
            def each(i, j, n):
                q = first + j
                dve.wait_ge(K.high_split.sem, i * RING + (K.high_split.base + j + 1))
                dve.tensor_tensor(K.w_low[:, q % 2], K.ring[:, q % RING], K.w_high[:, q % 2].bitcast(F32),
                                  ALU.subtract).then_inc(K.unit_used.sem, 1)
                dve.wait_ge(high_ready.sem, i * RING + (high_ready.base + j + 1))
                dve.tensor_tensor(mv[1][:, q % 2, :, 0:W], hidden(n), mv[0][:, q % 2, :, 0:W].bitcast(F32),
                                  ALU.subtract).then_inc(low_ready.sem, 1)

            def add(a):
                dve.wait_ge(K.unit_done.sem, K.unit_done.base + half * (a + 1))
                for o in range(4):
                    n = 4 * a + o
                    ins = dve.scalar_tensor_tensor(K.xT[:, n, 0:S], K.ps[o][:, :], K.mods[:, layer, 5 * KD + n, 0:1],
                                                   K.xT[:, n, 0:S], ALU.mult, ALU.add)
                put.up(ins)
                for o in range(4 if with_ctx else 0):
                    n = 4 * a + o
                    ins = dve.scalar_tensor_tensor(K.xT[:, n, S:S + C], K.ps[4 + o][:, 0:C],
                                                   K.mods[:, layer, 5 * KD + n, 1:2], K.xT[:, n, S:S + C],
                                                   ALU.mult, ALU.add)
                if with_ctx:
                    ctx_put.up(ins)

            for a in (0, half):
                with dve.Fori(0, 2) as i:
                    for j in range(RING):
                        each(i, a + j, i * RING + j)
                for j in range(8, half):
                    each(0, a + j, j)
                add(a // half)
        for s in (K.unit_used, K.unit_done, K.high_split, high_ready, low_ready):
            s.n += KF
        K.unit += KF
        meet(K)



SIGNALS = ("met", "act_step", "dve_step", "conv_step", "unit_used", "loaded_late", "unit_done", "high_split",
           "high_ready", "low_ready", "square", "stat", "rstd", "normed", "main_free", "ctx_free",
           "scored", "max_ready", "exped", "weighted", "turned_up", "turned_out", "mixed", "put",
           "ctx_put", "prepared", "soft", "summed", "produced", "taken", "x_ready", "x_used",
           "m_up", "m_out", "t_up", "t_out", "w_up", "w_out", "u_up", "u_out", "y_up", "y_out",
           "s_out", "tile_done", "conv", "silu", "pair_done", "loaded", "stored")

N_UNITS = N1F + N1T + KD + 2 * 6 * KD + 2 * (N2F + 8 + KD + 44 + 22)


def build(nc, dram):
    with ExitStack() as ctx:
        K = Kit()
        K.nc, K.serial, K.unit = nc, 0, 0
        K.signals = {n: Signal(nc, ctx, n) for n in SIGNALS}
        K.met, K.unit_used, K.loaded_late = (K.signals[n] for n in ("met", "unit_used", "loaded_late"))
        K.unit_done, K.high_split = K.signals["unit_done"], K.signals["high_split"]
        K.act_step, K.dve_step, K.conv_step = (K.signals[n] for n in ("act_step", "dve_step", "conv_step"))
        K.slot_full = [Signal(nc, ctx, f"slot_full{j}") for j in range(RING)]
        K.w_units, K.lru_w_dram, K.lora_dram = dram["w_units"], dram["lru_w"], dram["lora"]
        sb = lambda name, shape: ctx.enter_context(nc.sbuf_tensor(name, shape, F32))
        K.psum = ctx.enter_context(nc.psum_tensor("psum", [P, 8 * S], F32))
        K.ps = [K.psum[:, j * S:(j + 1) * S] for j in range(8)]
        K.ring = sb("ring", [P, RING, KD * P])
        K.xT = sb("xT", [P, KD, S + C])
        K.w_high, K.w_low = arena_pair(K, ctx, "unit", [P, 2, KD * P])
        K.cst = sb("constants", [P, width(CONST)])
        K.prm = sb("parameters", [P, NPRM])
        K.rows = sb("row_parameters", [P, NROW - ROWS_FIRST])
        K.mods = sb("mods", [P, 2, 6 * KD, 2])
        K.gains = sb("gains", [P, 2, 2, 2, KD])
        K.cond = sb("cond", [P, KD, 2])
        scal = sb("scalars", [P, 8])
        K.eps, K.gn_eps, K.one, K.half, K.minus_half = (scal[:, j:j + 1] for j in range(5))
        first = ctx.enter_context(ExitStack())
        K.cst_first = arena(K, first, "constants_first", [P, width(CONST_FIRST)])
        K.rows_first = arena(K, first, "row_parameters_first", [P, ROWS_FIRST])
        K.block = ctx.enter_context(nc.Block())
        loaded = K.signals["loaded"]

        @K.block.scalar
        def _(act):
            for dst, src in ((K.xT[:, :, 0:S], dram["x"]), (K.cst[:, :], dram["constants"]),
                             (K.cst_first[:, :], dram["constants_first"]),
                             (K.prm[:, :], dram["parameters"]), (K.rows[:, :], dram["row_parameters"][:, ROWS_FIRST:]),
                             (K.rows_first[:, :], dram["row_parameters"][:, 0:ROWS_FIRST]),
                             (K.xT[:, :, S:S + C], dram["ctx"])):
                loaded.up(act.dma_start(dst, src), 16)
            act.wait_ge(loaded.sem, loaded.n)

        @K.block.gpsimd
        def _(pool):
            for at, value in ((K.eps, EPS), (K.gn_eps, GN_EPS), (K.one, 1.0), (K.half, HALF),
                              (K.minus_half, -HALF)):
                pool.memset(at, value)
        stream_weights(K, N_UNITS)

        @K.block.tensor
        def _(pe):
            pe.sem_inc(K.unit_done.sem, 1)
        K.unit_done.n = 1
        meet(K)

        first_block(K)
        first.close()
        second_block(K, dram)

        @K.block.sync
        def _(sp):
            sp.wait_ge(K.met.sem, K.met.n)
            sp.dma_start(dram["out"], K.xT[:, :, 0:S]).then_inc(K.signals["stored"].sem, 16)
            sp.wait_ge(K.signals["stored"].sem, 16)


def first_block(K):
    @K.block.scalar
    def _(act):
        act.activation(K.cond[:, :, :], prm(K, "c", 0, 2 * KD).rearrange("p (s k) -> p k s", s=2), ACT.Silu)
    outer = ExitStack()
    with ExitStack() as ctx:
        K.yT = arena(K, outer, "yT", [P, KD, S])
        p = arena(K, ctx, "p", [P, N1F, PAD + S])
        v = arena(K, ctx, "v", [P, NT, 2 * G])
        inner = ctx.enter_context(ExitStack())
        h = arena_pair(K, inner, "h", [P, KD, S])
        rms_phase(K, K.xT, h, [(0, S, lambda k: prm(K, "norm_g", k), None)])

        @K.block.gpsimd
        def _(pool):
            pool.memset(p[:, :, 0:PAD], 0.0)
        project(K, N1F, False,
                lambda dve, u, bank: dve.tensor_copy(at_unit(p, u, PAD, PAD + S), bank[:, :]), None, h)
        project_tokens(K, v, NT, h)
        inner.close()
        y = arena(K, ctx, "y", [P, NT, G])

        @K.block.scalar
        def _(act):
            for u in range(GATE, GATE + 8):
                act.activation(p[:, u, PAD:], p[:, u, PAD:], ACT.Silu)
        meet(K)

        K.modulation_first, K.tiles_modulated = K.unit, 0

        def gated(group):
            return lambda dve, u, psum: dve.tensor_tensor(K.yT[:, 2 * group + u, 0:S], psum,
                                                          p[:, GATE + 2 * group + u, PAD:], ALU.mult)
        tiles = range(NT)
        forgetting_attention(K, p, v[:, :, 0:G], y)
        to_feature_major(K, y, tiles, gated(0))
        stick_breaking_attention(K, p, v[:, :, G:2 * G], y)
        to_feature_major(K, y, tiles, gated(1))
        rg_lru(K, p, lambda dve, i, h: dve.tensor_tensor(K.yT[:, 6 + i, 0:S], h, p[:, GATE + 6 + i, PAD:],
                                                         ALU.mult))
        rwkv(K, p, y)
        to_feature_major(K, y, tiles, gated(2))
    finish_modulation(K)

    def add_to_x(dve, u, bank):
        x = at_unit(K.xT, u, 0, S)
        return dve.tensor_tensor(x, x, bank[:, :], ALU.add)
    with outer, ExitStack() as ctx:
        parts = arena_pair(K, ctx, "y", [P, KD, S])
        split_phase(K, K.yT, parts, S)
        project(K, KD, False, add_to_x, None, parts)
    rms_phase(K, K.xT, K.xT, [(0, S, lambda k: prm(K, "final_g", k), None)])


def at_unit(buf, u, a, b):
    if isinstance(u, int):
        return buf[:, u, a:b]
    return buf[:, ds(u, 1), a:b].rearrange("p a w -> p (a w)")


def second_block(K, dram):
    @K.block.vector
    def _(dve):
        dve.tensor_scalar(prm(K, "dqn", 0, 2), prm(K, "dqn", 0, 2), 32 ** -0.5, None, ALU.mult)
        dve.tensor_scalar(prm(K, "nqn", 0, 2), prm(K, "nqn", 0, 2), HD ** -0.5, None, ALU.mult)
    meet(K)
    for layer in range(2):
        ctx_out = layer == 0
        outer = ExitStack()
        K.yT = arena(K, outer, "yT", [P, KD, S + C])
        mixers(K, layer, ctx_out, dram)

        def lat(dve, u, bank):
            x = at_unit(K.xT, u, 0, S)
            m = K.mods[:, layer, ds(u + 2 * KD, 1), 0:1].rearrange("p a b -> p (a b)")
            return dve.scalar_tensor_tensor(x, bank[:, :], m, x, ALU.mult, ALU.add)

        def cnt(act, u, bank):
            m = K.mods[:, layer, ds(u + 2 * KD, 1), 1:2].rearrange("p a b -> p (a b)")
            return act.activation(at_unit(K.ctx_gain, u, 0, C), bank[:, 0:C], ACT.Identity, scale=m)
        with outer, ExitStack() as ctx:
            parts = arena_pair(K, ctx, "y", [P, KD, S + C])
            split_phase(K, K.yT, parts, S + C if ctx_out else S)
            if ctx_out:
                K.ctx_gain = arena(K, ctx, "ctx_gain", [P, KD, C])
            project(K, KD, ctx_out, lat, cnt, parts)
            if ctx_out:
                @K.block.vector
                def _(dve):
                    dve.tensor_tensor(K.xT[:, :, S:S + C], K.xT[:, :, S:S + C], K.ctx_gain[:, :, :], ALU.add)
                meet(K)
        feed_forward(K, layer, ctx_out)


def mixers(K, layer, ctx_out, dram):
    late = K.loaded_late
    lat_tiles, ctx_tiles, all_tiles = range(NT), range(NT, MT), range(MT)
    with ExitStack() as ctx:
        p = arena(K, ctx, "p", [P, N2F, S + C])
        v = arena(K, ctx, "v", [P, MT, 4 * P])
        uv = arena(K, ctx, "uv", [P, MT, 4 * P])
        y = arena(K, ctx, "y", [P, MT, G])
        inner = ctx.enter_context(ExitStack())
        h = arena_pair(K, inner, "h", [P, KD, S + C])
        modulated_norm(K, layer, 0, True, h, (K.yT[:, :, 0:S], y[:, 0:3, :].rearrange("p m f -> p (m f)")))

        def feature(first):
            return (lambda dve, u, bank: dve.tensor_copy(at_unit(p, u + first, 0, S), bank[:, :]),
                    lambda act, u, bank: act.copy(at_unit(p, u + first, S, S + C), bank[:, 0:C]))

        project(K, 4, True, *feature(0), h)
        project(K, 6, ctx_out, *feature(4), h)
        project_tokens(K, v, MT, h)
        project_tokens(K, uv, MT if ctx_out else NT, h)
        inner.close()

        tiles = all_tiles if ctx_out else lat_tiles
        with ExitStack() as inner:
            dft = arena(K, inner, "dft", [P, 2, NT, S])

            @K.block.gpsimd
            def _(pool):
                late.up(pool.dma_start(dft[:, :, :, :], dram["dft"]), 16)
                pool.wait_ge(late.sem, late.n)

            @K.block.scalar
            def _(act):
                act.activation(uv[:, 0:len(tiles), :], uv[:, 0:len(tiles), :], ACT.Gelu_apprx_tanh)
            meet(K)
            fourier(K, p, dft, [(0, S)] + ([(S, C)] if ctx_out else []))

        def put_unit(first, c0):
            return lambda dve, u, psum: dve.tensor_copy(K.yT[:, first + u, c0:c0 + psum.shape[1]], psum)

        def turn_all(first):
            to_feature_major(K, y, lat_tiles, put_unit(first, 0))
            if ctx_out:
                to_feature_major(K, y, ctx_tiles, put_unit(first, S))

        with ExitStack() as inner:
            ws = arena(K, inner, "gmlp_ws", [P, H, P])

            @K.block.gpsimd
            def _(pool):
                late.up(pool.dma_start(ws[:, :, :], dram["gmlp_ws"][:, layer]), 16)
                pool.wait_ge(late.sem, late.n)
            head_norm(K, uv[:, :, G:2 * G], row(K, "gmlp_g", layer * G), tiles)
            chunk_gmlp(K, layer, uv, y, tiles, ws)
            turn_all(6)
        with ExitStack() as inner:
            rope = arena(K, inner, "rope", [P, 2, S])

            @K.block.gpsimd
            def _(pool):
                late.up(pool.dma_start(rope[:, :, :], dram["rope"]), 16)
                pool.wait_ge(late.sem, late.n)
            meet(K)
            query_key_norms(K, layer, p, ctx_out, rope)
        differential_attention(K, layer, p, v, y, lat_tiles, all_tiles, 0)
        if ctx_out:
            differential_attention(K, layer, p, v, y, ctx_tiles, ctx_tiles, S)
        head_norm(K, y, row(K, "subln", layer * G), tiles, 1.0 - lambda_init(layer))
        turn_all(2)
        with ExitStack() as inner:
            bias = arena(K, inner, "bias", [P, H, 16, HD])

            @K.block.gpsimd
            def _(pool):
                late.up(pool.dma_start(bias[:, :, :, :], dram["na_bias"][:, layer]), 16)
                pool.wait_ge(late.sem, late.n)
                for h in range(H):
                    pool.tensor_tensor(bias[:, h], bias[:, h],
                                       const(K, "window").unsqueeze(1).to_broadcast([P, 16, HD]), ALU.add)
            meet(K)
            neighbourhood_attention(K, layer, p, v, y, lat_tiles, all_tiles, 0, bias)
        if ctx_out:
            neighbourhood_attention(K, layer, p, v, y, ctx_tiles, ctx_tiles, S, None)
        turn_all(4)



def width(table):
    return max(b for _, b in table.values())


def constant_tables():
    tables = [np.zeros((P, width(x)), np.float32) for x in (CONST, CONST_FIRST)]
    i, j = np.arange(P)[:, None], np.arange(P)[None, :]

    def put(name, value):
        a, b = CONST.get(name) or CONST_FIRST[name]
        tables[name not in CONST][:, a:b] = value
    put("ident", i == j)
    put("ones", 1.0)
    put("block32", i // 32 == j // 32)
    put("block64", i // 64 == j // 64)
    put("tri_ge", i >= j)
    put("causal_add", np.where(j > i, NEG, 0.0))
    put("stick_big", np.where(i >= j, -NEG, 0.0))
    put("strict_t", i < j)
    put("incl_t", i <= j)
    put("rope_swap", np.where(i // 32 == j // 32, np.where(i == j + 16, -1.0, np.where(i == j - 16, 1.0, 0.0)), 0.0))
    head_row = np.zeros((P, H, P))
    for h in range(H):
        head_row[64 + h, h] = HD ** 0.5
    put("head_row", head_row.reshape(P, -1))
    put("head_pair", i // 64 == np.arange(2)[None, :])
    level = np.zeros((P, LEVELS, P))
    for n in range(LEVELS):
        level[:, n] = (i // 2 ** n == j // 2 ** n + 1) & (i // 2 ** n % 2 == 1)
    put("level", level.reshape(P, -1))
    put("level0_t", level[:, 0].T)
    q, k = i % HD, np.arange(HD)[None, :]
    c0 = np.clip(q - 8, 0, HD - 16)
    put("window", np.where((k >= c0) & (k < c0 + 16), 0.0, NEG))
    put("chunk_keep", np.arange(S)[None, :] % CH != 0)
    put("keep_all", 1.0)
    d = np.arange(HD)
    angle = 2 * np.pi * np.outer(d, d) / HD
    two = lambda m: np.kron(np.eye(2), m)
    put("dft64", np.concatenate([two(np.cos(angle)), -two(np.sin(angle))], axis=1))
    return tables


def dft_table():
    n = np.arange(S)
    angle = 2 * np.pi * (np.outer(n, n) % S) / S
    both = np.stack([np.cos(angle), np.sin(angle)])
    return np.ascontiguousarray(both.reshape(2, NT, P, S).transpose(2, 0, 1, 3)).astype(np.float32)


def rope_table():
    freqs = 10000.0 ** (-np.arange(8, dtype=np.float32) / 8)
    t = np.arange(S)
    angle = np.concatenate([(t // 64)[None, :] * freqs[:, None], (t % 64)[None, :] * freqs[:, None]])
    full = np.tile(angle, (8, 1))
    return np.stack([np.cos(full), np.sin(full)], axis=1).astype(np.float32)



def tile_units(w):
    n = w.shape[1] // P
    return w.reshape(KD, P, n, P).transpose(2, 1, 0, 3).reshape(n, P, KD * P)


def token_units(w):
    return w.reshape(4, 2, P, S).transpose(0, 2, 1, 3).reshape(4, P, 2 * S)


def down_units(w):
    w = w.reshape(KF // 2, 2, P, 2, 4, P)
    return w.transpose(3, 0, 2, 1, 4, 5).reshape(KF, P, 8 * P)


def lay_out(a):
    cols = lambda w, at, n: w[:, at:at + n]
    g = G
    w1 = a["w_in"][0]
    at = {n: o for n, o in zip(("fq", "fk", "fv", "fg", "ff", "sq", "sk", "sv", "sg", "rw", "rg", "lx", "lg"),
                               np.cumsum([0, g, g, g, g, H, g, g, g, g, 3 * g + 2 * R, g, g]))}
    rw = at["rw"]
    first = [cols(w1, at[n], g) for n in ("fq", "fk", "sq", "sk")]
    first += [cols(w1, rw, 3 * g), cols(w1, rw + 3 * g, 2 * R), cols(w1, at["ff"], H),
              np.zeros((D, P - 2 * R - H), np.float32)]
    first += [cols(w1, at[n], g) for n in ("lx", "fg", "sg", "rg", "lg", "fv", "sv")]
    first = np.concatenate(first, axis=1)
    units = [tile_units(first[:, :N1F * P]), token_units(first[:, N1F * P:])]
    units += [tile_units(a["w_ada_2"][l]) for l in range(2)] + [tile_units(a["w_out"][0])]
    for l in range(2):
        w = a["w_in_2"][l]
        order = [2, 5, 0, 1, 4, 3, 6, 7, 8]
        second = [cols(w, n * g, g) for n in order]
        units.append(tile_units(np.concatenate(second[:5], axis=1)))
        units += [token_units(np.concatenate(second[n:n + 2], axis=1)) for n in (5, 7)]
        units.append(tile_units(a["w_out_2"][l]))
        up = a["ffn_up_2"][l].reshape(D, 2, KF, P).transpose(0, 2, 1, 3).reshape(D, 2 * FF)
        units += [tile_units(up), down_units(a["ffn_down_2"][l])]
    w_units = np.concatenate(units)

    prm_table = np.zeros((P, NPRM), np.float32)

    def put(name, values, col=0):
        f = PRM[name][0] + col
        v = np.asarray(values).reshape(-1, P)
        prm_table[:, f:f + len(v)] = v.T
    for name, src in (("norm_g", "norm_g"), ("w0", "rwkv_w0"), ("a0", "rwkv_a0"), ("k_k", "rwkv_k_k"),
                      ("k_a", "rwkv_k_a"), ("r_k", "rwkv_r_k"), ("conv_w", "lru_conv_w"), ("conv_b", "lru_conv_b"),
                      ("b_a", "lru_b_a"), ("b_x", "lru_b_x"), ("lam", "lru_lambda"), ("final_g", "final_g"),
                      ("g_mix", "g_mix_2"), ("g_ffn", "g_ffn_2"), ("b_ada", "b_ada_2"),
                      ("conv_w2", "ffn_conv_2"), ("conv_b2", "ffn_conv_b_2"), ("c", "c_2")):
        put(name, a[src])
    put("c", a["c_ctx_2"], KD)
    put("mu", np.concatenate([a["rwkv_mu"][0], np.zeros(64, np.float32)]))
    prm_table[64:64 + H, PRM["b_f"][0]] = a["b_forget"][0]
    for name, src, n in (("dqn", "diff_qn_2", 4), ("dkn", "diff_kn_2", 4), ("nqn", "na_qn_2", 2), ("nkn", "na_kn_2", 2)):
        put(name, np.tile(a[src], (1, n)))
    put("gmlp_b", a["gmlp_b_2"])

    row_table = np.concatenate([a["rwkv_ln_g"][0], a["rwkv_ln_b"][0], np.tile(a["diff_subln_2"], (1, H)).ravel(),
                                a["gmlp_norm_2"].ravel(), a["diff_lam_2"].ravel()])
    row_table = np.ascontiguousarray(np.broadcast_to(row_table, (P, NROW)))

    lru_w = np.zeros((P, 4, P), np.float32)
    for n, src in enumerate(("lru_w_a", "lru_w_x")):
        for i in range(2):
            for e in range(2):
                lru_w[64 * e:64 * e + HD, 2 * n + i, 64 * e:64 * e + HD] = a[src][0, 2 * i + e]
    lora = np.concatenate([a["rwkv_w2"][0], a["rwkv_a2"][0]])

    q, k = np.arange(HD)[:, None], np.arange(HD)[None, :]
    off = k - q + 15
    rpb = a["na_rpb_2"]
    spread = np.where((off >= 0) & (off <= 30), rpb[:, :, :, np.clip(off, 0, 30)], np.float32(0))
    bias = np.zeros((2, HD, 2, H, 16, HD), np.float32)
    for e in range(2):
        bias[e, :, :, :, e:e + 15] = spread.transpose(3, 0, 1, 2, 4)
    constants, constants_first = constant_tables()
    tokens = lambda x: np.ascontiguousarray(x.reshape(-1, KD, P).transpose(2, 1, 0))
    return {
        "x": tokens(a["x"][0]), "ctx": tokens(a["ctx_2"][0]), "w_units": w_units,
        "constants": constants, "constants_first": constants_first, "parameters": prm_table, "row_parameters": row_table,
        "lru_w": lru_w.reshape(P, -1), "lora": np.ascontiguousarray(lora), "dft": dft_table(), "rope": rope_table(),
        "gmlp_ws": np.ascontiguousarray(a["gmlp_ws_2"].transpose(3, 0, 1, 2)),
        "na_bias": bias.reshape(P, 2, H, 16, HD),
    }


def kernel(**inputs):
    import concourse.bacc as bacc
    from concourse.bass_utils import run_bass_kernel_spmd

    arrays = lay_out({k: np.asarray(v) for k, v in inputs.items()})
    nc = bacc.Bacc("TRN2", target_bir_lowering=False, num_devices=1)
    dram = {n: nc.dram_tensor(f"in_{n}", v.shape, F32, kind="ExternalInput").ap() for n, v in arrays.items()}
    dram["out"] = nc.dram_tensor("out_x", (P, KD, S), F32, kind="ExternalOutput").ap()
    build(nc, dram)
    r = run_bass_kernel_spmd(nc, [{f"in_{n}": v for n, v in arrays.items()}], core_ids=[0])
    out = r.results[0]["out_x"]
    return out.transpose(2, 1, 0).reshape(1, S, D)
```

```python
from contextlib import ExitStack

import numpy as np

import concourse.bass as bass
from concourse import mybir

F32 = mybir.dt.float32
F32R = mybir.dt.float32r
ALU = mybir.AluOpType
ACT = mybir.ActivationFunctionType
AX = mybir.AxisListType.X
ds = bass.ds

P = 128
D = 1024
KD = D // P
S = 512
C = 256
NT = S // P
CT = C // P
MT = NT + CT
G = 256
H = 4
HD = 64
R = 32
FF = 2816
KF = FF // P
EPS = 1e-6
GN_EPS = 64e-5
NEG = -1e30
PAD = 4
RING = 4
CH = 128
LEVELS = 7
DECAY = float(np.exp(-0.5))
HALF = DECAY * CH / 2

FQ, FK, SQ, SK, RR, RK, RV, MISC, LX, GATE = 0, 2, 4, 6, 8, 10, 12, 14, 15, 17
N1F, N1T = 25, 4
DK, NK, FO, DQ, NQ = 0, 2, 4, 6, 8
N2F = 10
MOD_UNITS = 2 * 6 * KD
MOD_GROUPS = MOD_UNITS // 4

CONST, CONST_FIRST = {}, {}
for _table, _entries in (
        (CONST, (("ident", P), ("ones", P), ("block32", P), ("block64", P), ("rope_swap", P), ("window", HD),
                 ("dft64", 2 * P))),
        (CONST_FIRST, (("tri_ge", P), ("causal_add", P), ("stick_big", P), ("strict_t", P), ("incl_t", P),
                       ("head_row", H * P), ("head_pair", 2), ("level", LEVELS * P), ("level0_t", P),
                       ("chunk_keep", S), ("keep_all", S)))):
    _at = 0
    for _name, _n in _entries:
        _table[_name] = (_at, _at + _n)
        _at += _n

PRM = {}
_at = 0
for _name, _n in (("norm_g", KD), ("final_g", KD), ("mu", 7), ("w0", 2), ("a0", 2), ("k_k", 2),
                  ("k_a", 2), ("r_k", 2), ("conv_w", 8), ("conv_b", 2), ("b_a", 2), ("b_x", 2),
                  ("lam", 2), ("b_f", 1), ("c", 2 * KD),
                  ("g_mix", 2 * KD), ("g_ffn", 2 * KD), ("b_ada", 2 * 48), ("conv_b2", 2 * 44),
                  ("conv_w2", 2 * 3 * 44), ("subln", 2), ("dqn", 2), ("dkn", 2), ("nqn", 2), ("nkn", 2),
                  ("gmlp_b", 2 * H)):
    PRM[_name] = (_at, _at + _n)
    _at += _n
NPRM = _at

ROW = {}
_at = 0
for _name, _n in (("ln_g", G), ("ln_b", G), ("gmlp_g", 2 * G), ("lam4", 2 * 128)):
    ROW[_name] = (_at, _at + _n)
    _at += _n
NROW = _at
ROWS_FIRST = 2 * G


def lambda_init(layer):
    return 0.8 - 0.6 * float(np.exp(-0.3 * layer))


class Kit:
    pass


class Signal:

    def __init__(self, nc, ctx, name):
        self.sem = ctx.enter_context(nc.semaphore(name))
        self.n = 0
        self.base = 0

    def up(self, instruction, by=1):
        instruction.then_inc(self.sem, by)
        self.n += by
        return self.n


def start_phase(K):
    for s in K.signals.values():
        s.base = s.n


def link(eng, signal, instruction):
    eng.wait_ge(signal.sem, signal.up(instruction))


def exp_and_log(act):
    act.preload_act_table_set("natural_log_exp_and_others")


def meet(K):
    goal = K.met.n + 4
    @K.block.tensor
    def _(e):
        e.drain().then_inc(K.met.sem, 1)
        e.wait_ge(K.met.sem, goal)
    @K.block.vector
    def _(e):
        e.drain().then_inc(K.met.sem, 1)
        e.wait_ge(K.met.sem, goal)
    @K.block.scalar
    def _(e):
        e.drain().then_inc(K.met.sem, 1)
        e.wait_ge(K.met.sem, goal)
    @K.block.gpsimd
    def _(e):
        e.drain().then_inc(K.met.sem, 1)
        e.wait_ge(K.met.sem, goal)
    K.met.n = goal
    start_phase(K)


def arena(K, ctx, name, shape, dtype=F32):
    K.serial += 1
    return ctx.enter_context(K.nc.sbuf_tensor(f"{name}_{K.serial}", shape, dtype))


def arena_pair(K, ctx, name, shape):
    return arena(K, ctx, name + "_high", shape, F32R), arena(K, ctx, name + "_low", shape, F32R)


def three_products(pe, out, lhs, rhs, first, last):
    (lh, ll), (rh, rl) = lhs, rhs
    pe.matmul(out, lh, rh, start=first, stop=False, skip_group_check=True)
    pe.matmul(out, lh, rl, start=False, stop=False, skip_group_check=True)
    return pe.matmul(out, ll, rh, start=False, stop=last, skip_group_check=True)


def const(K, name, rows=slice(0, P)):
    if name in CONST:
        a, b = CONST[name]
        return K.cst[rows, a:b]
    a, b = CONST_FIRST[name]
    return K.cst_first[rows, a:b]


def prm(K, name, col=0, n=1, rows=slice(0, P)):
    a = PRM[name][0] + col
    return K.prm[rows, a:a + n]


def row(K, name, first=0, n=G):
    a = ROW[name][0] + first
    return K.rows_first[:, a:a + n] if a < ROWS_FIRST else K.rows[:, a - ROWS_FIRST:a - ROWS_FIRST + n]



def stream_weights(K, n_units):
    @K.block.sync
    def _(sp):
        for j in range(RING):
            if j == 1:
                sp.wait_ge(K.signals["loaded"].sem, K.signals["loaded"].n)
            sp.dma_start(K.ring[:, j], K.w_units[j]).then_inc(K.slot_full[j].sem, 16)
        with sp.Fori(0, n_units // RING - 1) as i:
            for j in range(RING):
                sp.wait_ge(K.unit_used.sem, i * RING + j + 1)
                sp.dma_start(K.ring[:, j], K.w_units[ds(i * RING + (j + RING), 1)]
                             .rearrange("u p n -> (u p) n")).then_inc(K.slot_full[j].sem, 16)
        for u in range(n_units - n_units % RING, n_units):
            sp.wait_ge(K.unit_used.sem, u - RING + 1)
            sp.dma_start(K.ring[:, u % RING], K.w_units[u]).then_inc(K.slot_full[u % RING].sem, 16)



def rms_phase(K, src, dst, parts, room=None, end=True):
    square, added, stat, rstd_ready, scaled, high_ready, low_ready = (K.signals[n] for n in (
        "square", "added", "stat", "rstd", "normed", "high_ready", "low_ready"))
    split = isinstance(dst, tuple)
    width = max(c0 + w for c0, w, _, _ in parts)
    with ExitStack() as ctx:
        sq, rstd = room or (arena(K, ctx, "squares", [P, KD, width]), arena(K, ctx, "rstd", [P, width]))

        @K.block.scalar
        def _(act):
            exp_and_log(act)
            for c0, w, _, _ in parts:
                for k in range(KD):
                    square.up(act.activation(sq[:, k, c0:c0 + w], src[:, k, c0:c0 + w], ACT.Square))
            for n, (c0, w, _, shift) in enumerate(parts):
                act.wait_ge(stat.sem, stat.base + n + 1)
                link(act, K.act_step, act.activation(rstd[:, c0:c0 + w], K.ps[n][:, 0:w], ACT.Ln,
                                                     bias=K.eps[:, 0:1], scale=1.0 / D))
                rstd_ready.up(act.activation(rstd[:, c0:c0 + w], rstd[:, c0:c0 + w], ACT.Exp, scale=-0.5))
                for k in range(KD if split else 0):
                    act.wait_ge(scaled.sem, scaled.base + n * KD + k + 1)
                    t = sq[:, k, c0:c0 + w]
                    if shift is None:
                        high_ready.up(act.copy(dst[0][:, k, c0:c0 + w], t))
                    else:
                        high_ready.up(act.activation(dst[0][:, k, c0:c0 + w], t, ACT.Identity, bias=shift(k)))

        @K.block.tensor
        def _(pe):
            for n, (c0, w, _, _) in enumerate(parts):
                pe.wait_ge(added.sem, added.base + n + 1)
                stat.up(pe.matmul(K.ps[n][:, 0:w], const(K, "ones"), rstd[:, c0:c0 + w], start=True, stop=True))

        @K.block.vector
        def _(dve):
            for n, (c0, w, _, _) in enumerate(parts):
                for k in range(1, KD):
                    dve.wait_ge(square.sem, square.base + n * KD + k + 1)
                    so_far = sq[:, 0, c0:c0 + w] if k == 1 else rstd[:, c0:c0 + w]
                    ins = dve.tensor_tensor(rstd[:, c0:c0 + w], so_far, sq[:, k, c0:c0 + w], ALU.add)
                    if k < KD - 1:
                        link(dve, K.dve_step, ins)
                added.up(ins)
            for n, (c0, w, gain, shift) in enumerate(parts):
                dve.wait_ge(rstd_ready.sem, rstd_ready.base + n + 1)
                for k in range(KD + 2):
                    if k < KD:
                        to = sq[:, k, c0:c0 + w] if split else dst[:, k, c0:c0 + w]
                        scaled.up(dve.scalar_tensor_tensor(to, src[:, k, c0:c0 + w], gain(k), rstd[:, c0:c0 + w],
                                                           ALU.mult, ALU.mult))
                    if k < 2 or not split:
                        continue
                    dve.wait_ge(high_ready.sem, high_ready.base + n * KD + k - 1)
                    low, high = (dst[1][:, k - 2, c0:c0 + w], dst[0][:, k - 2, c0:c0 + w].bitcast(F32))
                    t = sq[:, k - 2, c0:c0 + w]
                    if shift is None:
                        low_ready.up(dve.tensor_tensor(low, t, high, ALU.subtract))
                    else:
                        low_ready.up(dve.scalar_tensor_tensor(low, t, shift(k - 2), high, ALU.add, ALU.subtract))
        if end:
            meet(K)


def split_moving(K, src, dst, w):
    high_ready, low_ready = K.signals["high_ready"], K.signals["low_ready"]

    @K.block.scalar
    def _(act):
        for k in range(KD):
            high_ready.up(act.copy(dst[0][:, k, 0:w], src[:, k, 0:w]))

    @K.block.vector
    def _(dve):
        for k in range(KD):
            dve.wait_ge(high_ready.sem, high_ready.base + k + 1)
            low_ready.up(dve.tensor_tensor(dst[1][:, k, 0:w], src[:, k, 0:w], dst[0][:, k, 0:w].bitcast(F32),
                                           ALU.subtract))



def split_high(K, act, i, j, guard=True):
    q = K.unit + j
    act.wait_ge(K.slot_full[q % RING].sem, i * 16 + 16 * (q // RING + 1))
    if guard:
        act.wait_ge(K.unit_done.sem, i * RING + (K.unit_done.base + j - 1))
    act.copy(K.w_high[:, q % 2], K.ring[:, q % RING]).then_inc(K.high_split.sem, 1)


def split_low(K, dve, i, j):
    q = K.unit + j
    dve.wait_ge(K.high_split.sem, i * RING + (K.high_split.n + j))
    dve.tensor_tensor(K.w_low[:, q % 2], K.ring[:, q % RING], K.w_high[:, q % 2].bitcast(F32),
                      ALU.subtract).then_inc(K.unit_used.sem, 1)


def split_first(K):
    @K.block.scalar
    def _(act):
        split_high(K, act, 0, 0, guard=False)
    K.high_split.n += 1

    @K.block.vector
    def _(dve):
        split_low(K, dve, 0, 0)
    K.unit_used.n += 1


def used_units(K, count, more):
    K.unit_used.n += count - 1 + more
    K.high_split.n += count - 1 + more
    K.unit_done.n += count
    K.unit += count


def weights(K, q, k):
    c = slice(k * P, k * P + P)
    return K.w_high[:, q % 2, c], K.w_low[:, q % 2, c]


def in_turns(eng, count, body):
    turns, rest = divmod(count, RING)
    if turns:
        for j in range(RING):
            body(0, j)
    if turns == 2:
        for j in range(RING):
            body(1, j)
    elif turns > 2:
        with eng.Fori(1, turns) as i:
            for j in range(RING):
                body(i, j)
    for j in range(rest):
        body(turns, j)


def feature_unit(K, pe, q, j, moving, with_ctx, waits):
    for s, (bank, a, b) in enumerate(((j, 0, S), (4 + j, S, S + C))[:1 + with_ctx]):
        for k in range(KD):
            if waits:
                pe.wait_ge(K.signals["low_ready"].sem, waits[s] + k + 1)
            mm = three_products(pe, K.ps[bank][:, 0:b - a], weights(K, q, k), tuple(m[:, k, a:b] for m in moving),
                                k == 0, k == KD - 1)
    mm.then_inc(K.unit_done.sem, 1)


def project(K, count, with_ctx, evac_main, evac_ctx, moving, waits=None):
    main_free, ctx_free = K.signals["main_free"], K.signals["ctx_free"]
    first = K.unit

    @K.block.tensor
    def _(pe):
        def unit(i, j):
            q = first + j
            pe.wait_ge(K.unit_used.sem, i * RING + (q + 1))
            pe.wait_ge(main_free.sem, i * RING + (j + main_free.base + 1))
            if with_ctx:
                pe.wait_ge(ctx_free.sem, i * RING + (j + ctx_free.base + 1))
            feature_unit(K, pe, q, j, moving, with_ctx, waits if isinstance(i, int) and i == j == 0 else None)
        in_turns(pe, count, unit)

    @K.block.vector
    def _(dve):
        def unit(i, j):
            split_low(K, dve, i, j + 1)
            dve.wait_ge(K.unit_done.sem, i * RING + (j + K.unit_done.base + 1))
            evac_main(dve, i * RING + j, K.ps[j]).then_inc(main_free.sem, 1)
        dve.sem_inc(main_free.sem, RING)
        in_turns(dve, count, unit)

    @K.block.scalar
    def _(act):
        def unit(i, j):
            split_high(K, act, i, j + 1)
            if with_ctx:
                act.wait_ge(K.unit_done.sem, i * RING + (j + K.unit_done.base + 1))
                evac_ctx(act, i * RING + j, K.ps[4 + j]).then_inc(ctx_free.sem, 1)
        if with_ctx:
            act.sem_inc(ctx_free.sem, RING)
        in_turns(act, count, unit)
    if with_ctx:
        ctx_free.n += RING + count
    main_free.n += RING + count
    used_units(K, count, True)
    meet(K)


def project_tokens(K, buf, tiles, moving, more=True):
    tile_done = K.signals["tile_done"]
    first, units = K.unit, 4

    @K.block.tensor
    def _(pe):
        for j in range(units):
            q = first + j
            pe.wait_ge(K.unit_used.sem, q + 1)
            for m in range(tiles):
                for kk in range(2):
                    k, c = 2 * j + kk, slice(kk * S, kk * S + S)
                    mm = three_products(pe, K.ps[m][:, :], tuple(x[:, k, m * P:m * P + P] for x in moving),
                                        (K.w_high[:, q % 2, c], K.w_low[:, q % 2, c]), k == 0, k == KD - 1)
                if j == units - 1:
                    tile_done.up(mm)
            if j < units - 1:
                mm.then_inc(K.unit_done.sem, 1)
        pe.drain().then_inc(K.unit_done.sem, 1)

    @K.block.vector
    def _(dve):
        for j in range(1, units + more):
            split_low(K, dve, 0, j)
        for m in range(min(NT, tiles)):
            dve.wait_ge(tile_done.sem, tile_done.base + m + 1)
            dve.tensor_copy(buf[:, m, :], K.ps[m][:, :])

    @K.block.scalar
    def _(act):
        for j in range(1, units + more):
            split_high(K, act, 0, j)
        for m in range(NT, tiles):
            act.wait_ge(tile_done.sem, tile_done.base + m + 1)
            act.copy(buf[:, m, :], K.ps[m][:, :])
    used_units(K, units, more)
    meet(K)



def softmax_attention(K, items, scale, neg_lam=None, beside=None):
    n_comp = len(items[0]["scores"])
    scored, max_ready, exped, weighted, turned_up, turned_out, mixed, put = (K.signals[n] for n in (
        "scored", "max_ready", "exped", "weighted", "turned_up", "turned_out", "mixed", "put"))
    n_items = len(items)
    kmax = max(i["kw"] for i in items)
    biased = items[0]["bias"] is not None
    split = kmax > S
    copies = 2 if split else 1
    slot, out_bank = (2 * S, 6) if split else (S, 2)
    with ExitStack() as ctx:
        probs = arena(K, ctx, "probs", [P, 2, n_comp, kmax])
        turned = arena(K, ctx, "turned", [P, 2, kmax])
        logits = arena(K, ctx, "logits", [P, 2, kmax]) if biased else None
        neg_max = arena(K, ctx, "neg_max", [P, n_items, n_comp])
        row_sum = arena(K, ctx, "row_sum", [P, n_items, n_comp])
        inv = arena(K, ctx, "inv", [P, n_items, n_comp])

        def score_tile(t, c, a, b):
            first = slot * ((t * n_comp + c) % 2)
            return K.psum[:, first + a:first + b]

        @K.block.tensor
        def _(pe):
            def scores(t):
                for c in range(n_comp):
                    n = t * n_comp + c
                    if n >= 2:
                        pe.wait_ge(exped.sem, exped.base + n - 1)
                    for group in items[t]["scores"][c]:
                        for g, (lhs, rhs, c0, w) in enumerate(group):
                            mm = pe.matmul(score_tile(t, c, c0, c0 + w), lhs, rhs,
                                           start=(g == 0), stop=(g == len(group) - 1),
                                           skip_group_check=len(group) > 1)
                    scored.up(mm)

            def turn(t):
                pe.wait_ge(weighted.sem, weighted.base + t + 1)
                if t >= 1:
                    pe.wait_ge(turned_out.sem, turned_out.base + copies * t)
                for b in range(items[t]["kw"] // P):
                    mm = pe.transpose(K.psum[:, 4 * S + b * P:4 * S + b * P + P],
                                      probs[:, t % 2, 0, b * P:b * P + P], const(K, "ident"))
                turned_up.up(mm)

            def mix(t):
                pe.wait_ge(turned_out.sem, turned_out.base + copies * (t + 1))
                if t >= 2:
                    pe.wait_ge(put.sem, put.base + t - 1)
                tiles = items[t]["tiles"]
                for b, tile in enumerate(tiles):
                    mm = pe.matmul(K.ps[out_bank + t % 2][items[t]["rows"], 0:P], items[t]["v"](tile),
                                   turned[:, t % 2, b * P:b * P + P], start=(b == 0), stop=(b == len(tiles) - 1))
                mixed.up(mm)

            for t in range(n_items + 2):
                if t < n_items:
                    scores(t)
                if beside:
                    beside(pe)
                if 0 <= t - 1 < n_items:
                    turn(t - 1)
                if 0 <= t - 2 < n_items:
                    mix(t - 2)

        @K.block.vector
        def _(dve):
            def maxima(t):
                kw, bias = items[t]["kw"], items[t]["bias"]
                for c in range(n_comp):
                    dve.wait_ge(scored.sem, scored.base + t * n_comp + c + 1)
                    m = neg_max[:, t, c:c + 1]
                    if bias is None:
                        link(dve, K.dve_step, dve.reduce_max(m, score_tile(t, c, 0, kw), AX, negate=True))
                        max_ready.up(dve.tensor_scalar(m, m, scale, None, ALU.mult))
                        continue
                    if t >= 2:
                        dve.wait_ge(exped.sem, exped.base + t - 1)
                    ins = dve.scalar_tensor_tensor(logits[:, t % 2, 0:S], score_tile(t, c, 0, S), scale, bias,
                                                   ALU.mult, ALU.add)
                    if kw > S:
                        ins = dve.tensor_scalar(logits[:, t % 2, S:kw], score_tile(t, c, S, kw), scale, None,
                                                ALU.mult)
                    link(dve, K.dve_step, ins)
                    max_ready.up(dve.reduce_max(m, logits[:, t % 2, 0:kw], AX, negate=True))

            def combine(t):
                kw = items[t]["kw"]
                dve.wait_ge(exped.sem, exped.base + (t + 1) * n_comp)
                link(dve, K.dve_step, dve.reciprocal(inv[:, t, :], row_sum[:, t, :]))
                if n_comp == 1:
                    weighted.up(dve.tensor_scalar(probs[:, t % 2, 0, 0:kw], probs[:, t % 2, 0, 0:kw],
                                                  inv[:, t, 0:1], None, ALU.mult))
                    return
                link(dve, K.dve_step, dve.tensor_tensor(inv[:, t, 1:2], inv[:, t, 1:2], neg_lam, ALU.mult))
                p0, p1 = probs[:, t % 2, 0, 0:kw], probs[:, t % 2, 1, 0:kw]
                link(dve, K.dve_step, dve.tensor_scalar(p1, p1, inv[:, t, 1:2], None, ALU.mult))
                weighted.up(dve.scalar_tensor_tensor(p0, p0, inv[:, t, 0:1], p1, ALU.mult, ALU.add))

            def copy_turned(t):
                dve.wait_ge(turned_up.sem, turned_up.base + t + 1)
                if t >= 2:
                    dve.wait_ge(mixed.sem, mixed.base + t - 1)
                w = min(items[t]["kw"], S)
                turned_out.up(dve.tensor_copy(turned[:, t % 2, 0:w], K.psum[:, 4 * S:4 * S + w]))

            def output(t):
                dve.wait_ge(mixed.sem, mixed.base + t + 1)
                put.up(items[t]["out"](dve, K.ps[out_bank + t % 2][items[t]["rows"], 0:P]))

            for t in range(n_items + 2):
                if 0 <= t - 1 < n_items:
                    combine(t - 1)
                if t < n_items:
                    maxima(t)
                if 0 <= t - 1 < n_items:
                    copy_turned(t - 1)
                if 0 <= t - 2 < n_items:
                    output(t - 2)

        @K.block.scalar
        def _(act):
            def exponentials(t):
                kw, bias = items[t]["kw"], items[t]["bias"]
                if t >= 2:
                    act.wait_ge(turned_up.sem, turned_up.base + t - 1)
                for c in range(n_comp):
                    act.wait_ge(max_ready.sem, max_ready.base + t * n_comp + c + 1)
                    src = logits[:, t % 2, 0:kw] if bias is not None else score_tile(t, c, 0, kw)
                    exped.up(act.activation(probs[:, t % 2, c, 0:kw], src, ACT.Exp, bias=neg_max[:, t, c:c + 1],
                                            scale=1.0 if bias is not None else scale,
                                            accum_out=row_sum[:, t, c:c + 1]))

            def copy_turned(t):
                act.wait_ge(turned_up.sem, turned_up.base + t + 1)
                if t >= 2:
                    act.wait_ge(mixed.sem, mixed.base + t - 1)
                turned_out.up(act.copy(turned[:, t % 2, S:kmax], K.psum[:, 5 * S:4 * S + kmax]))

            act.preload_act_table(ACT.Exp)
            for t in range(n_items + 1):
                if t < n_items:
                    exponentials(t)
                if split and 0 <= t - 1 < n_items:
                    copy_turned(t - 1)
        meet(K)


def to_feature_major(K, y, tiles, put):
    turned_up, put_done = K.signals["turned_up"], K.signals["put"]

    @K.block.tensor
    def _(pe):
        for u in range(2):
            for n, m in enumerate(tiles):
                mm = pe.transpose(K.ps[u][:, n * P:n * P + P], y[:, m, u * P:u * P + P], const(K, "ident"))
            turned_up.up(mm)

    @K.block.vector
    def _(dve):
        for u in range(2):
            dve.wait_ge(turned_up.sem, turned_up.base + u + 1)
            put_done.up(put(dve, u, K.ps[u][:, 0:len(tiles) * P]))
    meet(K)



def forgetting_attention(K, p, v, put):
    gates, = (K.signals[n] for n in ("prepared",))
    rows = slice(64, 64 + H)
    with ExitStack() as ctx:
        x = arena(K, ctx, "gate_x", [P, S])
        a = arena(K, ctx, "gate_a", [P, S])
        cum = arena(K, ctx, "neg_cum", [P, S])

        @K.block.tensor
        def _(pe):
            modulation_units(K, pe, 3)

        @K.block.vector
        def _(dve):
            dve.memset(cum[:, :], 0.0)
            link(dve, K.dve_step, dve.tensor_scalar(x[rows, :], p[rows, MISC, PAD:PAD + S],
                                                    prm(K, "b_f", rows=rows), None, ALU.add))
            gates.up(dve.tensor_scalar(a[rows, :], x[rows, :], -1.0, None, ALU.mult))
            dve.wait_ge(K.signals["soft"].sem, K.signals["soft"].base + 1)
            link(dve, K.dve_step, dve.tensor_scalar(x[rows, :], x[rows, :], 0.0, -1.0, ALU.min, ALU.mult))
            link(dve, K.dve_step, dve.tensor_tensor(x[rows, :], x[rows, :], a[rows, :], ALU.add))
            link(dve, K.dve_step, dve.tensor_tensor_scan(cum[rows, :], const(K, "keep_all", rows), x[rows, :], 0.0,
                                                         ALU.mult, ALU.add))

        @K.block.scalar
        def _(act):
            exp_and_log(act)
            act.wait_ge(gates.sem, gates.base + 1)
            for func, scale, bias in ((ACT.Abs, 1.0, 0.0), (ACT.Exp, -1.0, 0.0)):
                link(act, K.act_step, act.activation(a[rows, :], a[rows, :], func, scale=scale))
            K.signals["soft"].up(act.activation(a[rows, :], a[rows, :], ACT.Ln, bias=K.one[rows, 0:1]))
        meet(K)

        items = []
        for h in range(H):
            i, r = h // 2, slice(64 * (h % 2), 64 * (h % 2) + HD)
            for t in range(NT):
                kw = (t + 1) * P
                q = p[r, FQ + i, PAD + t * P:PAD + t * P + P]
                items.append(dict(
                    scores=[[[(q, p[r, FK + i, PAD:PAD + kw], 0, kw),
                              (const(K, "head_row")[:, h * P:h * P + P], cum[:, 0:kw], 0, kw),
                              (const(K, "ident"), const(K, "causal_add"), t * P, P)]]],
                    kw=kw, tiles=range(t + 1), bias=None,
                    v=lambda m, h=h: v[:, m, h * HD:h * HD + HD], rows=r,
                    out=lambda dve, psum, r=r, i=i, t=t: put(dve, i, psum, r, slice(t * P, t * P + P))))
        softmax_attention(K, items, HD ** -0.5, beside=lambda pe: modulation_units(K, pe, 1))



def stick_breaking_attention(K, p, v, out):
    scored, zed, softp, summed, diff, weighed, mixed, put = (K.signals[n] for n in (
        "scored", "exped", "soft", "summed", "prepared", "weighted", "mixed", "put"))
    with ExitStack() as ctx:
        z = arena(K, ctx, "stick_z", [P, 2, S])
        e = arena(K, ctx, "stick_e", [P, 2, S])
        sp = arena(K, ctx, "stick_softplus", [P, 2, NT, S])
        w = arena(K, ctx, "stick_weights", [P, 2, NT, S])
        steps = [(h, t) for h in range(H) for t in reversed(range(NT))]

        @K.block.tensor
        def _(pe):
            def scores(n):
                h, t = steps[n]
                i, r = h // 2, slice(64 * (h % 2), 64 * (h % 2) + HD)
                if n >= 2:
                    pe.wait_ge(softp.sem, softp.base + n - 1)
                    pe.wait_ge(zed.sem, zed.base + n - 1)
                scored.up(pe.matmul(K.ps[n % 2][:, t * P:S], p[r, SK + i, PAD + t * P:PAD + t * P + P],
                                    p[r, SQ + i, PAD + t * P:PAD + S], start=True, stop=True))

            def sums(n):
                h, t = steps[n]
                pe.wait_ge(softp.sem, softp.base + n + 1)
                if n >= 2:
                    pe.wait_ge(diff.sem, diff.base + n - 1)
                bank = K.ps[2 + n % 2]
                pe.matmul(bank[:, t * P:S], const(K, "tri_ge"), sp[:, h % 2, t, t * P:S],
                          start=True, stop=False, skip_group_check=True)
                for j in range(t + 1, NT):
                    pe.matmul(bank[:, j * P:S], const(K, "ones"), sp[:, h % 2, j, j * P:S],
                              start=False, stop=False, skip_group_check=True)
                summed.up(pe.matmul(bank[:, t * P:t * P + P], const(K, "ident"), const(K, "stick_big"),
                                    start=False, stop=True, skip_group_check=True))

            def mix(h):
                pe.wait_ge(weighed.sem, weighed.base + NT * (h + 1))
                if h >= 2:
                    pe.wait_ge(put.sem, put.base + h - 1)
                r = slice(64 * (h % 2), 64 * (h % 2) + HD)
                for t in range(NT):
                    mm = pe.matmul(K.ps[4 + h % 2][r, t * P:S], v[:, t, h * HD:h * HD + HD], w[:, h % 2, t, t * P:S],
                                   start=(t == 0), stop=(t == NT - 1), skip_group_check=True)
                mixed.up(mm)

            for n in range(len(steps) + 1):
                if n < len(steps):
                    scores(n)
                modulation_units(K, pe, 1)
                if n >= 1:
                    sums(n - 1)
                if n % NT == 1 and n > NT:
                    mix(n // NT - 1)
            mix(H - 1)

        @K.block.scalar
        def _(act):
            def soft(n):
                h, t = steps[n]
                src = K.ps[n % 2][:, t * P:S]
                act.wait_ge(scored.sem, scored.base + n + 1)
                if n >= 2:
                    act.wait_ge(softp.sem, softp.base + n - 1)
                    act.wait_ge(diff.sem, diff.base + n - 1)
                act.activation(z[:, n % 2, t * P:S], src, ACT.Identity, scale=HD ** -0.5)
                link(act, K.act_step, act.activation(e[:, n % 2, t * P:S], src, ACT.Abs, scale=HD ** -0.5))
                link(act, K.act_step, act.activation(e[:, n % 2, t * P:S], e[:, n % 2, t * P:S], ACT.Exp,
                                                     scale=-1.0))
                zed.up(act.activation(e[:, n % 2, t * P:S], e[:, n % 2, t * P:S], ACT.Ln, bias=K.one[:, 0:1]))

            def weigh(n):
                h, t = steps[n]
                act.wait_ge(diff.sem, diff.base + n + 1)
                part = w[:, h % 2, t, t * P:S]
                weighed.up(act.activation(part, part, ACT.Exp))

            exp_and_log(act)
            for n in range(len(steps) + 1):
                if n < len(steps):
                    soft(n)
                if n >= 1:
                    weigh(n - 1)

        @K.block.vector
        def _(dve):
            def soft(n):
                h, t = steps[n]
                dve.wait_ge(zed.sem, zed.base + n + 1)
                if h >= 2 and t == NT - 1:
                    dve.wait_ge(summed.sem, summed.base + NT * (h - 1))
                part = sp[:, h % 2, t, t * P:S]
                link(dve, K.dve_step, dve.scalar_tensor_tensor(part, z[:, n % 2, t * P:S], 0.0,
                                                               e[:, n % 2, t * P:S], ALU.max, ALU.add))
                part = sp[:, h % 2, t, t * P:t * P + P]
                softp.up(dve.tensor_tensor(part, part, const(K, "strict_t"), ALU.mult))

            def differ(n):
                h, t = steps[n]
                dve.wait_ge(summed.sem, summed.base + n + 1)
                if h >= 2 and t == NT - 1:
                    dve.wait_ge(mixed.sem, mixed.base + h - 1)
                diff.up(dve.tensor_tensor(w[:, h % 2, t, t * P:S], z[:, n % 2, t * P:S],
                                          K.ps[2 + n % 2][:, t * P:S], ALU.subtract))

            def output(h):
                dve.wait_ge(mixed.sem, mixed.base + h + 1)
                r = slice(64 * (h % 2), 64 * (h % 2) + HD)
                put.up(out(dve, h // 2, K.ps[4 + h % 2][r, :], r, slice(0, S)))

            for n in range(len(steps) + 1):
                if n < len(steps):
                    soft(n)
                if n >= 1:
                    differ(n - 1)
                if n % NT == 2 and n > NT:
                    output(n // NT - 1)
            output(H - 1)
        meet(K)



def rg_lru(K, p, out):
    conv, gated, rate_ready, done = (K.signals[n] for n in ("prepared", "scored", "exped", "weighted"))
    with ExitStack() as ctx:
        xc = arena(K, ctx, "lru_x", [P, 2, S])
        r = arena(K, ctx, "lru_r", [P, 2, S])
        g = arena(K, ctx, "lru_i", [P, 2, S])
        a = arena(K, ctx, "lru_a", [P, 2, S])
        th = arena(K, ctx, "lru_tanh", [P, 2, S])
        s8 = arena(K, ctx, "lru_rate", [P, 2])
        w = arena(K, ctx, "lru_w", [P, 4, P])

        @K.block.gpsimd
        def _(pool):
            K.loaded_late.up(pool.dma_start(w[:, :, :], K.lru_w_dram.rearrange("p (a b) -> p a b", a=4)), 16)
        w_value = K.loaded_late.n

        @K.block.vector
        def _(dve):
            for i in range(2):
                x = lambda k: p[:, LX + i, PAD - 3 + k:PAD - 3 + k + S]
                cw = lambda k: prm(K, "conv_w", 2 * k + i)
                link(dve, K.dve_step, dve.tensor_scalar(xc[:, i], x(0), cw(0), prm(K, "conv_b", i),
                                                        ALU.mult, ALU.add))
                for k in range(1, 4):
                    ins = dve.scalar_tensor_tensor(xc[:, i], x(k), cw(k), xc[:, i], ALU.mult, ALU.add)
                    if k < 3:
                        link(dve, K.dve_step, ins)
                conv.up(ins)
            for i in range(2):
                dve.wait_ge(rate_ready.sem, rate_ready.base + 1 + i)
                link(dve, K.dve_step, dve.tensor_tensor(g[:, i], g[:, i], xc[:, i], ALU.mult))
                link(dve, K.dve_step, dve.scalar_tensor_tensor(th[:, i], r[:, i], 1.0, th[:, i], ALU.add, ALU.mult))
            done.up(dve.tensor_scalar(th[:, :, :], th[:, :, :], 0.0, None, ALU.max))
            dve.wait_ge(rate_ready.sem, rate_ready.base + 4)
            for i in range(2):
                link(dve, K.dve_step, dve.tensor_tensor(g[:, i], g[:, i], th[:, i], ALU.mult))
                link(dve, K.dve_step, dve.tensor_tensor_scan(xc[:, i], a[:, i], g[:, i], 0.0, ALU.mult, ALU.add))
                out(dve, i, xc[:, i])

        @K.block.tensor
        def _(pe):
            pe.wait_ge(K.loaded_late.sem, w_value)
            for i in range(2):
                pe.wait_ge(conv.sem, conv.base + i + 1)
                pe.matmul(K.ps[2 * i][:, :], w[:, i], xc[:, i], start=True, stop=True)
                gated.up(pe.matmul(K.ps[2 * i + 1][:, :], w[:, 2 + i], xc[:, i], start=True, stop=True))
            modulation_units(K, pe, 11)

        @K.block.scalar
        def _(act):
            t0, t1 = th[:, 0, 0:2], th[:, 0, 2:4]
            link(act, K.act_step, act.activation(t0, prm(K, "lam", 0, 2), ACT.Abs))
            link(act, K.act_step, act.activation(t0, t0, ACT.Exp, scale=-1.0))
            link(act, K.act_step, act.activation(t0, t0, ACT.Ln, bias=K.one[:, 0:1]))
            link(act, K.act_step, act.activation(t1, prm(K, "lam", 0, 2), ACT.Relu, scale=-1.0))
            link(act, K.act_step, act.activation(t1[:, 0:1], t1[:, 0:1], ACT.Identity, bias=t0[:, 0:1]))
            link(act, K.act_step, act.activation(t1[:, 1:2], t1[:, 1:2], ACT.Identity, bias=t0[:, 1:2]))
            link(act, K.act_step, act.activation(s8[:, :], t1, ACT.Identity, scale=-8.0))
            act.wait_ge(gated.sem, gated.base + 2)
            for i in range(2):
                act.activation(r[:, i], K.ps[2 * i][:, :], ACT.Sigmoid, bias=prm(K, "b_a", i))
                link(act, K.act_step, act.activation(g[:, i], K.ps[2 * i + 1][:, :], ACT.Sigmoid,
                                                     bias=prm(K, "b_x", i)))
            for i in range(2):
                link(act, K.act_step, act.activation(r[:, i], r[:, i], ACT.Identity, scale=s8[:, i:i + 1]))
                act.activation(a[:, i], r[:, i], ACT.Exp)
                link(act, K.act_step, act.activation(th[:, i], r[:, i], ACT.Tanh, scale=-1.0))
                rate_ready.up(act.activation(r[:, i], r[:, i], ACT.Exp, scale=2.0))
            act.wait_ge(done.sem, done.base + 1)
            for i in range(2):
                rate_ready.up(act.activation(th[:, i], th[:, i], ACT.Sqrt))
        meet(K)



def rwkv(K, p, spare, y):
    sig = K.signals
    with ExitStack() as ctx:
        nd = arena(K, ctx, "log_decay", [P, 2, S])
        cl = arena(K, ctx, "cum_log_decay", [P, 2, S])
        rate = arena(K, ctx, "rate", [P, 2, S])
        kk = arena(K, ctx, "kk", [P, 2, S])
        t0 = arena(K, ctx, "rwkv_t0", [P, 2, S])
        t1 = arena(K, ctx, "rwkv_t1", [P, 2, S])
        t2 = arena(K, ctx, "rwkv_t2", [P, 2, S])
        rkr = arena(K, ctx, "rwkv_rkr", [P, 2, S])
        decay_end = arena(K, ctx, "decay_end", [P, 2, NT])
        one_less = arena(K, ctx, "one_less_k_a", [P, 2])
        inner = ctx.enter_context(ExitStack())
        shifted = arena(K, inner, "shifted", [P, S])
        low = arena(K, inner, "low_rank", [P, S])
        lora = arena(K, inner, "lora", [64, G])
        col = lambda u: p[:, u:u + 2, PAD:PAD + S]
        r, k, v = col(RR), col(RK), col(RV)

        @K.block.gpsimd
        def _(pool):
            K.loaded_late.up(pool.dma_start(lora[:, :], K.lora_dram), 16)
        lora_value = K.loaded_late.n

        mixed, low_ready, projected, act_out, kk_out, normed = (sig[n] for n in (
            "prepared", "soft", "scored", "exped", "weighted", "summed"))

        @K.block.vector
        def _(dve):
            for n, u in enumerate((MISC, RR, RR + 1, RK, RK + 1, RV, RV + 1)):
                rows = slice(0, 64) if u == MISC else slice(0, P)
                if n:
                    dve.wait_ge(mixed.sem, mixed.base + n)
                cur, prev = p[rows, u, PAD:PAD + S], p[rows, u, PAD - 1:PAD - 1 + S]
                link(dve, K.dve_step, dve.tensor_tensor(shifted[rows, :], prev, cur, ALU.subtract))
                mixed.up(dve.scalar_tensor_tensor(cur, shifted[rows, :], prm(K, "mu", (n - 1) % 7, rows=rows), cur,
                                                  ALU.mult, ALU.add))
            dve.wait_ge(mixed.sem, mixed.base + 7)
            dve.tensor_scalar(one_less[:, :], prm(K, "k_a", 0, 2), -1.0, 1.0, ALU.mult, ALU.add)
            for i in range(2):
                ins = dve.tensor_scalar(kk[:, i], k[:, i], prm(K, "k_k", i), None, ALU.mult)
            kk_out.up(ins)
            dve.wait_ge(act_out.sem, act_out.base + 1)
            link(dve, K.dve_step, dve.tensor_scalar(nd[:, :, :], nd[:, :, :], -DECAY, None, ALU.mult))
            for i in range(2):
                ins = dve.tensor_tensor_scan(cl[:, i], const(K, "chunk_keep"), nd[:, i], 0.0, ALU.mult, ALU.add)
            link(dve, K.dve_step, ins)
            kk_out.up(dve.tensor_tensor(nd[:, :, :], cl[:, :, :], nd[:, :, :], ALU.subtract))
            for i in range(2):
                ins = dve.tensor_scalar(t0[:, i], rate[:, i], prm(K, "k_a", i), one_less[:, i:i + 1],
                                        ALU.mult, ALU.add)
            link(dve, K.dve_step, ins)
            link(dve, K.dve_step, dve.tensor_tensor(k, k, t0[:, :, :], ALU.mult))
            for i in range(2):
                dve.scalar_tensor_tensor(rkr[:, i], r[:, i], prm(K, "r_k", i), k[:, i], ALU.mult, ALU.mult)
            dve.wait_ge(normed.sem, normed.base + 1)
            for i in range(2):
                ins = dve.tensor_scalar(t0[:, i], K.ps[4 + i][:, :], 1e-12, None, ALU.max)
            kk_out.up(ins)
            dve.wait_ge(act_out.sem, act_out.base + 2)
            link(dve, K.dve_step, dve.tensor_tensor(kk[:, :, :], kk[:, :, :], t0[:, :, :], ALU.mult))
            dve.wait_ge(act_out.sem, act_out.base + 3)
            link(dve, K.dve_step, dve.tensor_tensor(rate[:, :, :], rate[:, :, :], kk[:, :, :], ALU.mult))
            dve.tensor_tensor(rate[:, :, :], rate[:, :, :], t2[:, :, :], ALU.mult)
            dve.scalar_tensor_tensor(kk[:, :, :], kk[:, :, :], -1.0, nd[:, :, :], ALU.mult, ALU.mult)
            dve.tensor_tensor(k, k, t2[:, :, :], ALU.mult)
            dve.tensor_tensor(r, r, t1[:, :, :], ALU.mult)

        @K.block.scalar
        def _(act):
            act.wait_ge(mixed.sem, mixed.base + 1)
            low_ready.up(act.activation(low[0:32, :], p[0:32, MISC, PAD:PAD + S], ACT.Tanh))
            low_ready.up(act.copy(low[32:64, :], p[32:64, MISC, PAD:PAD + S]))
            act.wait_ge(projected.sem, projected.base + 1)
            for i in range(2):
                act.activation(nd[:, i], K.ps[i][:, :], ACT.Sigmoid, bias=prm(K, "w0", i))
                ins = act.activation(rate[:, i], K.ps[2 + i][:, :], ACT.Sigmoid, bias=prm(K, "a0", i))
            act_out.up(ins)
            act.wait_ge(kk_out.sem, kk_out.base + 1)
            low_ready.up(act.activation(t1[:, :, :], kk[:, :, :], ACT.Square))
            act.wait_ge(kk_out.sem, kk_out.base + 3)
            link(act, K.act_step, act.activation(t0[:, :, :], t0[:, :, :], ACT.Ln))
            act_out.up(act.activation(t0[:, :, :], t0[:, :, :], ACT.Exp, scale=-0.5))
            act.activation(t1[:, :, :], cl[:, :, :], ACT.Exp, bias=K.half[:, 0:1])
            act.activation(t2[:, :, :], cl[:, :, :], ACT.Exp, bias=K.minus_half[:, 0:1], scale=-1.0)
            act.activation(decay_end[:, :, :], cl[:, :, CH - 1::CH], ACT.Exp)
            act_out.up(act.activation(nd[:, :, :], nd[:, :, :], ACT.Exp, bias=K.half[:, 0:1]))

        @K.block.tensor
        def _(pe):
            modulation_units(K, pe, 1)
            pe.wait_ge(K.loaded_late.sem, lora_value)
            pe.wait_ge(low_ready.sem, low_ready.base + 2)
            for i in range(2):
                pe.matmul(K.ps[i][:, :], lora[0:32, i * P:i * P + P], low[0:32, :], start=True, stop=True)
            for i in range(2):
                mm = pe.matmul(K.ps[2 + i][:, :], lora[32:64, i * P:i * P + P], low[32:64, :], start=True, stop=True)
            projected.up(mm)
            modulation_units(K, pe, 4)
            pe.wait_ge(low_ready.sem, low_ready.base + 3)
            for i in range(2):
                mm = pe.matmul(K.ps[4 + i][:, :], const(K, "block64"), t1[:, i], start=True, stop=True)
            normed.up(mm)
            modulation_units(K, pe, 6)
        meet(K)
        inner.close()

        tok = [x[:, :, :].rearrange("p i s -> p (i s)").rearrange("p (c f) -> p c f", c=NT) for x in (t0, t1, t2, cl)]
        a_tok, b_tok, k_tok, v_tok = tok
        turned_up, turned_out = sig["turned_up"], (sig["turned_out"], sig["put"])

        @K.block.tensor
        def _(pe):
            for q, x in enumerate((kk, rate, k, v)):
                for i in range(2):
                    if q == 3:
                        pe.wait_ge(turned_out[i].sem, turned_out[i].base + 1)
                    for c in range(NT):
                        mm = pe.transpose(K.ps[(2 * q + i) % 6][:, c * P:c * P + P], x[:, i, c * P:c * P + P],
                                          const(K, "ident"))
                    turned_up.up(mm)

        @K.block.vector
        def _(dve):
            for n in range(0, 8, 2):
                dve.wait_ge(turned_up.sem, turned_up.base + n + 1)
                ins = dve.tensor_copy(tok[n // 2][:, :, 0:P], K.ps[n % 6][:, :].rearrange("p (c f) -> p c f", c=NT))
                turned_out[0].up(ins)

        @K.block.scalar
        def _(act):
            for n in range(1, 8, 2):
                act.wait_ge(turned_up.sem, turned_up.base + n + 1)
                turned_out[1].up(act.copy(tok[n // 2][:, :, P:2 * P],
                                          K.ps[n % 6][:, :].rearrange("p (c f) -> p c f", c=NT)))
        meet(K)
        rwkv_chunks(K, kk, rate, k, r, a_tok, b_tok, k_tok, v_tok, decay_end, rkr, p, spare, y)


def rwkv_chunks(K, ad, bd, kd, rd, a_tok, b_tok, k_tok, v_tok, decay_end, rkr, p, spare, y):
    sig = K.signals
    produced, taken, w_up, w_out, u_up, u_out, y_up, y_out, s_out = (
        sig[n] for n in ("produced", "taken", "w_up", "w_out", "u_up", "u_out", "y_up", "y_out", "s_out"))
    x_ready, m_up, m_out, t_up, t_out = ([sig[f"{n}{b}"] for b in range(2)] for n in (
        "x_ready", "m_up", "m_out", "t_up", "t_out"))
    heads = [(e, i) for e in range(2) for i in range(2)]
    wide = lambda ap: ap.unsqueeze(1).to_broadcast([P, 2, P])
    flat = lambda ap: ap.rearrange("p e i t -> p (e i t)")
    M_BANK, T_BANK, W_BANK = (6, 2), (0, 3), (2, 0)
    STEPS = LEVELS - 1
    with ExitStack() as ctx:
        rooms = [[p[:, u, PAD:] for u in range(FQ, FQ + 7)],
                 [p[:, u, PAD:] for u in (SK + 1, MISC, LX, LX + 1)] + [spare[:, n, :] for n in range(3)]]
        a_mat, ak_t, rk_t, rb_t, t_mat, t_t, m_mat = (
            [rooms[b][n].rearrange("p (e i t) -> p e i t", e=2, i=2) for b in range(2)] for n in range(7))
        x_mat = arena(K, ctx, "x_mat", [P, 2, 2, 2, P])
        ta_t = arena(K, ctx, "ta_t", [P, 2, 2, P])
        w1 = arena(K, ctx, "w1", [P, 2, G])
        u = arena(K, ctx, "u", [P, G])
        state = arena(K, ctx, "state", [P, 2, HD])
        bonus = arena(K, ctx, "bonus", [P, NT, H])
        row64 = lambda e: slice(64 * e, 64 * e + HD)
        hcol = lambda e, i: slice(i * P + e * HD, i * P + e * HD + HD)

        @K.block.tensor
        def _(pe):
            def produce(c):
                tc_ = slice(c * CH, c * CH + CH)
                if c % 2:
                    pe.wait_ge(t_out[0].sem, t_out[0].base + c // 2 * LEVELS + 1)
                else:
                    if c:
                        pe.wait_ge(y_out.sem, y_out.base + c)
                    pe.wait_ge(s_out.sem, s_out.base + c + 1)
                for e in range(2):
                    r = row64(e)
                    for n, (l, m) in enumerate(((ad, bd), (bd, ad), (kd, ad), (kd, rd), (bd, rd))):
                        for i in range(2):
                            at = (n % 2) * 2 * P + i * P
                            pe.matmul(K.ps[3 * e + n // 2][:, at:at + P], l[r, i, tc_], m[r, i, tc_],
                                      start=True, stop=True)
                for i in range(2):
                    mm = pe.matmul(K.ps[5][:, 2 * P + i * 2:2 * P + i * 2 + 2], rkr[:, i, tc_], const(K, "head_pair"),
                                   start=True, stop=True)
                produced.up(mm)

            def level_m(g, lev, b):
                n = g * STEPS + lev - 1
                pe.wait_ge(x_ready[b].sem, x_ready[b].base + n + 1)
                pe.wait_ge(t_out[b].sem, t_out[b].base + g * LEVELS + lev)
                for h, (e, i) in enumerate(heads):
                    mm = pe.matmul(K.ps[M_BANK[b]][:, h * P:h * P + P], x_mat[:, b, e, i], t_t[b][:, e, i],
                                   start=True, stop=True)
                m_up[b].up(mm)

            def level_t(g, lev, b):
                n = g * STEPS + lev - 1
                pe.wait_ge(m_out[b].sem, m_out[b].base + n + 1)
                for h, (e, i) in enumerate(heads):
                    pe.matmul(K.ps[T_BANK[b]][:, h * P:h * P + P], t_mat[b][:, e, i], m_mat[b][:, e, i],
                              start=True, stop=True)
                for h, (e, i) in enumerate(heads):
                    mm = pe.matmul(K.ps[T_BANK[b] + 1][:, h * P:h * P + P], m_mat[b][:, e, i], t_mat[b][:, e, i],
                                   start=True, stop=True)
                t_up[b].up(mm)

            def apply(c):
                b = c % 2
                for e, i in heads:
                    pe.matmul(K.ps[W_BANK[b]][:, hcol(e, i)], ak_t[b][:, e, i], v_tok[:, c, hcol(e, i)],
                              start=True, stop=True)
                for e, i in heads:
                    mm = pe.matmul(K.ps[W_BANK[b] + 1][row64(e), i * P:i * P + P], a_tok[:, c, hcol(e, i)],
                                   t_t[b][:, e, i], start=True, stop=True)
                w_up.up(mm)

            def advance(c):
                b, tc_ = c % 2, slice(c * CH, c * CH + CH)
                pe.wait_ge(w_out.sem, w_out.base + c + 1)
                if b:
                    pe.wait_ge(s_out.sem, s_out.base + c + 1)
                for e, i in heads:
                    pe.matmul(K.ps[4 + e][:, i * HD:i * HD + HD], t_t[b][:, e, i], w1[:, b, hcol(e, i)],
                              start=True, stop=False)
                    mm = pe.matmul(K.ps[4 + e][:, i * HD:i * HD + HD], ta_t[row64(e), b, i], state[row64(e), i],
                                   start=False, stop=True)
                u_up.up(mm)
                modulation_units(K, pe, 1)
                pe.wait_ge(u_out.sem, u_out.base + c + 1)
                if b:
                    pe.wait_ge(y_out.sem, y_out.base + c)
                for e, i in heads:
                    to = K.ps[6][row64(e), i * HD:i * HD + HD]
                    pe.matmul(to, b_tok[:, c, hcol(e, i)], u[:, hcol(e, i)], start=True, stop=False)
                    pe.matmul(to, k_tok[:, c, hcol(e, i)], v_tok[:, c, hcol(e, i)], start=False, stop=True)
                for e, i in heads:
                    to = K.ps[2 + e][:, P * 2 + i * HD:P * 2 + i * HD + HD]
                    pe.matmul(to, rd[row64(e), i, tc_], state[row64(e), i], start=True, stop=False)
                    pe.matmul(to, rb_t[b][:, e, i], u[:, hcol(e, i)], start=False, stop=False)
                    mm = pe.matmul(to, rk_t[b][:, e, i], v_tok[:, c, hcol(e, i)], start=False, stop=True)
                y_up.up(mm)
                modulation_units(K, pe, 2)

            for g in range(NT // 2):
                produce(2 * g)
                modulation_units(K, pe, 2)
                produce(2 * g + 1)
                modulation_units(K, pe, 2)
                pe.wait_ge(t_out[1].sem, t_out[1].base + g * LEVELS + 1)
                for lev in range(1, LEVELS):
                    level_m(g, lev, 0)
                    level_m(g, lev, 1)
                    if lev % 2:
                        modulation_units(K, pe, 1)
                    level_t(g, lev, 0)
                    level_t(g, lev, 1)
                for b in range(2):
                    pe.wait_ge(t_out[b].sem, t_out[b].base + (g + 1) * LEVELS)
                apply(2 * g)
                apply(2 * g + 1)
                advance(2 * g)
                advance(2 * g + 1)

        @K.block.gpsimd
        def _(pool):
            for g in range(NT // 2):
                for lev in range(1, LEVELS):
                    for b in range(2):
                        n = g * STEPS + lev - 1
                        pool.wait_ge(taken.sem, taken.base + 2 * g + b + 1)
                        if n:
                            pool.wait_ge(m_up[b].sem, m_up[b].base + n)
                        mask = const(K, "level")[:, lev * P:lev * P + P]
                        for e in range(2):
                            ins = pool.tensor_tensor(x_mat[:, b, e], a_mat[b][:, e], wide(mask), ALU.mult)
                        x_ready[b].up(ins)

        @K.block.vector
        def _(dve):
            def take_products(c):
                g, b = divmod(c, 2)
                dve.wait_ge(produced.sem, produced.base + c + 1)
                if g:
                    dve.wait_ge(x_ready[b].sem, x_ready[b].base + g * STEPS)
                prod = lambda n, e: K.ps[3 * e + n // 2][:, (n % 2) * 2 * P:(n % 2) * 2 * P + 2 * P] \
                    .rearrange("p (i t) -> p i t", i=2)
                for e in range(2):
                    ins = dve.tensor_copy(a_mat[b][:, e], prod(0, e))
                taken.up(ins)
                for e in range(2):
                    dve.tensor_tensor(t_mat[b][:, e], prod(0, e), wide(const(K, "level")[:, 0:P]), ALU.mult)
                    ins = dve.tensor_tensor(t_t[b][:, e], prod(1, e), wide(const(K, "level0_t")), ALU.mult)
                link(dve, K.dve_step, ins)
                for e in range(2):
                    dve.tensor_tensor(t_mat[b][:, e], t_mat[b][:, e], wide(const(K, "ident")), ALU.add)
                    dve.tensor_tensor(t_t[b][:, e], t_t[b][:, e], wide(const(K, "ident")), ALU.add)
                for e in range(2):
                    dve.tensor_tensor(ak_t[b][:, e], prod(2, e), wide(const(K, "strict_t")), ALU.mult)
                    dve.tensor_tensor(rk_t[b][:, e], prod(3, e), wide(const(K, "incl_t")), ALU.mult)
                    dve.tensor_tensor(rb_t[b][:, e], prod(4, e), wide(const(K, "incl_t")), ALU.mult)
                t_out[b].up(dve.tensor_copy(bonus[:, c, :], K.ps[5][:, 2 * P:2 * P + H]))

            def add_level(g, lev, b):
                dve.wait_ge(t_up[b].sem, t_up[b].base + g * STEPS + lev)
                dve.tensor_tensor(flat(t_t[b]), flat(t_t[b]), K.ps[T_BANK[b]][:, :], ALU.add)
                t_out[b].up(dve.tensor_tensor(flat(t_mat[b]), flat(t_mat[b]), K.ps[T_BANK[b] + 1][:, :], ALU.add))

            def take_applied(c):
                b = c % 2
                dve.wait_ge(w_up.sem, w_up.base + c + 1)
                dve.tensor_copy(w1[:, b, :], K.ps[W_BANK[b]][:, 0:G])
                w_out.up(dve.tensor_copy(ta_t[:, b], K.ps[W_BANK[b] + 1][:, 0:2 * P].rearrange("p (i t) -> p i t", i=2)))

            def advance(c):
                dve.wait_ge(u_up.sem, u_up.base + c + 1)
                for e in range(2):
                    ins = dve.tensor_copy(u[:, :].rearrange("p (i e d) -> p e i d", i=2, e=2)[:, e],
                                          K.ps[4 + e][:, 0:2 * HD].rearrange("p (i d) -> p i d", i=2))
                u_out.up(ins)
                dve.wait_ge(y_up.sem, y_up.base + c + 1)
                for i in range(2):
                    ins = dve.tensor_scalar(state[:, i], state[:, i], decay_end[:, i, c:c + 1], None, ALU.mult)
                link(dve, K.dve_step, ins)
                for i in range(2):
                    ins = dve.scalar_tensor_tensor(state[:, i], K.ps[6][:, i * HD:i * HD + HD],
                                                   decay_end[:, i, c:c + 1], state[:, i], ALU.mult, ALU.add)
                s_out.up(ins)
                for e in range(2):
                    ins = dve.tensor_copy(y[:, c, :].rearrange("p (i e d) -> p e i d", i=2, e=2)[:, e],
                                          K.ps[2 + e][:, 2 * P:2 * P + 2 * HD].rearrange("p (i d) -> p i d", i=2))
                y_out.up(ins)

            s_out.up(dve.memset(state[:, :, :], 0.0))
            for g in range(NT // 2):
                take_products(2 * g)
                take_products(2 * g + 1)
                for lev in range(1, LEVELS):
                    add_level(g, lev, 0)
                    add_level(g, lev, 1)
                take_applied(2 * g)
                take_applied(2 * g + 1)
                advance(2 * g)
                advance(2 * g + 1)

        @K.block.scalar
        def _(act):
            for n in range(NT // 2 * STEPS):
                for b in range(2):
                    act.wait_ge(m_up[b].sem, m_up[b].base + n + 1)
                    if n:
                        act.wait_ge(t_up[b].sem, t_up[b].base + n)
                    m_out[b].up(act.copy(flat(m_mat[b]), K.ps[M_BANK[b]][:, :]))
        meet(K)

        stats = arena(K, ctx, "gn_stats", [P, NT * H])
        stats2 = arena(K, ctx, "gn_stats2", [P, NT * H])
        sq = x_mat[:, :, :, :, :].rearrange("p b e i t -> p (b e i t)").rearrange("p (c f) -> p c f", c=NT)
        yh = y[:, :, :].rearrange("p c (h d) -> p (c h) d", d=HD)
        sqh = sq[:, :, :].rearrange("p c (h d) -> p (c h) d", d=HD)
        per_head = lambda ap: ap.unsqueeze(2).to_broadcast([P, NT * H, HD])
        per_tile = lambda ap: ap.unsqueeze(1).to_broadcast([P, NT, G])

        @K.block.tensor
        def _(pe):
            modulation_units(K, pe, MOD_UNITS)
        centred, squared, inv = sig["prepared"], sig["soft"], sig["exped"]

        @K.block.vector
        def _(dve):
            link(dve, K.dve_step, dve.tensor_reduce(stats[:, :], yh, AX, ALU.add))
            link(dve, K.dve_step, dve.tensor_scalar(stats[:, :], stats[:, :], 1.0 / HD, None, ALU.mult))
            centred.up(dve.tensor_tensor(yh, yh, per_head(stats[:, :]), ALU.subtract))
            dve.wait_ge(squared.sem, squared.base + 1)
            centred.up(dve.tensor_reduce(stats2[:, :], sqh, AX, ALU.add))
            dve.wait_ge(inv.sem, inv.base + 1)
            link(dve, K.dve_step, dve.tensor_tensor(yh, yh, per_head(stats2[:, :]), ALU.mult))
            link(dve, K.dve_step, dve.tensor_tensor(y[:, :, :], y[:, :, :], per_tile(row(K, "ln_g")), ALU.mult))
            dve.tensor_tensor(sqh, v_tok[:, :, :].rearrange("p c (h d) -> p (c h) d", d=HD),
                              per_head(bonus[:, :, :].rearrange("p c h -> p (c h)")), ALU.mult)
            link(dve, K.dve_step, dve.tensor_tensor(y[:, :, :], y[:, :, :], per_tile(row(K, "ln_b")), ALU.add))
            dve.tensor_tensor(y[:, :, :], y[:, :, :], sq[:, :, :], ALU.add)

        @K.block.scalar
        def _(act):
            exp_and_log(act)
            act.wait_ge(centred.sem, centred.base + 1)
            squared.up(act.activation(sqh, yh, ACT.Square))
            act.wait_ge(centred.sem, centred.base + 2)
            link(act, K.act_step, act.activation(stats2[:, :], stats2[:, :], ACT.Ln, bias=K.gn_eps[:, 0:1],
                                                 scale=1.0 / HD))
            inv.up(act.activation(stats2[:, :], stats2[:, :], ACT.Exp, scale=-0.5))
        meet(K)



def modulation_units(K, pe, n):
    for _ in range(min(n, MOD_UNITS - K.units_modulated)):
        q, (g, j) = K.modulation_first + K.units_modulated, divmod(K.units_modulated, 4)
        at = 2 * (MOD_GROUPS - 1 - g)
        pe.wait_ge(K.slot_full[q % RING].sem, 16 * (q // RING + 1))
        for kk in range(2):
            mm = pe.matmul(K.ps[7][0:2 * MOD_GROUPS, :], K.cond[:, 2 * j + kk, at:at + 2 * MOD_GROUPS],
                           K.ring[:, q % RING, kk * S:kk * S + S], start=(g == j == kk == 0),
                           stop=(K.units_modulated == MOD_UNITS - 1 and kk == 1), skip_group_check=True)
        K.unit_used.up(mm)
        K.unit += 1
        K.units_modulated += 1


def finish_modulation(K):
    rows, per_layer = 2 * MOD_GROUPS, MOD_GROUPS // 2
    summed, copied, turned_up = (K.signals[n] for n in ("summed", "prepared", "turned_up"))
    with ExitStack() as ctx:
        by_row = arena(K, ctx, "mods_by_row", [P, S])

        @K.block.tensor
        def _(pe):
            summed.up(pe.drain())
            pe.wait_ge(copied.sem, copied.base + 1)
            for j in range(4):
                mm = pe.transpose(K.ps[0][:, j * rows:(j + 1) * rows], by_row[0:rows, j * P:j * P + P],
                                  const(K, "ident", slice(0, rows))[:, 0:rows])
            turned_up.up(mm)

        @K.block.vector
        def _(dve):
            dve.wait_ge(summed.sem, summed.base + 1)
            copied.up(dve.tensor_copy(by_row[0:rows, :], K.ps[7][0:rows, :]))
            dve.wait_ge(turned_up.sem, turned_up.base + 1)
            bias = prm(K, "b_ada", 0, 2 * 6 * KD)
            for j in range(4):
                ins = dve.tensor_tensor(
                    K.mods[:, :, j::4, :],
                    K.ps[0][:, j * rows:(j + 1) * rows].rearrange("p (l g s) -> p l g s", l=2, s=2),
                    bias[:, j::4].rearrange("p (l g) -> p l g", l=2).unsqueeze(3)
                    .to_broadcast([P, 2, per_layer, 2]), ALU.add)
            link(dve, K.dve_step, ins)
            for layer in range(2):
                for n, (name, at) in enumerate((("g_mix", KD), ("g_ffn", 4 * KD))):
                    for s in range(2):
                        dve.scalar_tensor_tensor(K.gains[:, layer, n, s, :], K.mods[:, layer, at:at + KD, s], 1.0,
                                                 prm(K, name, layer * KD, KD), ALU.add, ALU.mult)
        meet(K)


def modulated_norm(K, layer, which, with_ctx, h, room=None):
    def part(s, c0, w):
        shift = 3 * KD * which
        return (c0, w, lambda k: K.gains[:, layer, which, s, k:k + 1],
                lambda k: K.mods[:, layer, shift + k, s:s + 1])
    base = K.signals["low_ready"].n
    rms_phase(K, K.xT, h, [part(0, 0, S)] + ([part(1, S, C)] if with_ctx else []), room, end=False)
    return base, base + KD



def feature_head_norms(K, layer, p, jobs):
    squared, summed, inv, done = (K.signals[n] for n in ("square", "stat", "rstd", "normed"))
    with ExitStack() as ctx:
        sq = arena(K, ctx, "head_squares", [P, 3, S])
        rs = arena(K, ctx, "head_rstd", [P, 3, S])

        @K.block.vector
        def _(dve):
            def square(n):
                u, _, _, _, c0, w = jobs[n]
                if n >= 3:
                    dve.wait_ge(summed.sem, summed.base + n - 2)
                x = p[:, u, c0:c0 + w]
                squared.up(dve.tensor_tensor(sq[:, n % 3, 0:w], x, x, ALU.mult))

            def scale(n):
                u, name, _, _, c0, w = jobs[n]
                dve.wait_ge(inv.sem, inv.base + n + 1)
                done.up(dve.scalar_tensor_tensor(p[:, u, c0:c0 + w], p[:, u, c0:c0 + w], prm(K, name, layer),
                                                 rs[:, n % 3, 0:w], ALU.mult, ALU.mult))

            for n in range(len(jobs) + 2):
                if n < len(jobs):
                    square(n)
                if n >= 2:
                    scale(n - 2)

        @K.block.tensor
        def _(pe):
            for n, (u, _, block, _, c0, w) in enumerate(jobs):
                pe.wait_ge(squared.sem, squared.base + n + 1)
                if n >= 3:
                    pe.wait_ge(inv.sem, inv.base + n - 2)
                summed.up(pe.matmul(K.ps[n % 3][:, 0:w], const(K, block), sq[:, n % 3, 0:w],
                                    start=True, stop=True))

        @K.block.scalar
        def _(act):
            exp_and_log(act)
            for n, (u, _, _, width, c0, w) in enumerate(jobs):
                act.wait_ge(summed.sem, summed.base + n + 1)
                if n >= 3:
                    act.wait_ge(done.sem, done.base + n - 2)
                link(act, K.act_step, act.activation(rs[:, n % 3, 0:w], K.ps[n % 3][:, 0:w], ACT.Ln,
                                                     bias=K.eps[:, 0:1], scale=1.0 / width))
                inv.up(act.activation(rs[:, n % 3, 0:w], rs[:, n % 3, 0:w], ACT.Exp, scale=-0.5))
        meet(K)


def query_key_norms(K, layer, p, with_ctx_q, rope):
    jobs = []
    for u, name, block, width in ((DK, "dkn", "block32", 32), (NK, "nkn", "block64", 64),
                                  (DQ, "dqn", "block32", 32), (NQ, "nqn", "block64", 64)):
        for i in range(2):
            jobs.append((u + i, name, block, width, 0, S))
            if with_ctx_q or u in (DK, NK):
                jobs.append((u + i, name, block, width, S, C))
    feature_head_norms(K, layer, p, jobs)
    summed = K.signals["stat"]
    with ExitStack() as ctx:
        turned = arena(K, ctx, "qk_turned", [P, 4, S])

        @K.block.tensor
        def _(pe):
            for n, u in enumerate((DK, DK + 1, DQ, DQ + 1)):
                summed.up(pe.matmul(K.ps[n][:, :], const(K, "rope_swap"), p[:, u, 0:S], start=True, stop=True))

        @K.block.vector
        def _(dve):
            for n, u in enumerate((DK, DK + 1, DQ, DQ + 1)):
                dve.wait_ge(summed.sem, summed.base + n + 1)
                dve.tensor_tensor(p[:, u, 0:S], p[:, u, 0:S], rope[:, 0], ALU.mult)
                link(dve, K.dve_step, dve.tensor_tensor(turned[:, n], K.ps[n][:, :], rope[:, 1], ALU.mult))
                dve.tensor_tensor(p[:, u, 0:S], p[:, u, 0:S], turned[:, n], ALU.add)
        meet(K)



def fourier(K, p, dft, parts):
    first_up, first_out, second_up, put = (K.signals[n] for n in ("scored", "exped", "mixed", "put"))
    jobs = [(i, c0, w) for c0, w in parts for i in range(2)]
    with ExitStack() as ctx:
        z = arena(K, ctx, "fourier_z", [P, 2, NT, 2 * P])

        @K.block.tensor
        def _(pe):
            def features(n):
                i, c0, w = jobs[n]
                for t in range(w // P):
                    if n:
                        pe.wait_ge(first_out.sem, first_out.base + 2 * n)
                    at = t * 2 * P if w == S else t * S
                    mm = pe.matmul(K.psum[:, at:at + 2 * P], p[:, FO + i, c0 + t * P:c0 + t * P + P],
                                   const(K, "dft64"), start=True, stop=True)
                first_up.up(mm)

            def tokens(n):
                i, c0, w = jobs[n]
                pe.wait_ge(first_out.sem, first_out.base + 2 * (n + 1))
                if n >= 2:
                    pe.wait_ge(put.sem, put.base + n - 1)
                for t in range(w // P):
                    for q in range(2):
                        mm = pe.matmul(K.ps[2 + n % 2][:, 0:w], z[:, n % 2, t, q * P:q * P + P],
                                       dft[:, q, t, 0:S:S // w], start=(t == 0 and q == 0),
                                       stop=(t == w // P - 1 and q == 1))
                second_up.up(mm)

            for n in range(len(jobs) + 1):
                if n < len(jobs):
                    features(n)
                if n == 1:
                    pe.wait_ge(K.loaded_late.sem, K.loaded_late.n)
                if n:
                    tokens(n - 1)

        half = lambda buf, n, q, w: buf[:, n % 2, q * w // P // 2:(q + 1) * w // P // 2, :]
        src = lambda q, w: K.psum[:, q * S:q * S + w].rearrange("p (t f) -> p t f", f=2 * P) if w == S \
            else K.psum[:, q * S:q * S + 2 * P].unsqueeze(1)

        def first(eng, q, op):
            for n, (i, c0, w) in enumerate(jobs):
                eng.wait_ge(first_up.sem, first_up.base + n + 1)
                if n >= 2:
                    eng.wait_ge(second_up.sem, second_up.base + n - 1)
                first_out.up(op(half(z, n, q, w), src(q, w)))
                if q and n:
                    last(eng, n - 1)
            if q:
                last(eng, len(jobs) - 1)

        def last(act, n):
            i, c0, w = jobs[n]
            act.wait_ge(second_up.sem, second_up.base + n + 1)
            put.up(act.activation(K.yT[:, i, c0:c0 + w], K.ps[2 + n % 2][:, 0:w], ACT.Identity,
                                  scale=float((w * HD) ** -0.5)))

        @K.block.vector
        def _(dve):
            first(dve, 0, dve.tensor_copy)

        @K.block.scalar
        def _(act):
            first(act, 1, act.copy)
        meet(K)


def store(K, u, r, m):
    return lambda dve, psum: dve.tensor_copy(K.yT[r, u, m * P:m * P + P], psum)


def differential_attention(K, layer, p, v, tiles, key_tiles, key0):
    with ExitStack() as ctx:
        neg_lam = arena(K, ctx, "neg_lam", [P, 4])
        prod = arena(K, ctx, "lam_products", [P, 2, 32])
        summed, exped = K.signals["prepared"], K.signals["soft"]
        l4 = row(K, "lam4", layer * 128, 128).rearrange("p (a d) -> p a d", a=4)

        @K.block.vector
        def _(dve):
            link(dve, K.dve_step, dve.tensor_tensor(prod[:, :, :], l4[:, 0:4:2], l4[:, 1:4:2], ALU.mult))
            summed.up(dve.tensor_reduce(neg_lam[:, 0:2], prod[:, :, :], AX, ALU.add))
            dve.wait_ge(exped.sem, exped.base + 1)
            link(dve, K.dve_step, dve.tensor_tensor(neg_lam[:, 2:3], neg_lam[:, 1:2], neg_lam[:, 0:1], ALU.subtract))
            dve.tensor_scalar(neg_lam[:, 3:4], neg_lam[:, 2:3], -lambda_init(layer), None, ALU.add)

        @K.block.scalar
        def _(act):
            act.wait_ge(summed.sem, summed.base + 1)
            exped.up(act.activation(neg_lam[:, 0:2], neg_lam[:, 0:2], ACT.Exp))
        meet(K)

        kw = len(key_tiles) * P
        items = []
        for h in range(H):
            for m in tiles:
                scores, rows = [], slice(64 * (h % 2), 64 * (h % 2) + HD)
                for c in range(2):
                    first_row = 64 * (h % 2) + 32 * c
                    r, i = slice(first_row, first_row + 32), h // 2
                    q = p[r, DQ + i, m * P:m * P + P]
                    scores.append([[(q, p[r, DK + i, key0 + a:key0 + min(a + S, kw)], a, min(S, kw - a))]
                                   for a in range(0, kw, S)])
                items.append(dict(scores=scores, kw=kw, tiles=key_tiles, bias=None,
                                  v=lambda t, h=h: v[:, t, h * HD:h * HD + HD], rows=rows,
                                  out=store(K, 2 + h // 2, rows, m)))
        softmax_attention(K, items, 1.0, neg_lam[:, 3:4])


def neighbourhood_attention(K, p, v, tiles, key_tiles, key0, bias):
    kw = len(key_tiles) * P
    items = []
    for h in range(H):
        r, i = slice(64 * (h % 2), 64 * (h % 2) + HD), h // 2
        for m in tiles:
            q = p[r, NQ + i, m * P:m * P + P]
            first = 7 - 2 * m
            b = None if bias is None else bias[:, h, first:first + 8, :].rearrange("p a k -> p (a k)")
            items.append(dict(
                scores=[[[(q, p[r, NK + i, key0 + a:key0 + min(a + S, kw)], a, min(S, kw - a))]
                         for a in range(0, kw, S)]],
                kw=kw, tiles=key_tiles, bias=b, v=lambda t, h=h: v[:, t, G + h * HD:G + h * HD + HD],
                rows=r, out=store(K, 4 + i, r, m)))
    softmax_attention(K, items, 1.0)


def head_norm(K, ctx, src, gain, tiles):
    n = len(tiles)
    m = slice(tiles[0], tiles[-1] + 1)
    squared, summed, inv = (K.signals[x] for x in ("square", "stat", "rstd"))
    sq = arena(K, ctx, "head_squares", [P, n, G])
    st = arena(K, ctx, "head_stats", [P, n, H])
    heads = lambda ap: ap.rearrange("p m (h d) -> p m h d", d=HD)

    @K.block.scalar
    def _(act):
        exp_and_log(act)
        squared.up(act.activation(sq[:, :, :], src[:, m, :], ACT.Square))
        act.wait_ge(summed.sem, summed.base + 1)
        link(act, K.act_step, act.activation(st[:, :, :], st[:, :, :], ACT.Ln, bias=K.eps[:, 0:1],
                                             scale=1.0 / HD))
        inv.up(act.activation(st[:, :, :], st[:, :, :], ACT.Exp, scale=-0.5))

    @K.block.vector
    def _(dve):
        dve.wait_ge(squared.sem, squared.base + 1)
        summed.up(dve.tensor_reduce(st[:, :, :], heads(sq[:, :, :]), AX, ALU.add))
        dve.wait_ge(inv.sem, inv.base + 1)
        for t in range(n):
            ins = dve.tensor_tensor(
                src[:, tiles[0] + t, :].rearrange("p (h d) -> p h d", d=HD),
                src[:, tiles[0] + t, :].rearrange("p (h d) -> p h d", d=HD),
                st[:, t, :].unsqueeze(2).to_broadcast([P, H, HD]), ALU.mult)
        link(dve, K.dve_step, ins)
        for t in range(n):
            dve.tensor_tensor(src[:, tiles[0] + t, :], src[:, tiles[0] + t, :], gain, ALU.mult)


def chunk_gmlp(K, layer, uv, y, tiles, ws):
    mixed = K.signals["mixed"]
    m, w = slice(tiles[0], tiles[-1] + 1), len(tiles) * HD

    @K.block.tensor
    def _(pe):
        for h in range(H):
            mixed.up(pe.matmul(K.ps[h][:, 0:w], ws[:, h], uv[:, m, G + h * HD:G + h * HD + HD],
                               start=True, stop=True))

    @K.block.vector
    def _(dve):
        for h in range(H):
            dve.wait_ge(mixed.sem, mixed.base + h + 1)
            c = slice(h * HD, h * HD + HD)
            dve.scalar_tensor_tensor(y[:, m, c], K.ps[h][:, 0:w].rearrange("p (m d) -> p m d", d=HD),
                                     prm(K, "gmlp_b", layer * H + h), uv[:, m, c], ALU.add, ALU.mult)
    meet(K)



def feed_forward(K, layer, with_ctx):
    W = S + C if with_ctx else S
    conv, gate_done, emptied = K.signals["conv"], K.signals["silu"], K.signals["main_free"]
    ZW = S + C + 4
    spans = [(0, S, 1)] + ([(S, C, S + 3)] if with_ctx else [])
    first = K.unit
    wc = PRM["conv_w2"][0] + layer * 3 * 44
    bc = PRM["conv_b2"][0] + layer * 44
    TURNS = 2 * KF // RING
    with ExitStack() as ctx:
        h = arena_pair(K, ctx, "h", [P, KD, S + C])
        hid = arena(K, ctx, "hidden", [P, KF, S + C])
        inner = ctx.enter_context(ExitStack())
        z = arena(K, inner, "z", [P, 4, ZW])
        t = arena(K, inner, "conv_out", [P, 4, S + C])
        padded = K.signals["padded"]

        @K.block.gpsimd
        def _(pool):
            padded.up(pool.memset(z[:, :, :], 0.0))
        waits = modulated_norm(K, layer, 1, with_ctx, h, (hid[:, 0:KD, :], hid[:, KD, :]))

        @K.block.tensor
        def _(pe):
            def unit(i, j):
                q = first + j
                pe.wait_ge(K.unit_used.sem, i * RING + (q + 1))
                pe.wait_ge(emptied.sem, i * RING + (j + emptied.base + 1))
                feature_unit(K, pe, q, j, h, with_ctx, waits if isinstance(i, int) and i == j == 0 else None)
            in_turns(pe, 2 * KF, unit)

        @K.block.scalar
        def _(act):
            def empty(i, j):
                act.wait_ge(K.unit_done.sem, i * RING + (j + K.unit_done.base + 1))
                act.wait_ge(conv.sem, i * RING + (j + conv.base + 1))
                for n, (c0, w, z0) in enumerate(spans):
                    ins = act.copy(z[:, j, z0:z0 + w], K.ps[4 * n + j][:, 0:w])
                ins.then_inc(emptied.sem, 1)
                if j % 2:
                    act.wait_ge(conv.sem, i * RING + (j + conv.base + RING))
                    act.activation(t[:, j - 1, 0:W], t[:, j - 1, 0:W], ACT.Silu).then_inc(gate_done.sem, 1)

            def unit(i, j):
                split_high(K, act, i, j + 1)
                empty(i, j)
            act.sem_inc(emptied.sem, RING)
            act.wait_ge(padded.sem, padded.n)
            in_turns(act, 2 * KF, unit)

        @K.block.vector
        def _(dve):
            def convolve(i, j):
                tile = (j % 2) * KF + j // 2
                column = lambda c: K.prm[:, ds(i * 2 + (c + tile), 1)]
                dve.wait_ge(emptied.sem, i * RING + (j + emptied.base + RING + 1))
                if j % 2 == 0:
                    dve.wait_ge(K.conv_step.sem, i * STEPS + (K.conv_step.base + 1))
                at = 1 + 5 * (j // 2) + 2 * (j % 2)
                for tap in range(3):
                    if tap:
                        dve.wait_ge(K.conv_step.sem, i * STEPS + (K.conv_step.base + at + tap))
                    for s, (c0, w, z0) in enumerate(spans):
                        to, src = t[:, j, c0:c0 + w], z[:, j, z0 - 1 + tap:z0 - 1 + tap + w]
                        if tap == 0:
                            ins = dve.tensor_scalar(to, src, column(wc), column(bc), ALU.mult, ALU.add)
                        else:
                            ins = dve.scalar_tensor_tensor(to, src, column(wc + 44 * tap), to, ALU.mult, ALU.add)
                    ins.then_inc(conv.sem if tap == 2 else K.conv_step.sem, 1)
                if j % 2:
                    dve.wait_ge(conv.sem, i * RING + (j + conv.base + RING + 1))
                    dve.wait_ge(gate_done.sem, i * 2 + (j // 2 + gate_done.base + 1))
                    dve.tensor_tensor(hid[:, ds(i * 2 + j // 2, 1), 0:W].rearrange("p a w -> p (a w)"),
                                      t[:, j - 1, 0:W], t[:, j, 0:W], ALU.mult).then_inc(K.conv_step.sem, 1)

            def unit(i, j):
                split_low(K, dve, i, j + 1)
                convolve(i, j)
            STEPS = 10
            dve.sem_inc(conv.sem, RING)
            dve.sem_inc(K.conv_step.sem, 1)
            in_turns(dve, 2 * KF, unit)

        K.conv_step.n += TURNS * 10 + 1
        conv.n += RING + 2 * KF
        gate_done.n += KF
        emptied.n += RING + 2 * KF
        used_units(K, 2 * KF, True)
        meet(K)
        inner.close()

        put, ctx_put, high_ready, low_ready = (K.signals[n] for n in ("put", "ctx_put", "high_ready", "low_ready"))
        mv = arena_pair(K, ctx, "hidden_part", [P, 2, 2, S + C])
        first, half, more = K.unit, KF // 2, layer == 0

        def hidden(n):
            return hid[:, ds(n * 2, 2), 0:W]

        @K.block.tensor
        def _(pe):
            def unit(i, j, n=None):
                q = first + j
                n = j if n is None else n
                spare = 4 * (not with_ctx and j >= half)
                pe.wait_ge(K.unit_used.sem, i * RING + (q + 1))
                pe.wait_ge(low_ready.sem, i * RING + (low_ready.base + j + 1))
                for kk in range(2):
                    start, stop = n % half == 0 and kk == 0, n % half == half - 1 and kk == 1
                    for o in range(4):
                        w = weights(K, q, kk * 4 + o)
                        mm = three_products(pe, K.ps[o + spare][:, :], w, tuple(m[:, q % 2, kk, 0:S] for m in mv),
                                            start, stop)
                        if with_ctx:
                            mm = three_products(pe, K.ps[4 + o][:, 0:C], w,
                                                tuple(m[:, q % 2, kk, S:S + C] for m in mv), start, stop)
                mm.then_inc(K.unit_done.sem, 1)

            for a in (0, half):
                if a and with_ctx:
                    pe.wait_ge(put.sem, put.base + 1)
                    pe.wait_ge(ctx_put.sem, ctx_put.base + 1)
                unit(0, a)
                with pe.Fori(0, 2) as i:
                    for j in range(RING):
                        unit(i, a + 1 + j, 1)
                unit(0, a + 9)
                unit(0, a + 10)

        @K.block.scalar
        def _(act):
            def each(i, j, n):
                q = first + j
                act.wait_ge(K.unit_done.sem, i * RING + (K.unit_done.base + j - 1))
                act.copy(mv[0][:, q % 2, :, 0:W], hidden(n)).then_inc(high_ready.sem, 1)
                if more or j + 1 < KF:
                    split_high(K, act, i, j + 1)
            for a in (0, half):
                with act.Fori(0, 2) as i:
                    for j in range(RING):
                        each(i, a + j, i * RING + j)
                for j in range(8, half):
                    each(0, a + j, j)

        @K.block.vector
        def _(dve):
            def each(i, j, n):
                q = first + j
                dve.wait_ge(high_ready.sem, i * RING + (high_ready.base + j + 1))
                dve.tensor_tensor(mv[1][:, q % 2, :, 0:W], hidden(n), mv[0][:, q % 2, :, 0:W].bitcast(F32),
                                  ALU.subtract).then_inc(low_ready.sem, 1)
                if more or j + 1 < KF:
                    split_low(K, dve, i, j + 1)

            def add(a):
                dve.wait_ge(K.unit_done.sem, K.unit_done.base + half * (a + 1))
                for o in range(4):
                    n = 4 * a + o
                    bank = K.ps[o if with_ctx else n]
                    ins = dve.scalar_tensor_tensor(K.xT[:, n, 0:S], bank[:, :], K.mods[:, layer, 5 * KD + n, 0:1],
                                                   K.xT[:, n, 0:S], ALU.mult, ALU.add)
                put.up(ins)
                for o in range(4 if with_ctx else 0):
                    n = 4 * a + o
                    ins = dve.scalar_tensor_tensor(K.xT[:, n, S:S + C], K.ps[4 + o][:, 0:C],
                                                   K.mods[:, layer, 5 * KD + n, 1:2], K.xT[:, n, S:S + C],
                                                   ALU.mult, ALU.add)
                if with_ctx:
                    ctx_put.up(ins)

            for a in (0, half + 1):
                with dve.Fori(0, 2) as i:
                    for j in range(RING):
                        each(i, a + j, i * RING + (j + a % half))
                for j in range(a + 8, min(a + 12, KF)):
                    each(0, j, j % half)
                add(a // half)
        high_ready.n += KF
        low_ready.n += KF
        used_units(K, KF, more)
        meet(K)



SIGNALS = ("met", "act_step", "dve_step", "conv_step", "unit_used", "loaded_late", "unit_done", "high_split",
           "high_ready", "low_ready", "square", "added", "stat", "rstd", "normed", "main_free", "ctx_free",
           "scored", "max_ready", "exped", "weighted", "turned_up", "turned_out", "mixed", "put",
           "ctx_put", "prepared", "soft", "summed", "produced", "taken", "x_ready0", "x_ready1",
           "m_up0", "m_up1", "m_out0", "m_out1", "t_up0", "t_up1", "t_out0", "t_out1", "w_up",
           "w_out", "u_up", "u_out", "y_up", "y_out", "s_out", "tile_done", "conv", "silu",
           "pair_done", "loaded", "padded", "loaded_tables", "loaded_rest", "stored")

N_UNITS = N1F + N1T + KD + MOD_UNITS + 2 * (N2F + 8 + KD + 44 + 22)


def build(nc, dram):
    with ExitStack() as ctx:
        K = Kit()
        K.nc, K.serial, K.unit = nc, 0, 0
        K.signals = {n: Signal(nc, ctx, n) for n in SIGNALS}
        K.met, K.unit_used, K.loaded_late = (K.signals[n] for n in ("met", "unit_used", "loaded_late"))
        K.unit_done, K.high_split = K.signals["unit_done"], K.signals["high_split"]
        K.act_step, K.dve_step, K.conv_step = (K.signals[n] for n in ("act_step", "dve_step", "conv_step"))
        K.slot_full = [Signal(nc, ctx, f"slot_full{j}") for j in range(RING)]
        K.w_units, K.lru_w_dram, K.lora_dram = dram["w_units"], dram["lru_w"], dram["lora"]
        sb = lambda name, shape: ctx.enter_context(nc.sbuf_tensor(name, shape, F32))
        K.psum = ctx.enter_context(nc.psum_tensor("psum", [P, 8 * S], F32))
        K.ps = [K.psum[:, j * S:(j + 1) * S] for j in range(8)]
        K.ring = sb("ring", [P, RING, KD * P])
        K.xT = sb("xT", [P, KD, S + C])
        K.w_high, K.w_low = arena_pair(K, ctx, "unit", [P, 2, KD * P])
        K.cst = sb("constants", [P, width(CONST)])
        K.prm = sb("parameters", [P, NPRM])
        K.rows = sb("row_parameters", [P, NROW - ROWS_FIRST])
        K.mods = sb("mods", [P, 2, 6 * KD, 2])
        K.gains = sb("gains", [P, 2, 2, 2, KD])
        scal = sb("scalars", [P, 8])
        K.eps, K.gn_eps, K.one, K.half, K.minus_half = (scal[:, j:j + 1] for j in range(5))
        first = ctx.enter_context(ExitStack())
        K.cst_first = arena(K, first, "constants_first", [P, width(CONST_FIRST)])
        K.rows_first = arena(K, first, "row_parameters_first", [P, ROWS_FIRST])
        K.cond = arena(K, first, "cond", [P, KD, 4 * MOD_GROUPS - 2])
        K.block = ctx.enter_context(nc.Block())
        loaded, K.loaded_rest = K.signals["loaded"], K.signals["loaded_rest"]

        @K.block.scalar
        def _(act):
            for dst, src in ((K.xT[:, :, 0:S], dram["x"]), (K.cst[:, :], dram["constants"]),
                             (K.prm[:, :], dram["parameters"])):
                loaded.up(act.dma_start(dst, src), 16)
            for dst, src in ((K.cst_first[:, :], dram["constants_first"]),
                             (K.rows[:, :], dram["row_parameters"][:, ROWS_FIRST:]),
                             (K.rows_first[:, :], dram["row_parameters"][:, 0:ROWS_FIRST]),
                             (K.xT[:, :, S:S + C], dram["ctx"])):
                K.loaded_rest.up(act.dma_start(dst, src), 16)
            act.wait_ge(loaded.sem, loaded.n)

        @K.block.gpsimd
        def _(pool):
            for at, value in ((K.eps, EPS), (K.gn_eps, GN_EPS), (K.one, 1.0), (K.half, HALF),
                              (K.minus_half, -HALF)):
                pool.memset(at, value)
            pool.memset(K.cond[:, :, :], 0.0)
        stream_weights(K, N_UNITS)

        @K.block.tensor
        def _(pe):
            pe.sem_inc(K.unit_done.sem, 1)
        K.unit_done.n = 1
        meet(K)

        first_block(K)
        first.close()
        second_block(K, dram)

        @K.block.sync
        def _(sp):
            sp.wait_ge(K.met.sem, K.met.n)
            sp.dma_start(dram["out"], K.xT[:, :, 0:S]).then_inc(K.signals["stored"].sem, 16)
            sp.wait_ge(K.signals["stored"].sem, 16)


def first_block(K):
    @K.block.scalar
    def _(act):
        act.activation(K.cond[:, :, 2 * MOD_GROUPS - 2:2 * MOD_GROUPS],
                       prm(K, "c", 0, 2 * KD).rearrange("p (s k) -> p k s", s=2), ACT.Silu)
    outer = ExitStack()
    with ExitStack() as ctx:
        K.yT = arena(K, outer, "yT", [P, KD, S])
        p = arena(K, ctx, "p", [P, N1F, PAD + S])
        v = arena(K, ctx, "v", [P, NT, 2 * G])
        inner = ctx.enter_context(ExitStack())
        h = arena_pair(K, inner, "h", [P, KD, S])
        split_first(K)
        rms_phase(K, K.xT, h, [(0, S, lambda k: prm(K, "norm_g", k), None)], (K.yT, v[:, 0, :]), end=False)

        @K.block.gpsimd
        def _(pool):
            pool.memset(p[:, :, 0:PAD], 0.0)

        @K.block.scalar
        def _(act):
            act.wait_ge(K.loaded_rest.sem, K.loaded_rest.n)
        project(K, N1F, False,
                lambda dve, u, bank: dve.tensor_copy(at_unit(p, u, PAD, PAD + S), bank[:, :]), None, h,
                (K.signals["low_ready"].base,))
        project_tokens(K, v, NT, h, more=False)
        inner.close()
        y = arena(K, ctx, "y", [P, NT, G])

        @K.block.scalar
        def _(act):
            for u in range(GATE, GATE + 8):
                act.activation(p[:, u, PAD:], p[:, u, PAD:], ACT.Silu)

        K.modulation_first, K.units_modulated = K.unit, 0

        @K.block.tensor
        def _(pe):
            modulation_units(K, pe, 3)

        def gated(group):
            def put(dve, u, psum, r=slice(0, P), c=slice(0, S)):
                return dve.tensor_tensor(K.yT[r, 2 * group + u, c], psum,
                                         p[r, GATE + 2 * group + u, PAD + c.start:PAD + c.stop], ALU.mult)
            return put
        tiles = range(NT)
        forgetting_attention(K, p, v[:, :, 0:G], gated(0))
        stick_breaking_attention(K, p, v[:, :, G:2 * G], gated(1))
        rg_lru(K, p, lambda dve, i, h: dve.tensor_tensor(K.yT[:, 6 + i, 0:S], h, p[:, GATE + 6 + i, PAD:],
                                                         ALU.mult))
        rwkv(K, p, v, y)
        to_feature_major(K, y, tiles, gated(2))
    finish_modulation(K)

    def add_to_x(dve, u, bank):
        x = at_unit(K.xT, u, 0, S)
        return dve.tensor_tensor(x, x, bank[:, :], ALU.add)
    with outer, ExitStack() as ctx:
        parts = arena_pair(K, ctx, "y", [P, KD, S])
        split_first(K)
        split_moving(K, K.yT, parts, S)
        project(K, KD, False, add_to_x, None, parts, (K.signals["low_ready"].base,))
    rms_phase(K, K.xT, K.xT, [(0, S, lambda k: prm(K, "final_g", k), None)])


def at_unit(buf, u, a, b):
    if isinstance(u, int):
        return buf[:, u, a:b]
    return buf[:, ds(u, 1), a:b].rearrange("p a w -> p (a w)")


def second_block(K, dram):
    @K.block.vector
    def _(dve):
        dve.tensor_scalar(prm(K, "dqn", 0, 2), prm(K, "dqn", 0, 2), 32 ** -0.5, None, ALU.mult)
        dve.tensor_scalar(prm(K, "nqn", 0, 2), prm(K, "nqn", 0, 2), HD ** -0.5, None, ALU.mult)
        for layer in range(2):
            dve.tensor_scalar(prm(K, "subln", layer), prm(K, "subln", layer), 1.0 - lambda_init(layer), None, ALU.mult)
    meet(K)
    for layer in range(2):
        ctx_out = layer == 0
        outer = ExitStack()
        K.yT = arena(K, outer, "yT", [P, KD, S + C])
        mixers(K, layer, ctx_out, dram)

        def lat(dve, u, bank):
            x = at_unit(K.xT, u, 0, S)
            m = K.mods[:, layer, ds(u + 2 * KD, 1), 0:1].rearrange("p a b -> p (a b)")
            return dve.scalar_tensor_tensor(x, bank[:, :], m, x, ALU.mult, ALU.add)

        def cnt(act, u, bank):
            m = K.mods[:, layer, ds(u + 2 * KD, 1), 1:2].rearrange("p a b -> p (a b)")
            return act.activation(at_unit(K.ctx_gain, u, 0, C), bank[:, 0:C], ACT.Identity, scale=m)
        with outer, ExitStack() as ctx:
            parts = arena_pair(K, ctx, "y", [P, KD, S + C])
            split_moving(K, K.yT, parts, S + C if ctx_out else S)
            if ctx_out:
                K.ctx_gain = arena(K, ctx, "ctx_gain", [P, KD, C])
            project(K, KD, ctx_out, lat, cnt, parts, (K.signals["low_ready"].base,) * 2)
            if ctx_out:
                @K.block.vector
                def _(dve):
                    dve.tensor_tensor(K.xT[:, :, S:S + C], K.xT[:, :, S:S + C], K.ctx_gain[:, :, :], ALU.add)
                meet(K)
        feed_forward(K, layer, ctx_out)


def mixers(K, layer, ctx_out, dram):
    late, tables = K.loaded_late, K.signals["loaded_tables"]
    spans = [(0, S), (S, C)] if ctx_out else [(0, S)]
    lat_tiles, ctx_tiles, all_tiles = range(NT), range(NT, MT), range(MT)
    with ExitStack() as ctx:
        p = arena(K, ctx, "p", [P, N2F, S + C])
        v = arena(K, ctx, "v", [P, MT, 4 * P])
        uv = arena(K, ctx, "uv", [P, MT, 4 * P])
        y = arena(K, ctx, "y", [P, MT, G])
        inner = ctx.enter_context(ExitStack())
        h = arena_pair(K, inner, "h", [P, KD, S + C])
        waits = modulated_norm(K, layer, 0, True, h, (K.yT, y[:, 0:3, :].rearrange("p m f -> p (m f)")))

        def feature(first):
            return (lambda dve, u, bank: dve.tensor_copy(at_unit(p, u + first, 0, S), bank[:, :]),
                    lambda act, u, bank: act.copy(at_unit(p, u + first, S, S + C), bank[:, 0:C]))

        project(K, 4, True, *feature(0), h, waits)
        project(K, 6, ctx_out, *feature(4), h)
        project_tokens(K, v, MT, h)
        project_tokens(K, uv, MT if ctx_out else NT, h)
        inner.close()

        tiles = all_tiles if ctx_out else lat_tiles
        rope = arena(K, ctx, "rope", [P, 2, S])
        ws = arena(K, ctx, "gmlp_ws", [P, H, P])
        bias = arena(K, ctx, "bias", [P, H, 16, HD])
        with ExitStack() as inner:
            dft = arena(K, inner, "dft", [P, 2, NT, S])

            @K.block.gpsimd
            def _(pool):
                late.up(pool.dma_start(dft[:, :, :, :], dram["dft"]), 16)
                pool.wait_ge(late.sem, late.n)
                for table, src in ((ws[:, :, :], dram["gmlp_ws"][:, layer]), (rope[:, :, :], dram["rope"]),
                                   (bias[:, :, :, :], dram["na_bias"][:, layer])):
                    tables.up(pool.dma_start(table, src), 16)
                pool.wait_ge(tables.sem, tables.n)
                for h in range(H):
                    pool.tensor_tensor(bias[:, h], bias[:, h],
                                       const(K, "window").unsqueeze(1).to_broadcast([P, 16, HD]), ALU.add)

            @K.block.scalar
            def _(act):
                link(act, K.act_step, act.activation(uv[:, 0:len(tiles), :], uv[:, 0:len(tiles), :],
                                                     ACT.Gelu_apprx_tanh))
            head_norm(K, inner, uv[:, :, G:2 * G], row(K, "gmlp_g", layer * G), tiles)
            fourier(K, p, dft, spans)

        def put_unit(first, c0):
            return lambda dve, u, psum: dve.tensor_copy(K.yT[:, first + u, c0:c0 + psum.shape[1]], psum)

        def turn_all(first):
            to_feature_major(K, y, lat_tiles, put_unit(first, 0))
            if ctx_out:
                to_feature_major(K, y, ctx_tiles, put_unit(first, S))

        chunk_gmlp(K, layer, uv, y, tiles, ws)
        turn_all(6)
        query_key_norms(K, layer, p, ctx_out, rope)
        differential_attention(K, layer, p, v, lat_tiles, all_tiles, 0)
        if ctx_out:
            differential_attention(K, layer, p, v, ctx_tiles, ctx_tiles, S)
        feature_head_norms(K, layer, K.yT, [(u, "subln", "block64", HD, c0, w) for c0, w in spans for u in (2, 3)])
        neighbourhood_attention(K, p, v, lat_tiles, all_tiles, 0, bias)
        if ctx_out:
            neighbourhood_attention(K, p, v, ctx_tiles, ctx_tiles, S, None)



def width(table):
    return max(b for _, b in table.values())


def constant_tables():
    tables = [np.zeros((P, width(x)), np.float32) for x in (CONST, CONST_FIRST)]
    i, j = np.arange(P)[:, None], np.arange(P)[None, :]

    def put(name, value):
        a, b = CONST.get(name) or CONST_FIRST[name]
        tables[name not in CONST][:, a:b] = value
    put("ident", i == j)
    put("ones", 1.0)
    put("block32", i // 32 == j // 32)
    put("block64", i // 64 == j // 64)
    put("tri_ge", i >= j)
    put("causal_add", np.where(j > i, NEG, 0.0))
    put("stick_big", np.where(i >= j, -NEG, 0.0))
    put("strict_t", i < j)
    put("incl_t", i <= j)
    put("rope_swap", np.where(i // 32 == j // 32, np.where(i == j + 16, -1.0, np.where(i == j - 16, 1.0, 0.0)), 0.0))
    head_row = np.zeros((P, H, P))
    for h in range(H):
        head_row[64 + h, h] = HD ** 0.5
    put("head_row", head_row.reshape(P, -1))
    put("head_pair", i // 64 == np.arange(2)[None, :])
    level = np.zeros((P, LEVELS, P))
    for n in range(LEVELS):
        level[:, n] = (i // 2 ** n == j // 2 ** n + 1) & (i // 2 ** n % 2 == 1)
    put("level", level.reshape(P, -1))
    put("level0_t", level[:, 0].T)
    q, k = i % HD, np.arange(HD)[None, :]
    c0 = np.clip(q - 8, 0, HD - 16)
    put("window", np.where((k >= c0) & (k < c0 + 16), 0.0, NEG))
    put("chunk_keep", np.arange(S)[None, :] % CH != 0)
    put("keep_all", 1.0)
    d = np.arange(HD)
    angle = 2 * np.pi * np.outer(d, d) / HD
    two = lambda m: np.kron(np.eye(2), m)
    put("dft64", np.concatenate([two(np.cos(angle)), -two(np.sin(angle))], axis=1))
    return tables


def dft_table():
    n = np.arange(S)
    angle = 2 * np.pi * (np.outer(n, n) % S) / S
    both = np.stack([np.cos(angle), np.sin(angle)])
    return np.ascontiguousarray(both.reshape(2, NT, P, S).transpose(2, 0, 1, 3)).astype(np.float32)


def rope_table():
    freqs = 10000.0 ** (-np.arange(8, dtype=np.float32) / 8)
    t = np.arange(S)
    angle = np.concatenate([(t // 64)[None, :] * freqs[:, None], (t % 64)[None, :] * freqs[:, None]])
    full = np.tile(angle, (8, 1))
    return np.stack([np.cos(full), np.sin(full)], axis=1).astype(np.float32)



def tile_units(w):
    n = w.shape[1] // P
    return w.reshape(KD, P, n, P).transpose(2, 1, 0, 3).reshape(n, P, KD * P)


def token_units(w):
    return w.reshape(4, 2, P, S).transpose(0, 2, 1, 3).reshape(4, P, 2 * S)


def down_units(w):
    w = w.reshape(KF // 2, 2, P, 2, 4, P)
    return w.transpose(3, 0, 2, 1, 4, 5).reshape(KF, P, 8 * P)


def lay_out(a):
    cols = lambda w, at, n: w[:, at:at + n]
    g = G
    w1 = a["w_in"][0]
    at = {n: o for n, o in zip(("fq", "fk", "fv", "fg", "ff", "sq", "sk", "sv", "sg", "rw", "rg", "lx", "lg"),
                               np.cumsum([0, g, g, g, g, H, g, g, g, g, 3 * g + 2 * R, g, g]))}
    rw = at["rw"]
    first = [cols(w1, at[n], g) for n in ("fq", "fk", "sq", "sk")]
    first += [cols(w1, rw, 3 * g), cols(w1, rw + 3 * g, 2 * R), cols(w1, at["ff"], H),
              np.zeros((D, P - 2 * R - H), np.float32)]
    first += [cols(w1, at[n], g) for n in ("lx", "fg", "sg", "rg", "lg", "fv", "sv")]
    first = np.concatenate(first, axis=1)
    units = [tile_units(first[:, :N1F * P]), token_units(first[:, N1F * P:])]
    units += [token_units(cols(a["w_ada_2"][l], n, S)) for l in range(2) for n in range(0, 6 * D, S)] + [tile_units(a["w_out"][0])]
    for l in range(2):
        w = a["w_in_2"][l]
        order = [2, 5, 0, 1, 4, 3, 6, 7, 8]
        second = [cols(w, n * g, g) for n in order]
        units.append(tile_units(np.concatenate(second[:5], axis=1)))
        units += [token_units(np.concatenate(second[n:n + 2], axis=1)) for n in (5, 7)]
        units.append(tile_units(a["w_out_2"][l]))
        up = a["ffn_up_2"][l].reshape(D, 2, KF, P).transpose(0, 2, 1, 3).reshape(D, 2 * FF)
        units += [tile_units(up), down_units(a["ffn_down_2"][l])]
    w_units = np.concatenate(units)

    prm_table = np.zeros((P, NPRM), np.float32)

    def put(name, values, col=0):
        f = PRM[name][0] + col
        v = np.asarray(values).reshape(-1, P)
        prm_table[:, f:f + len(v)] = v.T
    for name, src in (("norm_g", "norm_g"), ("w0", "rwkv_w0"), ("a0", "rwkv_a0"), ("k_k", "rwkv_k_k"),
                      ("k_a", "rwkv_k_a"), ("r_k", "rwkv_r_k"), ("conv_w", "lru_conv_w"), ("conv_b", "lru_conv_b"),
                      ("b_a", "lru_b_a"), ("b_x", "lru_b_x"), ("lam", "lru_lambda"), ("final_g", "final_g"),
                      ("g_mix", "g_mix_2"), ("g_ffn", "g_ffn_2"), ("b_ada", "b_ada_2"),
                      ("conv_w2", "ffn_conv_2"), ("conv_b2", "ffn_conv_b_2"), ("c", "c_2")):
        put(name, a[src])
    put("c", a["c_ctx_2"], KD)
    put("mu", np.concatenate([a["rwkv_mu"][0], np.zeros(64, np.float32)]))
    prm_table[64:64 + H, PRM["b_f"][0]] = a["b_forget"][0]
    for name, src, n in (("dqn", "diff_qn_2", 4), ("dkn", "diff_kn_2", 4), ("nqn", "na_qn_2", 2), ("nkn", "na_kn_2", 2),
                         ("subln", "diff_subln_2", 2)):
        put(name, np.tile(a[src], (1, n)))
    put("gmlp_b", a["gmlp_b_2"])

    row_table = np.concatenate([a["rwkv_ln_g"][0], a["rwkv_ln_b"][0],
                                a["gmlp_norm_2"].ravel(), a["diff_lam_2"].ravel()])
    row_table = np.ascontiguousarray(np.broadcast_to(row_table, (P, NROW)))

    lru_w = np.zeros((P, 4, P), np.float32)
    for n, src in enumerate(("lru_w_a", "lru_w_x")):
        for i in range(2):
            for e in range(2):
                lru_w[64 * e:64 * e + HD, 2 * n + i, 64 * e:64 * e + HD] = a[src][0, 2 * i + e]
    lora = np.concatenate([a["rwkv_w2"][0], a["rwkv_a2"][0]])

    q, k = np.arange(HD)[:, None], np.arange(HD)[None, :]
    off = k - q + 15
    rpb = a["na_rpb_2"]
    spread = np.where((off >= 0) & (off <= 30), rpb[:, :, :, np.clip(off, 0, 30)], np.float32(0))
    bias = np.zeros((2, HD, 2, H, 16, HD), np.float32)
    for e in range(2):
        bias[e, :, :, :, e:e + 15] = spread.transpose(3, 0, 1, 2, 4)
    constants, constants_first = constant_tables()
    tokens = lambda x: np.ascontiguousarray(x.reshape(-1, KD, P).transpose(2, 1, 0))
    return {
        "x": tokens(a["x"][0]), "ctx": tokens(a["ctx_2"][0]), "w_units": w_units,
        "constants": constants, "constants_first": constants_first, "parameters": prm_table, "row_parameters": row_table,
        "lru_w": lru_w.reshape(P, -1), "lora": np.ascontiguousarray(lora), "dft": dft_table(), "rope": rope_table(),
        "gmlp_ws": np.ascontiguousarray(a["gmlp_ws_2"].transpose(3, 0, 1, 2)),
        "na_bias": bias.reshape(P, 2, H, 16, HD),
    }


def kernel(**inputs):
    import concourse.bacc as bacc
    from concourse.bass_utils import run_bass_kernel_spmd

    arrays = lay_out({k: np.asarray(v) for k, v in inputs.items()})
    nc = bacc.Bacc("TRN2", target_bir_lowering=False, num_devices=1)
    dram = {n: nc.dram_tensor(f"in_{n}", v.shape, F32, kind="ExternalInput").ap() for n, v in arrays.items()}
    dram["out"] = nc.dram_tensor("out_x", (P, KD, S), F32, kind="ExternalOutput").ap()
    build(nc, dram)
    r = run_bass_kernel_spmd(nc, [{f"in_{n}": v for n, v in arrays.items()}], core_ids=[0])
    out = r.results[0]["out_x"]
    return out.transpose(2, 1, 0).reshape(1, S, D)
```
